# Optimizing a Trainium2 kernel written in Bass

```python
import jax, jax.numpy as jnp
from jax import lax
import numpy as np

D_MODEL = 1024
BATCH = 1
SEQ = 256
DEPTH = 1
DEC_BATCH = 8
DEC_SEQ = 4
PAST_LEN = 2048
PAGE_SIZE = 128

N_META = 16
D_CONV = D_MODEL
CONV_W = 31
DN_HEADS = 8
DN_DK = 128
DN_DV = 128
DN_QK = DN_HEADS * DN_DK
DN_V = DN_HEADS * DN_DV
DN_QKV = 2 * DN_QK + DN_V
SHORT_W = 4
CHUNK = 64
O_GLU = 0
O_Q = O_GLU + 2 * D_CONV
O_K = O_Q + DN_QK
O_V = O_K + DN_QK
O_Z = O_V + DN_V
O_A = O_Z + DN_V
O_B = O_A + DN_HEADS
O_GATE = O_B + DN_HEADS
IN_COLS = O_GATE + 2 * D_MODEL
N_EXPERTS = 32
TOP_K = 4
D_FF = D_MODEL
SWIGLU_LIMIT = 7.0
SWIGLU_ALPHA = 1.702
MOE_BLOCK = 128
EPS = 1e-6

kernel_name = 'hybrid_conformer_gdn_moe_step'

def rmsnorm(x, w):
    xf = x.astype(jnp.float32)
    y = xf * lax.rsqrt(jnp.mean(xf * xf, axis=-1, keepdims=True) + EPS)
    return (y * w.astype(jnp.float32)).astype(x.dtype)

def layernorm(x, g, b):
    xf = x.astype(jnp.float32)
    mu = jnp.mean(xf, axis=-1, keepdims=True)
    var = jnp.mean(jnp.square(xf - mu), axis=-1, keepdims=True)
    y = (xf - mu) * lax.rsqrt(var + EPS) * g.astype(jnp.float32) + b.astype(jnp.float32)
    return y.astype(x.dtype)

def l2norm(x):
    xf = x.astype(jnp.float32)
    return xf * lax.rsqrt(jnp.sum(xf * xf, axis=-1, keepdims=True) + EPS)

def causal_dwconv(x_hist, w):
    C = x_hist.shape[-1]
    return lax.conv_general_dilated(
        x_hist, w.astype(x_hist.dtype)[:, None, :], window_strides=(1,), padding='VALID',
        dimension_numbers=('NWC', 'WIO', 'NWC'), feature_group_count=C)

def gated_delta_chunked(q, k, v, g, beta, S0):
    N, L, H, DK = q.shape
    DV = v.shape[-1]
    nc = L // CHUNK
    f32 = jnp.float32

    def to_chunks(t):
        t = t.astype(f32).reshape((N, nc, CHUNK, H) + t.shape[3:])
        return jnp.moveaxis(t, 3, 1)

    q, k, v, g, beta = [to_chunks(t) for t in (q, k, v, g, beta)]
    gc = jnp.cumsum(g, axis=-1)
    causal = jnp.tril(jnp.ones((CHUNK, CHUNK), dtype=bool))
    strict = jnp.tril(jnp.ones((CHUNK, CHUNK), dtype=bool), k=-1)
    diff = gc[..., :, None] - gc[..., None, :]
    decay = jnp.where(causal, jnp.exp(jnp.where(causal, diff, 0.0)), 0.0)
    kb = k * beta[..., None]
    m_low = jnp.where(strict, jnp.einsum('nhcid,nhcjd->nhcij', kb, k) * decay, 0.0)
    a_mat = m_low + jnp.eye(CHUNK, dtype=f32)
    rhs = jnp.concatenate([v * beta[..., None], kb * jnp.exp(gc)[..., None]], axis=-1)
    sol = lax.linalg.triangular_solve(a_mat, rhs, left_side=True, lower=True)
    u = sol[..., :DV]
    w = sol[..., DV:]
    qk = jnp.where(causal, jnp.einsum('nhcid,nhcjd->nhcij', q, k) * decay, 0.0)
    q_dec = q * jnp.exp(gc)[..., None]
    g_last = gc[..., -1]
    k_dec = k * jnp.exp(g_last[..., None] - gc)[..., None]

    def step(S, xs):
        u_c, w_c, qk_c, qd_c, kd_c, gl_c = xs
        v_new = u_c - jnp.einsum('nhid,nhde->nhie', w_c, S)
        o = jnp.einsum('nhid,nhde->nhie', qd_c, S) + jnp.einsum('nhij,nhje->nhie', qk_c, v_new)
        S = S * jnp.exp(gl_c)[..., None, None] + jnp.einsum('nhid,nhie->nhde', kd_c, v_new)
        return S, o

    xs = tuple(jnp.moveaxis(t, 2, 0) for t in (u, w, qk, q_dec, k_dec, g_last))
    S, o = lax.scan(step, S0, xs)
    o = jnp.transpose(o, (1, 0, 3, 2, 4)).reshape(N, L, H, DV)
    return o, S

def moe(xn, w_router, b_router, w_up, b_up, w_down, b_down):
    N, L, D = xn.shape
    T = N * L
    f32 = jnp.float32
    xf = xn.reshape(T, D)
    logits = (xf @ w_router + b_router).astype(f32)
    top_v, top_i = lax.top_k(logits, TOP_K)
    gates = jax.nn.softmax(top_v, axis=-1)
    A = T * TOP_K
    n_blocks = -(-A // MOE_BLOCK) + N_EXPERTS
    R = n_blocks * MOE_BLOCK
    flat_e = top_i.reshape(-1).astype(jnp.int32)
    order = jnp.argsort(flat_e)
    se = flat_e[order]
    stok = (order // TOP_K).astype(jnp.int32)
    sgate = gates.reshape(-1)[order]
    counts = jnp.bincount(flat_e, length=N_EXPERTS)
    padded = (counts + MOE_BLOCK - 1) // MOE_BLOCK * MOE_BLOCK
    pend = jnp.cumsum(padded)
    pstart = pend - padded
    start = jnp.cumsum(counts) - counts
    dest = pstart[se] + jnp.arange(A) - start[se]
    tok_pad = jnp.full((R,), T, dtype=jnp.int32).at[dest].set(stok)
    gate_pad = jnp.zeros((R,), f32).at[dest].set(sgate)
    block_e = jnp.minimum(jnp.searchsorted(pend, jnp.arange(n_blocks) * MOE_BLOCK, side='right'),
                          N_EXPERTS - 1)
    x_ext = jnp.concatenate([xf, jnp.zeros((1, D), xf.dtype)], axis=0)
    xb = x_ext[tok_pad].reshape(n_blocks, MOE_BLOCK, D)

    def expert_block(args):
        xblk, e = args
        hmid = xblk @ w_up[e] + b_up[e]
        hg = jnp.minimum(hmid[:, :D_FF], SWIGLU_LIMIT)
        hl = jnp.clip(hmid[:, D_FF:], -SWIGLU_LIMIT, SWIGLU_LIMIT)
        act = hg * jax.nn.sigmoid(SWIGLU_ALPHA * hg) * (hl + 1.0)
        return act @ w_down[e] + b_down[e]

    yb = lax.map(expert_block, (xb, block_e))
    contrib = yb.reshape(R, D).astype(f32) * gate_pad[:, None]
    y = jax.ops.segment_sum(contrib, tok_pad, num_segments=T + 1)[:T]
    return y.astype(xn.dtype).reshape(N, L, D)

def _layer(h, conf_hist, dn_hist, S0, front_pad, lp):
    (norm_mix, w_in, w_conf_dw, b_conf_dw, ln_conf_g, ln_conf_b, w_conf_out, b_conf_out,
     w_dn_conv, dn_a_log, dn_dt_bias, dn_norm_w, w_dn_out, w_out,
     norm_ffn, w_router, b_router, w_up, b_up, w_down, b_down) = lp
    N, L, _ = h.shape
    f32 = jnp.float32
    xn = rmsnorm(h, norm_mix)
    p = xn @ w_in
    u = p[..., O_GLU:O_GLU + D_CONV] * jax.nn.sigmoid(p[..., O_GLU + D_CONV:O_Q])
    u_hist = jnp.concatenate([conf_hist.astype(u.dtype), u], axis=1)
    c = causal_dwconv(u_hist, w_conf_dw) + b_conf_dw
    c = jax.nn.silu(layernorm(c, ln_conf_g, ln_conf_b))
    y_a = c @ w_conf_out + b_conf_out
    qkv_hist = jnp.concatenate([dn_hist.astype(p.dtype), p[..., O_Q:O_Z]], axis=1)
    qkv = jax.nn.silu(causal_dwconv(qkv_hist, w_dn_conv))
    q = l2norm(qkv[..., :DN_QK].reshape(N, L, DN_HEADS, DN_DK)) * (DN_DK ** -0.5)
    k = l2norm(qkv[..., DN_QK:2 * DN_QK].reshape(N, L, DN_HEADS, DN_DK))
    v = qkv[..., 2 * DN_QK:].reshape(N, L, DN_HEADS, DN_DV).astype(f32)
    beta = jax.nn.sigmoid(p[..., O_B:O_GATE].astype(f32))
    g = -jnp.exp(dn_a_log.astype(f32)) * jax.nn.softplus(p[..., O_A:O_B].astype(f32) + dn_dt_bias.astype(f32))
    back = (-(front_pad + L)) % CHUNK

    def pad(t):
        return jnp.pad(t, [(0, 0), (front_pad, back)] + [(0, 0)] * (t.ndim - 2))

    o, S = gated_delta_chunked(pad(q), pad(k), pad(v), pad(g), pad(beta), S0.astype(f32))
    o = o[:, front_pad:front_pad + L]
    o = o * lax.rsqrt(jnp.mean(o * o, axis=-1, keepdims=True) + EPS) * dn_norm_w.astype(f32)
    o = o * jax.nn.silu(p[..., O_Z:O_A].reshape(N, L, DN_HEADS, DN_DV).astype(f32))
    y_b = o.reshape(N, L, DN_V).astype(h.dtype) @ w_dn_out
    gate = jax.nn.sigmoid(p[..., O_GATE:])
    mixed = gate[..., :D_MODEL] * y_a + gate[..., D_MODEL:] * y_b
    h = h + mixed @ w_out
    h = h + moe(rmsnorm(h, norm_ffn), w_router, b_router, w_up, b_up, w_down, b_down)
    return h, u_hist[:, -(CONV_W - 1):], qkv_hist[:, -(SHORT_W - 1):], S

def setup_inputs(seed: int = 0) -> dict:
    key = jax.random.key(seed)
    ks = jax.random.split(key, 32)
    f32 = jnp.float32
    nrm = lambda k, shape, s: jax.random.normal(k, shape, f32) * s
    dt = jnp.exp(jax.random.uniform(ks[12], (DEPTH, DN_HEADS), f32, np.log(1e-3), np.log(1e-1)))
    return {
        'x_prompt': nrm(ks[0], (BATCH, SEQ, D_MODEL), 1.0),
        'x_sample': nrm(ks[1], (DEC_BATCH, DEC_SEQ, D_MODEL), 1.0),
        'state_conf_conv': nrm(ks[2], (DEPTH, DEC_BATCH, CONV_W - 1, D_CONV), 0.5),
        'state_dn_conv': nrm(ks[3], (DEPTH, DEC_BATCH, SHORT_W - 1, DN_QKV), 1.0),
        'state_dn_S': nrm(ks[4], (DEPTH, DEC_BATCH, DN_HEADS, DN_DK, DN_DV), 0.5),
        'meta_tokens': nrm(ks[5], (N_META, D_MODEL), 1.0),
        'norm_mix': 1.0 + nrm(ks[6], (DEPTH, D_MODEL), 0.02),
        'w_in': nrm(ks[7], (DEPTH, D_MODEL, IN_COLS), D_MODEL ** -0.5),
        'w_conf_dw': nrm(ks[8], (DEPTH, CONV_W, D_CONV), CONV_W ** -0.5),
        'b_conf_dw': nrm(ks[9], (DEPTH, D_CONV), 0.02),
        'ln_conf_g': 1.0 + nrm(ks[10], (DEPTH, D_CONV), 0.02),
        'ln_conf_b': nrm(ks[11], (DEPTH, D_CONV), 0.02),
        'w_conf_out': nrm(ks[13], (DEPTH, D_CONV, D_MODEL), D_CONV ** -0.5),
        'b_conf_out': nrm(ks[14], (DEPTH, D_MODEL), 0.02),
        'w_dn_conv': nrm(ks[15], (DEPTH, SHORT_W, DN_QKV), SHORT_W ** -0.5),
        'dn_a_log': jnp.log(jax.random.uniform(ks[16], (DEPTH, DN_HEADS), f32, 1.0, 16.0)),
        'dn_dt_bias': dt + jnp.log(-jnp.expm1(-dt)),
        'dn_norm_w': 1.0 + nrm(ks[17], (DEPTH, DN_DV), 0.02),
        'w_dn_out': nrm(ks[18], (DEPTH, DN_V, D_MODEL), DN_V ** -0.5),
        'w_out': nrm(ks[19], (DEPTH, D_MODEL, D_MODEL), D_MODEL ** -0.5),
        'norm_ffn': 1.0 + nrm(ks[20], (DEPTH, D_MODEL), 0.02),
        'w_router': nrm(ks[21], (DEPTH, D_MODEL, N_EXPERTS), D_MODEL ** -0.5),
        'b_router': nrm(ks[22], (DEPTH, N_EXPERTS), 0.01),
        'w_up': nrm(ks[23], (DEPTH, N_EXPERTS, D_MODEL, 2 * D_FF), D_MODEL ** -0.5),
        'b_up': nrm(ks[24], (DEPTH, N_EXPERTS, 2 * D_FF), 0.02),
        'w_down': nrm(ks[25], (DEPTH, N_EXPERTS, D_FF, D_MODEL), D_FF ** -0.5),
        'b_down': nrm(ks[26], (DEPTH, N_EXPERTS, D_MODEL), 0.02),
        'norm_final': 1.0 + nrm(ks[27], (D_MODEL,), 0.02),
    }

def reference(x_prompt, x_sample, state_conf_conv, state_dn_conv, state_dn_S, meta_tokens,
              norm_mix, w_in, w_conf_dw, b_conf_dw, ln_conf_g, ln_conf_b, w_conf_out, b_conf_out,
              w_dn_conv, dn_a_log, dn_dt_bias, dn_norm_w, w_dn_out, w_out,
              norm_ffn, w_router, b_router, w_up, b_up, w_down, b_down, norm_final):
    B = x_prompt.shape[0]
    meta = jnp.broadcast_to(meta_tokens[None].astype(x_prompt.dtype), (B, N_META, D_MODEL))
    hp = jnp.concatenate([meta, x_prompt], axis=1)
    hs = x_sample
    prompt_front = (-N_META) % CHUNK
    sample_front = (PAST_LEN - N_META) % CHUNK
    cp, dp, sp, cs, ds, ss = [], [], [], [], [], []
    for l in range(DEPTH):
        lp = (norm_mix[l], w_in[l], w_conf_dw[l], b_conf_dw[l], ln_conf_g[l], ln_conf_b[l],
              w_conf_out[l], b_conf_out[l], w_dn_conv[l], dn_a_log[l], dn_dt_bias[l], dn_norm_w[l],
              w_dn_out[l], w_out[l], norm_ffn[l], w_router[l], b_router[l], w_up[l], b_up[l],
              w_down[l], b_down[l])
        hp, c1, c2, c3 = _layer(
            hp, jnp.zeros((B, CONV_W - 1, D_CONV), hp.dtype), jnp.zeros((B, SHORT_W - 1, DN_QKV), hp.dtype),
            jnp.zeros((B, DN_HEADS, DN_DK, DN_DV), jnp.float32), prompt_front, lp)
        hs, d1, d2, d3 = _layer(hs, state_conf_conv[l], state_dn_conv[l], state_dn_S[l], sample_front, lp)
        cp.append(c1); dp.append(c2); sp.append(c3)
        cs.append(d1); ds.append(d2); ss.append(d3)
    y_prompt = rmsnorm(hp, norm_final)[:, N_META:]
    y_sample = rmsnorm(hs, norm_final)
    return (y_prompt, y_sample, jnp.stack(cp), jnp.stack(dp), jnp.stack(sp),
            jnp.stack(cs), jnp.stack(ds), jnp.stack(ss))


_drawn_inputs = setup_inputs


def setup_inputs(seed=0):
    import zlib

    import numpy as np

    out = dict(_drawn_inputs(seed))
    spreads = {}
    factors = {'b_up': 5.39, 'b_down': 6.266, 'norm_final': 3.094}
    for name, (base, spread) in spreads.items():
        noise = np.random.default_rng([zlib.crc32(name.encode()), seed]).standard_normal(out[name].shape)
        drawn = base * np.exp(spread * noise) if base else spread * noise
        out[name] = __import__('jax').numpy.asarray(drawn.astype(out[name].dtype))
    for name, factor in factors.items():
        out[name] = (out[name] * factor).astype(out[name].dtype)
    return out
```

```python
import concourse.bass as bass
from concourse import mybir
from contextlib import ExitStack
import math

F32 = mybir.dt.float32
I32 = mybir.dt.int32
U32 = mybir.dt.uint32
ALU = mybir.AluOpType
ACT = mybir.ActivationFunctionType
AX = mybir.AxisListType

P = 128
D = 1024
KC = D // P
META = 16
SEQ = 256
NB, NS = 8, 4
PT = META + SEQ
T = PT + NB * NS
ROWS = [128, 128, T - 256]
TAIL = PT - 256
H = 8
CW = 31
CH = CW - 1
SW = 4
SH = SW - 1
UW = CH + PT + NB * (CH + NS)
QW = SH + PT + NB * (SH + NS)
NE = 32
TOPK = 4
SLOTS = 64
XB = 18
NBLK = NE + XB
HALF = 512
EPS = 1e-6
O_Z = 5120
O_A = 6144
O_GATE = 6160
BIG = 1e30
LEVELS = 7
LEVELS2 = 4

R_DW, R_NMIX, R_BDW, R_LNG, R_LNB, R_BCO, R_DN = 0, 31, 32, 33, 34, 35, 36
NROWS = R_DN + 3 * SW

WRING = 4
A_UH = WRING * 2048
A_XNT = A_UH + KC * UW
A_PRE = A_XNT + KC * T
A_XN = A_PRE + 8 * QW
A_PROW = A_XN + 3 * D
A_CH = A_PROW + D
A_S0 = 8192
A_PROJ = 16384
ARENA = 24576


def levels(eng, c):
    if c < 2:
        with eng.Fori(0, LEVELS) as lev:
            yield lev
    else:
        yield from range(LEVELS2)


def tile_tokens(c):
    return slice(128 * c, 128 * c + ROWS[c])


def build(nc, a):
    ctx = ExitStack()
    with ctx:
        def sb(name, shape, dt=F32):
            return ctx.enter_context(nc.sbuf_tensor(name, shape, dt))

        def sem(name):
            return ctx.enter_context(nc.semaphore(name))

        xn2_d = nc.dram_tensor("xn2_d", (T, D), F32, kind="Internal").ap()
        tok_d = nc.dram_tensor("tok_d", (SLOTS, NBLK), I32, kind="Internal").ap()
        y_d = nc.dram_tensor("y_d", (NBLK * SLOTS, D), F32, kind="Internal").ap()

        arena = sb("arena", [P, ARENA])
        xrow = sb("xrow", [P, 3, D])
        acc = sb("acc", [P, KC, T])
        qkv = sb("qkv", [P, 24, T])
        zs = sb("zs", [P, H, T])
        gate = sb("gate", [P, 2 * KC, T])
        pcol = sb("pcol", [P, KC, NROWS])
        ident = sb("ident", [P, P])
        ones = sb("ones", [P, P])
        causal = sb("causal", [P, P])
        causal2 = sb("causal2", [48, 48])
        same2 = sb("same2", [48, 48])
        neg = sb("neg", [P, P])
        neg2 = sb("neg2", [48, 48])
        segm = sb("segm", [48, 9])
        lmask = sb("lmask", [P, LEVELS, P])
        strict = sb("strict", [P, P])
        wab = sb("wab", [P, KC, 16])
        wr = sb("wr", [P, KC, NE])
        misc = sb("misc", [P, 720])
        temps = sb("temps", [P, 5 * 1024])

        off = [0]

        def small(n, dt=F32):
            v = misc[:, off[0]:off[0] + n]
            off[0] += n
            return v if dt == F32 else v.bitcast(dt)

        c_eps, c_one, c_lnq = small(1), small(1), small(1)
        half_col = small(1)
        dnw = small(1)
        ss = small(3)
        rstd = small(3)
        alog, dtb = small(8), small(8)
        abt = small(48).rearrange("p (c n) -> p c n", c=3)
        g_t = small(24).rearrange("p (c n) -> p c n", c=3)
        beta = small(24).rearrange("p (c n) -> p c n", c=3)
        nbeta = small(24).rearrange("p (c n) -> p c n", c=3)
        gw1 = small(24).rearrange("p (c n) -> p c n", c=3)
        gw2 = small(24).rearrange("p (c n) -> p c n", c=3)
        gcs = small(16)
        ekd = small(8)
        iota_e = small(32)
        tokid = small(3, I32)
        tokt = small(NBLK, I32)
        info_i = small(1 + XB, I32)
        idxcol = small(1, I32)
        brt = small(32)
        mx8 = small(24).rearrange("p (c n) -> p c n", c=3)
        ix8 = small(24, U32).rearrange("p (c n) -> p c n", c=3)
        gts = small(12).rearrange("p (c n) -> p c n", c=3)
        gsum = small(3)
        dli = small(12, I32).rearrange("p (c n) -> p c n", c=3)
        yli = small(12, I32).rearrange("p (c n) -> p c n", c=3)
        zero_i = small(NBLK, I32)
        wait_scratch = small(1)

        wring = arena[:, 0:WRING * 2048].rearrange("p (s k n) -> p s k n", s=WRING, k=KC)
        uh = arena[:, A_UH:A_XNT].rearrange("p (k n) -> p k n", k=KC)
        xnT = arena[:, A_XNT:A_PRE].rearrange("p (k n) -> p k n", k=KC)
        pre = arena[:, A_PRE:A_XN].rearrange("p (k n) -> p k n", k=8)
        xn = arena[:, A_XN:A_PROW].rearrange("p (c n) -> p c n", c=3)
        prow = arena[0:NROWS, A_PROW:A_CH]
        chrow = arena[0:120, A_CH:A_CH + 2 * D].rearrange("p (c n) -> p c n", c=2)
        dhrow = temps[0:24, 0:3072]
        dh = temps[:, 3072:3072 + 24 * 24].rearrange("p (k n) -> p k n", k=24)
        utail = temps[:, 3648:3648 + KC * 62].rearrange("p (k n) -> p k n", k=KC)
        qtail = temps[:, 4144:4144 + 24 * 27].rearrange("p (k n) -> p k n", k=24)
        uout = arena[0:62, 0:1024]
        qout = arena[0:27, 1024:4096]

        def unit(n, w=1):
            if n < 5:
                return temps[:, n * 1024:(n + w) * 1024]
            return arena[:, (n - 5) * 1024:(n - 5 + w) * 1024]

        def heads(u, R):
            return u[:, 0:H * R].rearrange("p (h n) -> p h n", h=H)
        u_dt, u_eg, u_um, u_kb, u_s = (unit(n) for n in range(5))
        u_kqe, u_u, u_qk, u_kd, u_vb, u_x, u_xt = unit(5, 2), unit(7), unit(8), unit(9), unit(10), unit(11), unit(12)
        S = u_s.rearrange("p (h n) -> p h n", h=H)
        s0 = arena[:, A_S0:A_S0 + 8192].rearrange("p (h n v) -> p h n v", h=H, n=NB)
        kqs = u_u[:, 0:768].rearrange("p (h a n) -> p h a n", h=H, a=2)
        vbd = qkv[:, 16:24, :].rearrange("p k n -> p (k n)")[0:48, 0:2304].rearrange("p (b s v) -> p b s v", b=2, s=9)
        proj = arena[:, A_PROJ:A_PROJ + 8192].rearrange("p (k n) -> p k n", k=KC)
        wout = arena[:, A_S0:A_S0 + 8192].rearrange("p (k n) -> p k n", k=KC)
        sq = arena[:, 0:KC * T].rearrange("p (k n) -> p k n", k=KC)
        mu = temps[:, 0:T]
        rs = [temps[:, 1024:1024 + T], temps[:, 2048:2048 + T]]
        sqh = [temps[:, 3072:3072 + T], temps[:, 4096:4096 + T]]

        nffn = acc[:, :, :].rearrange("p k n -> p (k n)")[:, 0:1024]
        nfin = acc[:, :, :].rearrange("p k n -> p (k n)")[:, 1024:2048]
        qflat = qkv[:, :, :].rearrange("p k n -> p (k n)")
        xn2 = gate[:, :, :].rearrange("p k n -> p (k n)")[:, 0:3072].rearrange("p (c n) -> p c n", c=3)
        xn2T = zs
        lg = temps[:, 0:96].rearrange("p (c n) -> p c n", c=3)
        oh = temps[:, 128:512].rearrange("p (c r n) -> p c r n", c=3, r=TOPK)
        ohm = temps[:, 512:896].rearrange("p (c r n) -> p c r n", c=3, r=TOPK)
        rt = [temps[:, 1024 + 96 * i:1120 + 96 * i].rearrange("p (c n) -> p c n", c=3) for i in range(9)]
        cnt, nbx, xs, ci = (temps[:, 2048 + 32 * i:2080 + 32 * i] for i in range(4))
        cs = [temps[:, 2304 + 32 * i:2336 + 32 * i] for i in range(2)]
        ixf = temps[:, 2400:2424].rearrange("p (c n) -> p c n", c=3)
        self_ = temps[:, 2432:2444].rearrange("p (c n) -> p c n", c=3)
        xio = temps[0:1, 2448:2448 + XB]
        info = temps[0:1, 2480:2480 + 1 + XB]
        bx = [temps[0:1, 2560 + 576 * i:3136 + 576 * i].rearrange("p (x e) -> p x e", x=XB) for i in range(3)]

        xg = qflat[:, 0:512]
        xgT = qflat[:, 512:1024].rearrange("p (c a n) -> p c a n", c=4, a=2)
        hg = qflat[:, 1024:1536]
        sg = qflat[:, 1536:2048]
        hl = qflat[:, 2048:2560]
        hgl = qflat[:, 2560:3072]
        act_h = qflat[:, 3072:3584]
        actT = qflat[:, 3584:4096].rearrange("p (c a n) -> p c a n", c=4, a=2)
        ysb = qflat[:, 4096:4608]
        brow = qflat[0:2, 4608:6144].rearrange("p (a n) -> p a n", a=3)
        halves = qflat[0:2, 6144:6272]
        wup = [arena[:, 2048 * k:2048 * (k + 1)] for k in range(KC)]
        wdn = [arena[:, A_PROJ + 1024 * k:A_PROJ + 1024 * (k + 1)] for k in range(KC)]
        ygat = [arena[:, 1024 * i:1024 * (i + 1)] for i in range(12)]

        bank = [ctx.enter_context(nc.psum_tensor(f"bank{i}", [P, 512], F32)) for i in range(8)]

        names = """y_zero y_zeroed x_in par_in small_in hist_in chist_in const_ready pool_chain dve_chain act_chain ss_ready rstd_ready
            xn_ready job_done job_evac ab_done win_used win_bank_free u_ready conf_done qkv_copied conv_ready
            silu_done tail_t_done tail_evac tail_out sum_done sumsq_done centered squared rstd_c scaled
            conf_act proj_in conf_mm_done conf_mm_evac l2_sq l2_sum l2_inv l2_scaled ab_ready beta_ready small_mm
            ekd_arg ekd_ready gl_ready bl_ready rows_done brow_done dt_arg dt_ready eg_ready kb_ready uq_done uq_evac
            tok_done tok_evac um_ready zt_done zt_copied vt_done x_updated kes_done r_ready vn_done vn_ready o_done
            o_evac s_done s_evac s0_in seg_done seg_copied vbd_ready sn_done s_out on_sq on_sum on_inv o_ready
            projd_in y_mm_done y_mm_evac wout_in o_mm_done h_ready hrstd_ready xn2_ready xn2_stored xn2t_done
            xn2t_evac lg_done gsub_ready gexp_ready mask_ready pos_done idx_ready zero_in scattered tok_in tok_ready
            norms_in bias_in bias_used up_used down_used xg_in xgt_done xgt_ready hg_ready sg_ready act_ready
            actt_done actt_ready y_ready y_stored experts_done fsq_ready frstd_ready final_ready out_done
            sampleconf_out idx_copied conv_chain expert_chain""".split()
        s = {n: sem(n) for n in names}
        win_in = [sem(f"win_in{i}") for i in range(WRING)]
        up_in = [sem(f"up_in{i}") for i in range(KC)]
        down_in = [sem(f"down_in{i}") for i in range(KC)]
        y_in = [sem(f"y_in{i}") for i in range(TOPK)]

        block = ctx.enter_context(nc.Block())

        w_in_v = a["w_in"][0].rearrange("(k p) n -> p k n", p=P)
        w_up_v = a["w_up"][0].rearrange("e (k p) n -> p e k n", p=P)
        w_dn_v = a["w_down"][0].rearrange("e (k p) n -> p e k n", p=P)
        b_up_v = a["b_up"][0].rearrange("e (a f n) -> f e a n", a=2, f=2)
        b_dn_v = a["b_down"][0].rearrange("e (f n) -> f e n", f=2)

        def prompt_u(k):
            return uh[:, k, CH:CH + PT]

        def sample_u(k):
            return uh[:, k, CH + PT:UW].rearrange("p (n t) -> p n t", n=NB)

        def tok2(v):
            return v[:, PT:T].rearrange("p (n t) -> p n t", n=NB)

        @block.sync
        def _(sp):
            for dst, src in ((xrow[0:META, 0, :], a["meta_tokens"]),
                             (xrow[META:128, 0, :], a["x_prompt"][0, 0:112, :]),
                             (xrow[:, 1, :], a["x_prompt"][0, 112:240, :]),
                             (xrow[0:TAIL, 2, :], a["x_prompt"][0, 240:256, :]),
                             (xrow[TAIL:48, 2, :], a["x_sample"].rearrange("n t d -> (n t) d"))):
                sp.dma_start(dst, src).then_inc(s["x_in"], 16)
            for r, src in ((R_DW, a["w_conf_dw"][0]), (R_NMIX, a["norm_mix"]), (R_BDW, a["b_conf_dw"]),
                           (R_LNG, a["ln_conf_g"]), (R_LNB, a["ln_conf_b"]), (R_BCO, a["b_conf_out"]),
                           (R_DN, a["w_dn_conv"][0].rearrange("t (a n) -> (t a) n", a=3))):
                sp.dma_start(prow[r:r + src.shape[0], :], src).then_inc(s["par_in"], 16)

            def win_load(step, col_a, col_b):
                slot = step % WRING
                for j, col in enumerate((col_a, col_b)):
                    sp.dma_start(wring[:, slot, :, 128 * j:128 * (j + 1)],
                                 w_in_v[:, :, bass.ds(col, 128)]).then_inc(win_in[slot], 16)

            for j in range(WRING):
                win_load(j, 128 * j, D + 128 * j)
            sp.dma_start(wab[:, :, :], w_in_v[:, :, O_A:O_GATE]).then_inc(s["small_in"], 16)
            sp.dma_start(alog, a["dn_a_log"].to_broadcast((P, H))).then_inc(s["small_in"], 16)
            sp.dma_start(dtb, a["dn_dt_bias"].to_broadcast((P, H))).then_inc(s["small_in"], 16)
            sp.dma_start(dnw, a["dn_norm_w"].rearrange("a n -> n a")).then_inc(s["small_in"], 16)
            sp.dma_start(wr[:, :, :], a["w_router"][0].rearrange("(k p) n -> p k n", p=P)).then_inc(s["small_in"], 16)
            sp.dma_start(brt, a["b_router"].to_broadcast((P, NE))).then_inc(s["small_in"], 16)
            for t in range(2):
                sp.dma_start(chrow[:, t, :], a["state_conf_conv"][0, 4 * t:4 * t + 4].rearrange("n t d -> (n t) d")
                             ).then_inc(s["chist_in"], 16)
            sp.dma_start(dhrow, a["state_dn_conv"][0].rearrange("n t d -> (n t) d")).then_inc(s["hist_in"], 16)
            for j in range(WRING):
                sp.wait_ge(s["win_used"], j + 1)
                win_load(j, 128 * (WRING + j), D + 128 * (WRING + j))

            def win_group(it, col0):
                for j in range(WRING):
                    sp.wait_ge(s["win_used"], WRING * it + j - (WRING - 1))
                    win_load(j, col0 + 256 * j, col0 + 256 * j + 128)

            with sp.Fori(2, 6) as it:
                win_group(it, it * 1024)
            with sp.Fori(6, 8) as it:
                win_group(it, it * 1024 + (O_GATE - 6 * 1024))
            sp.wait_ge(s["conv_ready"], 24)
            sp.wait_ge(s["job_evac"], 14)
            sp.dma_start(proj[:, :, :], a["w_conf_out"][0].rearrange("(k p) n -> p k n", p=P)).then_inc(s["proj_in"], 16)
            sp.wait_ge(s["conf_done"], KC)
            sp.wait_ge(s["win_used"], 32)
            sp.wait_ge(s["win_bank_free"], 34)
            for h in range(H):
                sp.dma_start(s0[:, h, :, :], a["state_dn_S"][0, :, h].rearrange("n k v -> k n v")
                             ).then_inc(s["s0_in"], 16)
            sp.wait_ge(s["conf_mm_done"], KC)
            sp.dma_start(proj[:, :, :], a["w_dn_out"][0].rearrange("(k p) n -> p k n", p=P)).then_inc(s["projd_in"], 16)
            sp.wait_ge(s["s_out"], 16 * (H + 1))
            sp.dma_start(wout[:, :, :], a["w_out"][0].rearrange("(k p) n -> p k n", p=P)).then_inc(s["wout_in"], 16)
            sp.wait_ge(s["conf_act"], KC)
            sp.wait_ge(s["conf_mm_done"], KC)
            sp.dma_start(nffn, a["norm_ffn"].to_broadcast((P, D))).then_inc(s["norms_in"], 16)
            sp.dma_start(nfin, a["norm_final"].rearrange("(a n) -> a n", a=1).to_broadcast((P, D))
                         ).then_inc(s["norms_in"], 16)

            def load_up(e, k):
                sp.dma_start(wup[k], w_up_v[:, e, k, :]).then_inc(up_in[k], 16)

            def load_down(e, k):
                sp.dma_start(wdn[k], w_dn_v[:, e, k, :]).then_inc(down_in[k], 16)

            def load_bias(e):
                sp.dma_start(brow[:, 0:2, :], b_up_v[:, e, :, :]).then_inc(s["bias_in"], 16)
                sp.dma_start(brow[:, 2, :], b_dn_v[:, e, :]).then_inc(s["bias_in"], 16)

            for k in range(4):
                load_up(0, k)
            sp.wait_ge(s["y_mm_done"], KC)
            for k in range(KC):
                load_down(0, k)
            load_bias(0)
            sp.wait_ge(s["o_mm_done"], 6)
            for k in range(4, KC):
                load_up(0, k)

            def load_block(b, e):
                for k in range(KC):
                    sp.wait_ge(s["up_used"], KC * b + k - (KC - 1))
                    load_up(e, k)
                sp.wait_ge(s["bias_used"], b)
                load_bias(e)
                for k in range(KC):
                    sp.wait_ge(s["down_used"], KC * b + k - (KC - 1))
                    load_down(e, k)

            with sp.Fori(1, NE) as b:
                load_block(b, b)
            sp.wait_ge(s["idx_ready"], 1)
            nx = sp.value_load(info_i[0:1, 0:1], min_val=0, max_val=XB)
            with sp.Fori(0, XB) as x:
                with sp.If(x < nx):
                    e = sp.value_load(info_i[0:1, bass.ds(x + 1, 1)], min_val=0, max_val=NE - 1)
                    load_block(x + NE, e)

            sp.wait_ge(s["final_ready"], 3)
            for dst, src in ((a["y_prompt"][0, 0:112, :], xn2[META:128, 0, :]),
                             (a["y_prompt"][0, 112:240, :], xn2[:, 1, :]),
                             (a["y_prompt"][0, 240:256, :], xn2[0:TAIL, 2, :]),
                             (a["y_sample"].rearrange("n t d -> (n t) d"), xn2[TAIL:48, 2, :])):
                sp.dma_start(dst, src).then_inc(s["out_done"], 16)
            sp.wait_ge(s["out_done"], 64)

        @block.gpsimd
        def _(pool):
            n = [0]

            def then(ins):
                n[0] += 1
                ins.then_inc(s["pool_chain"], 1)
                pool.wait_ge(s["pool_chain"], n[0])

            def keep(v, pattern, base, cm):
                then(nc.gpsimd.affine_select(out=v, in_=v, compare_op=ALU.is_ge, fill=0.0, base=base,
                                             pattern=pattern, channel_multiplier=cm))

            for v, c in ((ident, 0.0), (ones, 1.0), (causal, 1.0), (lmask, 0.0), (same2, 0.0)):
                nc.gpsimd.memset(v[:], c)
            for v, c in ((c_eps, EPS), (c_one, 1.0), (c_lnq, -0.5 * math.log(P)), (zero_i, 0)):
                nc.gpsimd.memset(v, c)
            nc.gpsimd.iota(tokid, pattern=[[128, 3]], base=0, channel_multiplier=1)
            then(nc.gpsimd.iota(iota_e, pattern=[[1, NE]], base=0, channel_multiplier=0,
                                allow_small_or_imprecise_dtypes=True))
            nc.gpsimd.tensor_scalar(half_col, tokid[:, 0:1], 64.0, None, ALU.is_ge)
            then(nc.gpsimd.affine_select(out=ident[:], in_=ident[:], compare_op=ALU.not_equal, fill=1.0, base=0,
                                         pattern=[[-1, P]], channel_multiplier=1))
            keep(causal[:], [[1, P]], 0, -1)
            for lev in range(LEVELS):
                b = 1 << lev
                v = lmask[:, lev, :].rearrange("p (n a b) -> p n a b", a=2, b=b)[:, :, 1, :]
                then(nc.gpsimd.memset(v, 1.0))
                keep(v, [[-2 * b, P // (2 * b)], [0, b]], 0, 1)
                keep(v, [[2 * b, P // (2 * b)], [0, b]], b - 1, -1)
            nc.gpsimd.memset(same2[:, 0:TAIL], 1.0)
            then(nc.gpsimd.memset(same2[:, TAIL:48], 1.0))
            keep(same2[:, 0:TAIL], [[0, TAIL]], TAIL - 1, -1)
            v = same2[:, TAIL:48].rearrange("p (n t) -> p n t", n=NB)
            keep(v, [[-NS, NB], [0, NS]], -TAIL, 1)
            keep(v, [[NS, NB], [0, NS]], TAIL + NS - 1, -1)
            nc.gpsimd.tensor_copy(segm[:, 0:1], same2[:, 0:1])
            nc.gpsimd.tensor_copy(segm[:, 1:9], same2[:, TAIL:48:NS])
            nc.gpsimd.tensor_tensor(strict[:], causal[:], ident[:], ALU.subtract)
            then(nc.gpsimd.tensor_tensor(causal2[:], same2[:], causal[0:48, 0:48], ALU.mult))
            nc.gpsimd.tensor_scalar(neg[:], causal[:], -1.0, BIG, ALU.add, ALU.mult)
            nc.gpsimd.tensor_scalar(neg2[:], causal2[:], -1.0, BIG, ALU.add, ALU.mult).then_inc(s["const_ready"], 1)
            pool.dma_start(tok_d, zero_i[0:SLOTS, :]).then_inc(s["zero_in"], 16)
            nc.gpsimd.memset(zs[:, 0:4, :], 0.0).then_inc(s["y_zero"], 1)
            pool.wait_ge(s["y_zero"], 1)
            pool.dma_start(y_d[NE * SLOTS:NBLK * SLOTS, :].rearrange("(p a) n -> p a n", p=P),
                           zs[:, 0:4, :].rearrange("p k n -> p (k n)")[:, 0:D].unsqueeze(1).to_broadcast((P, XB // 2, D))
                           ).then_inc(s["y_zeroed"], 16)
            pool.dma_start(a["cs"][0, :, 0:CH - NS, :], a["state_conf_conv"][0, :, NS:CH, :]
                           ).then_inc(s["sampleconf_out"], 16)
            pool.wait_ge(s["tail_evac"], 8)
            pool.dma_start(a["cp"][0, 0], uout[0:CH, :]).then_inc(s["tail_out"], 16)
            for b in range(NB):
                pool.dma_start(a["cs"][0, b, CH - NS:CH, :], uout[CH + NS * b:CH + NS * (b + 1), :]
                               ).then_inc(s["tail_out"], 16)
            pool.dma_start(a["dp"][0, 0], qout[0:SH, :]).then_inc(s["tail_out"], 16)
            pool.dma_start(a["ds"][0].rearrange("n t d -> (n t) d"), qout[SH:SH + NB * SH, :]
                           ).then_inc(s["tail_out"], 16)
            pool.wait_ge(s["tail_out"], 16 * (NB + 3))
            pool.wait_ge(s["sampleconf_out"], 16)

            for c in range(3):
                R = ROWS[c]
                cm = (causal if c < 2 else causal2)[0:R, 0:R]
                um, kb, uu = heads(u_um, R), heads(u_kb, R), heads(u_u, R)
                if c == 0:
                    pool.wait_ge(s["beta_ready"], 1)
                    pool.wait_ge(s["l2_scaled"], 16)
                if c:
                    pool.wait_ge(s["s_evac"], 2 * c)
                nc.gpsimd.tensor_tensor(um[0:R], g_t[0:R, c, :].unsqueeze(2).to_broadcast((R, H, R)),
                                        cm.unsqueeze(1).to_broadcast((R, H, R)), ALU.mult).then_inc(s["gl_ready"], 1)
                nc.gpsimd.tensor_tensor(kb[0:R], beta[0:R, c, :].unsqueeze(2).to_broadcast((R, H, R)),
                                        ident[0:R, 0:R].unsqueeze(1).to_broadcast((R, H, R)), ALU.mult
                                        ).then_inc(s["bl_ready"], 1)
                pool.wait_ge(s["uq_evac"], 4 * c + 2)
                for lev in levels(pool, c):
                    pool.wait_ge(s["zt_done"], lev * 2 + 14 * c)
                    nc.gpsimd.tensor_tensor(um[0:R], uu[0:R],
                                            lmask[0:R, bass.ds(lev, 1), 0:R].to_broadcast((R, H, R)), ALU.mult
                                            ).then_inc(s["um_ready"], 1)
                if c == 2:
                    for h in range(H):
                        pool.wait_ge(s["vn_ready"], 4 + h // 4 + 1)
                        if h >= 2:
                            pool.wait_ge(s["sn_done"], h - 1)
                        nc.gpsimd.tensor_tensor(vbd[:, h % 2, :, :],
                                                u_kb[0:48, :].rearrange("p (h n) -> p h n", h=H)[:, h, :].unsqueeze(1)
                                                .to_broadcast((48, 9, P)),
                                                segm[:].unsqueeze(2).to_broadcast((48, 9, P)), ALU.mult
                                                ).then_inc(s["vbd_ready"], 1)
                    for h in range(H):
                        pool.wait_ge(s["s_evac"], 4 + h + 1)
                        pool.dma_start(a["ss"][0, :, h].rearrange("n k v -> k n v"), s0[:, h, :, :]
                                       ).then_inc(s["s_out"], 16)
                    pool.dma_start(a["sp"][0, 0].rearrange("h k v -> k h v"), S).then_inc(s["s_out"], 16)
            pool.wait_ge(s["s_out"], 16 * (H + 1))

            pool.wait_ge(s["xn2_ready"], 3)
            for c in range(3):
                pool.dma_start(xn2_d[128 * c:128 * c + ROWS[c], :], xn2[0:ROWS[c], c, :]).then_inc(s["xn2_stored"], 16)
            pool.wait_ge(s["zero_in"], 16)
            pool.wait_ge(s["idx_ready"], 1)
            for c in range(3):
                for r in range(TOPK):
                    pool.indirect_dma_start(
                        out=tok_d.rearrange("a (b c) -> (a b) c", c=1),
                        out_offset=bass.IndirectOffsetOnAxis(ap=dli[0:ROWS[c], c, r:r + 1].bitcast(U32), axis=0),
                        in_=tokid[0:ROWS[c], c:c + 1], in_offset=None).then_inc(s["scattered"], 16)
            pool.wait_ge(s["scattered"], 16 * 3 * TOPK)
            for f in range(2):
                pool.dma_start(tokt[64 * f:64 * f + 64, :], tok_d).then_inc(s["tok_in"], 16)
            pool.wait_ge(s["tok_ready"], 1)
            pool.wait_ge(s["xn2_stored"], 48)
            xn2_halves = xn2_d.rearrange("t (f n) -> (t f) n", f=2)

            def gather(b):
                pool.wait_ge(s["xgt_done"], b)
                nc.gpsimd.tensor_copy(idxcol, tokt[:, bass.ds(b, 1)]).then_inc(s["idx_copied"], 1)
                pool.wait_ge(s["idx_copied"], b + 1)
                nc.gpsimd.tensor_tensor(wait_scratch, c_one, c_one, ALU.mult)
                pool.indirect_dma_start(out=xg, out_offset=None, in_=xn2_halves,
                                        in_offset=bass.IndirectOffsetOnAxis(ap=idxcol.bitcast(U32), axis=0)
                                        ).then_inc(s["xg_in"], 16)
                pool.wait_ge(s["xg_in"], b * 16 + 16)

            with pool.Fori(0, NE) as b:
                gather(b)
            nx = pool.value_load(info_i[0:1, 0:1], min_val=0, max_val=XB)
            with pool.Fori(0, XB) as x:
                with pool.If(x < nx):
                    gather(x + NE)
            pool.wait_ge(s["experts_done"], 1)
            for r in range(TOPK):
                for c in range(3):
                    pool.indirect_dma_start(out=ygat[3 * r + c][0:ROWS[c], :], out_offset=None, in_=y_d,
                                            in_offset=bass.IndirectOffsetOnAxis(
                                                ap=yli[0:ROWS[c], c, r:r + 1].bitcast(U32), axis=0)
                                            ).then_inc(y_in[r], 16)

        @block.tensor
        def _(pe):
            mm = nc.tensor.matmul
            pe.wait_ge(s["const_ready"], 1)
            job = [0]

            def job_bank():
                if job[0] >= 8:
                    pe.wait_ge(s["job_evac"], job[0] - 7)
                return bank[job[0] % 8]

            def transposes(parts):
                b = job_bank()
                for src, col in parts:
                    k, m = src.shape
                    last = nc.tensor.transpose(b[0:m, col:col + k], src, ident[0:k, 0:k])
                last.then_inc(s["job_done"], 1)
                job[0] += 1

            pe.wait_ge(s["par_in"], 112)
            transposes([(prow[:, P * k:P * (k + 1)], NROWS * k) for k in range(KC)])
            pe.wait_ge(s["xn_ready"], 3)
            for c in range(3):
                for g in range(2):
                    transposes([(xn[0:ROWS[c], c, P * k:P * (k + 1)], ROWS[c] * (k % 4)) for k in range(4 * g, 4 * g + 4)])
            pe.wait_ge(s["chist_in"], 32)
            for t in range(2):
                for g in range(2):
                    transposes([(chrow[:, t, P * k:P * (k + 1)], 120 * (k % 4)) for k in range(4 * g, 4 * g + 4)])
            pe.wait_ge(s["hist_in"], 16)
            for g in range(2):
                transposes([(dhrow[:, P * k:P * (k + 1)], 24 * (k % 12)) for k in range(12 * g, 12 * g + 12)])
            pe.wait_ge(s["job_evac"], 7)
            pe.wait_ge(s["small_in"], 96)
            b = job_bank()
            for c in range(3):
                for k in range(KC):
                    last = mm(b[0:ROWS[c], 16 * c:16 * c + 16], xnT[:, k, tile_tokens(c)], wab[:, k, :],
                              start=(k == 0), stop=(k == KC - 1))
            last.then_inc(s["ab_done"], 1)
            pe.wait_ge(s["job_evac"], 13)
            with pe.Fori(0, 8) as it:
                for j in range(WRING):
                    pe.wait_ge(win_in[j], it * 32 + 32)
                    pe.wait_ge(s["win_bank_free"], it * WRING + (j + 1))
                    for f in range(2):
                        for k in range(KC):
                            last = mm(bank[2 * (j % 2) + f][:, 0:T], wring[:, j, k, P * f:P * (f + 1)], xnT[:, k, :],
                                      start=(k == 0), stop=(k == KC - 1))
                    last.then_inc(s["win_used"], 1)
                    last_step = last
            pe.wait_ge(s["win_bank_free"], 34)
            for g in range(2):
                for k in range(4 * g, 4 * g + 4):
                    last = nc.tensor.transpose(bank[4 + g][0:62, P * (k % 4):P * (k % 4 + 1)], utail[:, k, :], ident[:])
                last.then_inc(s["tail_t_done"], 1)
            for g in range(6):
                if g >= 2:
                    pe.wait_ge(s["tail_evac"], g - 1)
                bk = bank[4 + (g + 2) % 4]
                for k in range(4 * g, 4 * g + 4):
                    last = nc.tensor.transpose(bk[0:27, P * (k % 4):P * (k % 4 + 1)], qtail[:, k, :], ident[:])
                last.then_inc(s["tail_t_done"], 1)
            pe.wait_ge(s["tail_evac"], 8)

            pe.wait_ge(s["conf_done"], KC)
            for k in range(KC):
                last = mm(bank[4][:, 0:T], ones[:], acc[:, k, :], start=(k == 0), stop=(k == KC - 1))
            last.then_inc(s["sum_done"], 1)
            pe.wait_ge(s["squared"], 1)
            for k in range(KC):
                last = mm(bank[5][:, 0:T], ones[:], sq[:, k, :], start=(k == 0), stop=(k == KC - 1))
            last.then_inc(s["sumsq_done"], 1)
            pe.wait_ge(s["proj_in"], 16)
            pe.wait_ge(s["conf_act"], KC)
            for m in range(KC):
                if m >= 2:
                    pe.wait_ge(s["conf_mm_evac"], m - 1)
                for k in range(KC):
                    last = mm(bank[6 + m % 2][:, 0:T], proj[:, k, P * m:P * (m + 1)], acc[:, k, :],
                              start=(k == 0), stop=(k == KC - 1))
                last.then_inc(s["conf_mm_done"], 1)

            for j in range(16):
                pe.wait_ge(s["l2_sq"], j + 1)
                if j >= 2:
                    pe.wait_ge(s["l2_inv"], j - 1)
                mm(bank[j % 2][:, 0:T], ones[:], sqh[j % 2], start=True, stop=True).then_inc(s["l2_sum"], 1)

            for c in range(3):
                R = ROWS[c]
                tt = tile_tokens(c)
                cm = (causal if c < 2 else causal2)[0:R, 0:R]
                sm = ones[0:R, 0:R] if c < 2 else same2[:, :]
                um, kb, dt, eg, uu, qk, x, xt = (heads(v, R) for v in
                                                 (u_um, u_kb, u_dt, u_eg, u_u, u_qk, u_x, u_xt))
                kqe = u_kqe[:, 0:2 * H * R].rearrange("p (h a n) -> p h a n", h=H, a=2)
                kd, vb, vn = (v.rearrange("p (h n) -> p h n", h=H) for v in (u_kd, u_vb, u_kb))
                zt = dt
                if c == 0:
                    pe.wait_ge(s["beta_ready"], 1)
                    pe.wait_ge(s["l2_scaled"], 16)
                else:
                    pe.wait_ge(s["s_evac"], 2 * c)
                    pe.wait_ge(s["o_evac"], 2 * c)
                mm(bank[0][0:R, 0:8], cm, g_t[0:R, c, :], start=True, stop=True)
                mm(bank[0][0:R, 8:16], sm, g_t[0:R, c, :], start=True, stop=True).then_inc(s["small_mm"], 1)
                pe.wait_ge(s["gl_ready"], c + 1)
                for g in range(2):
                    mm(bank[1 + g][:, 0:4 * R], ones[0:R, :], um[0:R, 4 * g:4 * g + 4, :], start=True, stop=True
                       ).then_inc(s["rows_done"], 1)
                pe.wait_ge(s["bl_ready"], c + 1)
                for g in range(2):
                    mm(bank[3 + g][:, 0:4 * R], ones[0:R, :], kb[0:R, 4 * g:4 * g + 4, :], start=True, stop=True
                       ).then_inc(s["brow_done"], 1)
                for g in range(2):
                    pe.wait_ge(s["kb_ready"], 2 * c + 2)
                    for kind, (bk, rhs) in enumerate(((bank[5 + g], kb), (bank[7 - 7 * g], None))):
                        for h in range(4 * g, 4 * g + 4):
                            mv = kb[:, h, :] if kind == 0 else qkv[:, h, tt]
                            last = mm(bk[0:R, R * (h % 4):R * (h % 4 + 1)], qkv[:, H + h, tt], mv, start=True, stop=True)
                        last.then_inc(s["uq_done"], 1)
                for g in range(4):
                    if g == 0:
                        pe.wait_ge(s["dt_arg"], c + 1)
                    for h in range(4 * (g % 2), 4 * (g % 2) + 4):
                        last = nc.tensor.transpose(bank[1 + g][0:R, P * (h % 4):P * (h % 4 + 1)],
                                                   qkv[:, H + h if g < 2 else 2 * H + h, tt], ident[:])
                    last.then_inc(s["tok_done"], 1)
                pe.wait_ge(s["uq_evac"], 4 * c + 4)
                pe.wait_ge(s["tok_evac"], 4 * c + 4)
                pe.wait_ge(s["x_updated"], 15 * c + 1)
                for lev in levels(pe, c):
                    pe.wait_ge(s["um_ready"], lev + (7 * c + 1))
                    for g in range(2):
                        pe.wait_ge(s["x_updated"], lev * 2 + (15 * c + g))
                        for h in range(4 * g, 4 * g + 4):
                            last = mm(bank[g][0:R, R * (h % 4):R * (h % 4 + 1)], um[0:R, h, :], xt[0:R, h, :],
                                      start=True, stop=True)
                        last.then_inc(s["zt_done"], 1)
                    for g in range(2):
                        pe.wait_ge(s["zt_copied"], lev * 2 + (14 * c + g + 1))
                        for h in range(4 * g, 4 * g + 4):
                            mm(bank[2 + g][0:R, R * (h % 4):R * (h % 4 + 1)], zt[0:R, h, :], x[0:R, h, :],
                               start=True, stop=True)
                        for h in range(4 * g, 4 * g + 4):
                            last = mm(bank[4 + g][0:R, R * (h % 4):R * (h % 4 + 1)], x[0:R, h, :], zt[0:R, h, :],
                                      start=True, stop=True)
                        last.then_inc(s["vt_done"], 1)
                pe.wait_ge(s["x_updated"], 15 * c + 1 + 2 * (LEVELS if c < 2 else LEVELS2))
                if c == 1:
                    for g in range(2):
                        for h in range(4 * g, 4 * g + 4):
                            last = mm(bank[6 + g][0:R, P * (h % 4):P * (h % 4 + 1)], kqe[:, h, 0, :], S[:, h, :],
                                      start=True, stop=True)
                        last.then_inc(s["kes_done"], 1)
                if c == 2:
                    for g in range(2):
                        for h in range(4 * g, 4 * g + 4):
                            pe.wait_ge(s["s0_in"], 16 * H)
                            bv = bank[6 + g][:, 96 * (h % 4):96 * (h % 4 + 1)].rearrange("p (a n) -> p a n", a=2)
                            mm(bv[:, :, 0:TAIL], S[:, h, :], kqe[:, h, :, 0:TAIL], start=True, stop=True)
                            for b in range(NB):
                                w = slice(TAIL + NS * b, TAIL + NS * (b + 1))
                                last = mm(bv[:, :, w], s0[:, h, b, :], kqe[:, h, :, w], start=True, stop=True)
                        last.then_inc(s["seg_done"], 1)
                    for g in range(2):
                        pe.wait_ge(s["seg_copied"], g + 1)
                        for h in range(4 * g, 4 * g + 4):
                            last = nc.tensor.transpose(bank[4 + g][0:R, P * (h % 4):P * (h % 4 + 1)],
                                                       kqs[:, h, 0, :], ident[:])
                        last.then_inc(s["kes_done"], 1)
                for g in range(2):
                    if c:
                        pe.wait_ge(s["r_ready"], 2 * (c - 1) + g + 1)
                    for h in range(4 * g, 4 * g + 4):
                        last = mm(bank[g][0:R, P * (h % 4):P * (h % 4 + 1)], x[0:R, h, :], vb[0:R, h, :],
                                  start=True, stop=True)
                    last.then_inc(s["vn_done"], 1)
                for g in range(2):
                    pe.wait_ge(s["vn_ready"], 2 * c + g + 1)
                    for h in range(4 * g, 4 * g + 4):
                        o = bank[2 + g][:, R * (h % 4):R * (h % 4 + 1)]
                        if c == 1:
                            mm(o, S[:, h, :], kqe[:, h, 1, :], start=True, stop=False)
                        last = mm(o, vn[0:R, h, :], qk[0:R, h, :], start=(c != 1), stop=True)
                    last.then_inc(s["o_done"], 1)
                if c < 2:
                    for g in range(2):
                        for h in range(4 * g, 4 * g + 4):
                            last = mm(bank[4 + g][:, P * (h % 4):P * (h % 4 + 1)], kd[0:R, h, :], vn[0:R, h, :],
                                      start=True, stop=True)
                        last.then_inc(s["s_done"], 1)
                else:
                    for h in range(H):
                        pe.wait_ge(s["vbd_ready"], h + 1)
                        if h == 0:
                            pe.wait_ge(s["r_ready"], 4)
                        if h == 1:
                            pe.wait_ge(s["o_evac"], 6)
                        if h >= 2:
                            pe.wait_ge(s["s_evac"], 4 + h - 1)
                        bs = (bank[4], bank[5], bank[6]) if h % 2 == 0 else (bank[7], bank[2], bank[3])
                        for q, (lo, hi) in enumerate(((0, 4), (4, 8), (8, 9))):
                            last = mm(bs[q][:, 0:P * (hi - lo)], kd[0:R, h, :], vbd[:, h % 2, lo:hi, :],
                                      start=True, stop=True)
                        last.then_inc(s["sn_done"], 1)

            for h in range(H):
                pe.wait_ge(s["on_sq"], h + 1)
                if h >= 2:
                    pe.wait_ge(s["on_inv"], h - 1)
                mm(bank[h % 2][:, 0:T], ones[:], sqh[h % 2], start=True, stop=True).then_inc(s["on_sum"], 1)
            pe.wait_ge(s["projd_in"], 16)
            pe.wait_ge(s["o_ready"], H)
            pe.wait_ge(s["s_evac"], 12)
            for m in range(KC):
                if m >= 2:
                    pe.wait_ge(s["y_mm_evac"], m - 1)
                for k in range(KC):
                    last = mm(bank[2 + m % 2][:, 0:T], proj[:, k, P * m:P * (m + 1)], qkv[:, k, :],
                              start=(k == 0), stop=(k == KC - 1))
                last.then_inc(s["y_mm_done"], 1)
            pe.wait_ge(s["wout_in"], 16)
            pe.wait_ge(s["y_mm_evac"], KC)
            for c in range(3):
                for f in range(2):
                    bk = bank[(4, 5, 6, 7, 0, 1)[2 * c + f]]
                    for k in range(KC):
                        last = mm(bk[0:ROWS[c], :], gate[:, k, tile_tokens(c)], wout[:, k, HALF * f:HALF * (f + 1)],
                                  start=(k == 0), stop=(k == KC - 1))
                    last.then_inc(s["o_mm_done"], 1)
            for c in range(3):
                pe.wait_ge(s["xn2_ready"], c + 1)
                for g in range(2):
                    n = 2 * c + g
                    if n >= 2:
                        pe.wait_ge(s["xn2t_evac"], n - 1)
                    for k in range(4 * g, 4 * g + 4):
                        last = nc.tensor.transpose(bank[2 + g][:, ROWS[c] * (k % 4):ROWS[c] * (k % 4 + 1)],
                                                   xn2[0:ROWS[c], c, P * k:P * (k + 1)], ident[0:ROWS[c], 0:ROWS[c]])
                    last.then_inc(s["xn2t_done"], 1)
            pe.wait_ge(s["xn2t_evac"], 6)
            pe.wait_ge(s["h_ready"], 6)
            for c in range(3):
                for k in range(KC):
                    last = mm(bank[4][0:ROWS[c], NE * c:NE * (c + 1)], xn2T[:, k, tile_tokens(c)], wr[:, k, :],
                              start=(k == 0), stop=(k == KC - 1))
            last.then_inc(s["lg_done"], 1)
            pe.wait_ge(s["mask_ready"], 1)
            mask = rt[0]
            for c in range(3):
                out = bank[5][0:ROWS[c], NE * c:NE * (c + 1)]
                for c2 in range(c):
                    mm(out, ones[:, 0:ROWS[c]], mask[:, c2, :], start=(c2 == 0), stop=False)
                mm(out, strict[0:ROWS[c], 0:ROWS[c]], mask[0:ROWS[c], c, :], start=(c == 0), stop=True)
            for c in range(3):
                last = mm(bank[5][:, 96:128], ones[0:ROWS[c], :], mask[0:ROWS[c], c, :], start=(c == 0), stop=(c == 2))
            last.then_inc(s["pos_done"], 1)

            def expert(b):
                pe.wait_ge(s["xg_in"], b * 16 + 16)
                for q in range(4):
                    last = nc.tensor.transpose(bank[0][:, P * q:P * (q + 1)], xg[:, P * q:P * (q + 1)], ident[:])
                last.then_inc(s["xgt_done"], 1)
                pe.wait_ge(s["bias_in"], b * 32 + 32)
                pe.wait_ge(s["act_ready"], b)
                for v in range(2):
                    mm(bank[1 + v][:], halves, brow[:, v, :], start=True, stop=False, skip_group_check=True)
                pe.wait_ge(s["xgt_ready"], b + 1)
                for k in range(KC):
                    pe.wait_ge(up_in[k], b * 16 + 16)
                    for v in range(2):
                        for f in range(2):
                            last = mm(bank[1 + v][64 * f:64 * f + 64, :], xgT[:, k % 4, k // 4, :],
                                      wup[k][:, D * v + HALF * f:D * v + HALF * (f + 1)],
                                      start=False, stop=(k == KC - 1), skip_group_check=True)
                    last.then_inc(s["up_used"], 1)
                pe.wait_ge(s["y_ready"], b)
                mm(bank[4][:], halves, brow[:, 2, :], start=True, stop=False, skip_group_check=True
                   ).then_inc(s["bias_used"], 1)
                pe.wait_ge(s["act_ready"], b + 1)
                for q in range(4):
                    last = nc.tensor.transpose(bank[3][:, P * q:P * (q + 1)], act_h[:, P * q:P * (q + 1)], ident[:])
                last.then_inc(s["actt_done"], 1)
                pe.wait_ge(s["actt_ready"], b + 1)
                for k in range(KC):
                    pe.wait_ge(down_in[k], b * 16 + 16)
                    for f in range(2):
                        last = mm(bank[4][64 * f:64 * f + 64, :], actT[:, k % 4, k // 4, :],
                                  wdn[k][:, HALF * f:HALF * (f + 1)],
                                  start=False, stop=(k == KC - 1), skip_group_check=True)
                    last.then_inc(s["down_used"], 1)

            pe.wait_ge(s["tok_ready"], 1)
            with pe.Fori(0, NE) as b:
                expert(b)
            nx = pe.value_load(info_i[0:1, 0:1], min_val=0, max_val=XB)
            with pe.Fori(0, XB) as x:
                with pe.If(x < nx):
                    expert(x + NE)

        @block.scalar
        def _(act):
            fn = nc.scalar.activation
            n = [0]

            def then(ins):
                n[0] += 1
                ins.then_inc(s["act_chain"], 1)
                act.wait_ge(s["act_chain"], n[0])

            act.wait_ge(s["const_ready"], 1)
            act.wait_ge(s["x_in"], 80)
            for c in range(3):
                last = fn(xn[0:ROWS[c], c, :], xrow[0:ROWS[c], c, :], ACT.Square, accum_out=ss[0:ROWS[c], c:c + 1])
            last.then_inc(s["ss_ready"], 1)
            act.wait_ge(s["ss_ready"], 1)
            for c in range(3):
                then(fn(rstd[0:ROWS[c], c:c + 1], ss[0:ROWS[c], c:c + 1], ACT.Ln, bias=c_eps[0:ROWS[c]], scale=1.0 / D))
            for c in range(3):
                last = fn(rstd[0:ROWS[c], c:c + 1], rstd[0:ROWS[c], c:c + 1], ACT.Exp, scale=-0.5)
                last.then_inc(s["rstd_ready"], 1)
            act.wait_ge(s["ab_ready"], 1)
            then(fn(gw2, gw1, ACT.Exp, scale=-1.0))
            then(fn(gw2, gw2, ACT.Ln, bias=c_one))
            then(fn(alog, alog, ACT.Exp))
            fn(beta, abt[:, :, 8:16], ACT.Sigmoid).then_inc(s["win_bank_free"], 1)
            fn(misc[:, off[0]:off[0] + 1], c_one, ACT.Copy).then_inc(s["win_bank_free"], 1)

            with act.Fori(0, 2) as it:
                for j in range(WRING):
                    act.wait_ge(s["win_used"], it * WRING + (j + 1))
                    bv, bg = bank[2 * (j % 2)], bank[2 * (j % 2) + 1]
                    k = it * WRING + j
                    fn(uh[:, bass.ds(k, 1), CH:CH + PT], bv[:, 0:PT].unsqueeze(1), ACT.Copy)
                    fn(uh[:, bass.ds(k, 1), CH + PT:UW].rearrange("p a (n t) -> p (a n) t", n=NB)[:, :, CH:CH + NS],
                       tok2(bv), ACT.Copy)
                    fn(acc[:, bass.ds(k, 1), :], bg[:, 0:T].unsqueeze(1), ACT.Sigmoid).then_inc(s["win_bank_free"], 1)

            def silu_step(v):
                act.wait_ge(s["conv_ready"], v * 2 + 2)
                fn(qkv[:, bass.ds(v * 2, 2), :], qkv[:, bass.ds(v * 2, 2), :], ACT.Silu).then_inc(s["silu_done"], 1)

            with act.Fori(0, 3) as it:
                for j in range(WRING):
                    act.wait_ge(s["win_used"], it * WRING + (8 + j + 1))
                    act.wait_ge(s["conv_ready"], it * 8)
                    for f in range(2):
                        src = bank[2 * (j % 2) + f]
                        k = it * 8 + (2 * j + f)
                        fn(pre[:, 2 * j + f, SH:SH + PT], src[:, 0:PT], ACT.Copy)
                        fn(pre[:, 2 * j + f, SH + PT:QW].rearrange("p (n t) -> p n t", n=NB)[:, :, SH:SH + NS],
                           tok2(src), ACT.Copy).then_inc(s["qkv_copied"], 1)
                        fn(qtail[:, bass.ds(k, 1), 0:SH], src[:, PT - SH:PT].unsqueeze(1), ACT.Copy)
                        last = fn(qtail[:, bass.ds(k, 1), SH:27].rearrange("p a (n t) -> p (a n) t", n=NB),
                                  tok2(src)[:, :, NS - SH:NS], ACT.Copy)
                    last.then_inc(s["win_bank_free"], 1)
                for j in range(WRING):
                    silu_step(it * WRING + j)
            for k in range(KC):
                act.wait_ge(s["u_ready"], KC)
                fn(utail[:, k, 0:CH], uh[:, k, CH + PT - CH:CH + PT], ACT.Copy)
                fn(utail[:, k, CH:62].rearrange("p (n t) -> p n t", n=NB), sample_u(k)[:, :, CH:CH + NS], ACT.Copy)
            act.wait_ge(s["y_zeroed"], 16)
            for j in range(WRING):
                act.wait_ge(s["win_used"], 20 + j + 1)
                for f in range(2):
                    last = fn(zs[:, 2 * j + f, :], bank[2 * (j % 2) + f][:, 0:T], ACT.Silu)
                last.then_inc(s["win_bank_free"], 1)
            with act.Fori(0, 2) as it:
                for j in range(WRING):
                    act.wait_ge(s["win_used"], it * WRING + (24 + j + 1))
                    for f in range(2):
                        last = fn(gate[:, bass.ds(it * 8 + (2 * j + f), 1), :], bank[2 * (j % 2) + f][:, 0:T].unsqueeze(1),
                                  ACT.Sigmoid)
                    last.then_inc(s["win_bank_free"], 1)
            act.wait_ge(s["centered"], 1)
            act.wait_ge(s["tail_out"], 16 * (NB + 3))
            fn(sq[:, :, :], acc[:, :, :], ACT.Square).then_inc(s["squared"], 1)
            act.wait_ge(s["sumsq_done"], 1)
            then(fn(rs[0], bank[5][:, 0:T], ACT.Ln, bias=c_eps, scale=1.0 / D))
            fn(rs[0], rs[0], ACT.Exp, scale=-0.5).then_inc(s["rstd_c"], 1)
            act.wait_ge(s["scaled"], 1)
            for k in range(KC):
                fn(acc[:, k, :], acc[:, k, :], ACT.Silu, bias=pcol[:, k, R_LNB:R_LNB + 1],
                   scale=pcol[:, k, R_LNG:R_LNG + 1]).then_inc(s["conf_act"], 1)
            for j in range(17):
                if j < 16:
                    if j >= 2:
                        act.wait_ge(s["l2_sum"], j - 1)
                    fn(sqh[j % 2], qkv[:, j, :], ACT.Square).then_inc(s["l2_sq"], 1)
                if j >= 1:
                    i = j - 1
                    act.wait_ge(s["l2_sum"], i + 1)
                    if i >= 2:
                        act.wait_ge(s["l2_scaled"], i - 1)
                    then(fn(rs[i % 2], bank[i % 2][:, 0:T], ACT.Ln, bias=c_eps))
                    if i < H:
                        last = fn(rs[i % 2], rs[i % 2], ACT.Exp, bias=c_lnq, scale=-0.5)
                    else:
                        last = fn(rs[i % 2], rs[i % 2], ACT.Exp, scale=-0.5)
                    last.then_inc(s["l2_inv"], 1)
            for c in range(3):
                R = ROWS[c]
                dt, eg = heads(u_dt, R), heads(u_eg, R)
                vn = u_kb.rearrange("p (h n) -> p h n", h=H)
                act.wait_ge(s["ekd_arg"], c + 1)
                fn(ekd[0:R], ekd[0:R], ACT.Exp).then_inc(s["ekd_ready"], 1)
                act.wait_ge(s["rows_done"], 2 * c + 2)
                if c:
                    act.wait_ge(s["s_evac"], 2 * c)
                    act.wait_ge(s["o_evac"], 2 * c)
                for g in range(2):
                    fn(eg[:, 4 * g:4 * g + 4, :], bank[1 + g][:, 0:4 * R].rearrange("p (h n) -> p h n", h=4), ACT.Exp
                       ).then_inc(s["eg_ready"], 1)
                act.wait_ge(s["dt_arg"], c + 1)
                fn(dt[0:R], dt[0:R], ACT.Exp).then_inc(s["dt_ready"], 1)
                act.wait_ge(s["uq_evac"], 4 * c + 4)
                for lev in levels(act, c):
                    for g in range(2):
                        act.wait_ge(s["zt_done"], lev * 2 + (14 * c + g + 1))
                        fn(dt[0:R, 4 * g:4 * g + 4, :], bank[g][0:R, 0:4 * R].rearrange("p (h n) -> p h n", h=4), ACT.Copy
                           ).then_inc(s["zt_copied"], 1)
                if c == 2:
                    for g in range(2):
                        act.wait_ge(s["seg_done"], g + 1)
                        fn(kqs[:, 4 * g:4 * g + 4, :, :],
                           bank[6 + g][:, 0:384].rearrange("p (h a n) -> p h a n", h=4, a=2), ACT.Copy
                           ).then_inc(s["seg_copied"], 1)
                for g in range(2):
                    act.wait_ge(s["vn_done"], 2 * c + g + 1)
                    fn(vn[0:R, 4 * g:4 * g + 4, :], bank[g][0:R, :].rearrange("p (h n) -> p h n", h=4), ACT.Copy
                       ).then_inc(s["vn_ready"], 1)
                if c < 2:
                    for g in range(2):
                        act.wait_ge(s["o_done"], 2 * c + g + 1)
                        fn(qkv[:, 4 * g:4 * g + 4, tile_tokens(c)],
                           bank[2 + g][:, 0:4 * R].rearrange("p (h n) -> p h n", h=4), ACT.Copy).then_inc(s["o_evac"], 1)
            act.wait_ge(s["o_evac"], 6)
            act.wait_ge(s["s_out"], 16 * (H + 1))
            for j in range(H + 1):
                if j < H:
                    if j >= 2:
                        act.wait_ge(s["on_sum"], j - 1)
                    fn(sqh[j % 2], qkv[:, j, :], ACT.Square).then_inc(s["on_sq"], 1)
                if j >= 1:
                    i = j - 1
                    act.wait_ge(s["on_sum"], i + 1)
                    if i >= 2:
                        act.wait_ge(s["o_ready"], i - 1)
                    then(fn(rs[i % 2], bank[i % 2][:, 0:T], ACT.Ln, bias=c_eps, scale=1.0 / P))
                    fn(rs[i % 2], rs[i % 2], ACT.Exp, scale=-0.5).then_inc(s["on_inv"], 1)
            for c in range(3):
                act.wait_ge(s["h_ready"], 2 * c + 2)
                if c == 0:
                    act.wait_ge(s["o_mm_done"], 6)
                then(fn(xn2[0:ROWS[c], c, :], xrow[0:ROWS[c], c, :], ACT.Square, accum_out=ss[0:ROWS[c], c:c + 1]))
                then(fn(rstd[0:ROWS[c], c:c + 1], ss[0:ROWS[c], c:c + 1], ACT.Ln, bias=c_eps[0:ROWS[c]], scale=1.0 / D))
                fn(rstd[0:ROWS[c], c:c + 1], rstd[0:ROWS[c], c:c + 1], ACT.Exp, scale=-0.5).then_inc(s["hrstd_ready"], 1)
            act.wait_ge(s["gsub_ready"], 1)
            fn(gts, gts, ACT.Exp).then_inc(s["gexp_ready"], 1)

            def expert(b):
                act.wait_ge(s["xgt_done"], b + 1)
                fn(xgT, bank[0][:].rearrange("p (c a n) -> p c a n", c=4, a=2), ACT.Copy).then_inc(s["xgt_ready"], 1)
                act.wait_ge(s["hg_ready"], b + 1)
                fn(sg, hg, ACT.Sigmoid, scale=1.702).then_inc(s["sg_ready"], 1)
                act.wait_ge(s["actt_done"], b + 1)
                fn(actT, bank[3][:].rearrange("p (c a n) -> p c a n", c=4, a=2), ACT.Copy).then_inc(s["actt_ready"], 1)
                act.wait_ge(s["y_ready"], b + 1)
                for f in range(2):
                    act.dma_start(y_d[bass.ds(b * SLOTS, SLOTS), HALF * f:HALF * (f + 1)], ysb[64 * f:64 * f + 64, :]
                                  ).then_inc(s["y_stored"], 16)

            with act.Fori(0, NE) as b:
                expert(b)
            act.wait_ge(s["y_stored"], 32 * NE)
            nx = act.value_load(info_i[0:1, 0:1], min_val=0, max_val=XB)
            with act.Fori(0, XB) as x:
                with act.If(x < nx):
                    expert(x + NE)
            act.wait_ge(s["y_stored"], nx * 32 + 32 * NE)
            fn(misc[:, off[0]:off[0] + 1], c_one, ACT.Copy).then_inc(s["experts_done"], 1)
            for c in range(3):
                act.wait_ge(s["fsq_ready"], c + 1)
                then(fn(xn2[0:ROWS[c], c, :], xrow[0:ROWS[c], c, :], ACT.Square, accum_out=ss[0:ROWS[c], c:c + 1]))
                then(fn(rstd[0:ROWS[c], c:c + 1], ss[0:ROWS[c], c:c + 1], ACT.Ln, bias=c_eps[0:ROWS[c]], scale=1.0 / D))
                fn(rstd[0:ROWS[c], c:c + 1], rstd[0:ROWS[c], c:c + 1], ACT.Exp, scale=-0.5).then_inc(s["frstd_ready"], 1)

        @block.vector
        def _(dve):
            v = nc.vector
            n = [0]

            def then(ins):
                n[0] += 1
                ins.then_inc(s["dve_chain"], 1)
                dve.wait_ge(s["dve_chain"], n[0])

            stt = v.scalar_tensor_tensor
            for k in range(KC):
                v.memset(uh[:, k, 0:CH], 0.0)
            for k in range(8):
                v.memset(pre[:, k, 0:SH], 0.0)
            then(v.memset(abt, 0.0))
            for c in range(3):
                dve.wait_ge(s["rstd_ready"], c + 1)
                v.tensor_scalar(xn[0:ROWS[c], c, :], xrow[0:ROWS[c], c, :], rstd[0:ROWS[c], c:c + 1], None, ALU.mult
                                ).then_inc(s["xn_ready"], 1)
            dve.wait_ge(s["job_done"], 1)
            v.tensor_copy(pcol[:, :, :], bank[0][:, 0:KC * NROWS].rearrange("p (k n) -> p k n", k=KC)
                          ).then_inc(s["job_evac"], 1)
            dve.wait_ge(s["job_evac"], 1)
            for c in range(3):
                for g in range(2):
                    j = 1 + 2 * c + g
                    R = ROWS[c]
                    dve.wait_ge(s["job_done"], j + 1)
                    v.tensor_tensor(xnT[:, 4 * g:4 * g + 4, tile_tokens(c)],
                                    bank[j % 8][:, 0:4 * R].rearrange("p (k n) -> p k n", k=4),
                                    pcol[:, 4 * g:4 * g + 4, R_NMIX:R_NMIX + 1].to_broadcast((P, 4, R)), ALU.mult
                                    ).then_inc(s["job_evac"], 1)
            for t in range(2):
                for g in range(2):
                    j = 7 + 2 * t + g
                    dve.wait_ge(s["job_done"], j + 1)
                    for k in range(4 * g, 4 * g + 4):
                        last = v.tensor_copy(sample_u(k)[:, 4 * t:4 * t + 4, 0:CH],
                                             bank[j % 8][:, 120 * (k % 4):120 * (k % 4 + 1)]
                                             .rearrange("p (n t) -> p n t", n=4))
                    last.then_inc(s["job_evac"], 1)
            for g in range(2):
                j = 11 + g
                dve.wait_ge(s["job_done"], j + 1)
                v.tensor_copy(dh[:, 12 * g:12 * g + 12, :],
                              bank[j % 8][:, 0:288].rearrange("p (k n) -> p k n", k=12)).then_inc(s["job_evac"], 1)
            dve.wait_ge(s["ab_done"], 1)
            for c in range(3):
                last = v.tensor_copy(abt[0:ROWS[c], c, :], bank[13 % 8][0:ROWS[c], 16 * c:16 * c + 16])
            last.then_inc(s["job_evac"], 1)
            dve.wait_ge(s["job_evac"], 14)
            then(v.tensor_tensor(g_t, abt[:, :, 0:8], dtb.unsqueeze(1).to_broadcast((P, 3, H)), ALU.add))
            then(v.tensor_scalar(gw1, g_t, -1.0, None, ALU.mult))
            then(v.tensor_tensor(gw1, gw1, g_t, ALU.max))
            v.tensor_scalar(g_t, g_t, 0.0, None, ALU.max).then_inc(s["ab_ready"], 1)
            dve.wait_ge(s["win_bank_free"], 1)
            dve.wait_ge(s["ab_ready"], 1)
            then(v.tensor_tensor(g_t, g_t, gw2, ALU.add))
            then(stt(g_t, g_t, -1.0, alog.unsqueeze(1).to_broadcast((P, 3, H)), ALU.mult, ALU.mult))
            v.tensor_scalar(nbeta, beta, -1.0, None, ALU.mult).then_inc(s["beta_ready"], 1)

            with dve.Fori(0, 2) as it:
                for j in range(WRING):
                    k = it * WRING + j
                    dve.wait_ge(s["win_bank_free"], it * WRING + (j + 3))
                    up = uh[:, bass.ds(k, 1), CH:CH + PT]
                    v.tensor_tensor(up, up, acc[:, bass.ds(k, 1), 0:PT], ALU.mult)
                    us = uh[:, bass.ds(k, 1), CH + PT:UW].rearrange("p a (n t) -> p (a n) t", n=NB)[:, :, CH:CH + NS]
                    v.tensor_tensor(us, us, acc[:, bass.ds(k, 1), PT:T].rearrange("p a (n t) -> p (a n) t", n=NB), ALU.mult
                                    ).then_inc(s["u_ready"], 1)
            dve.wait_ge(s["u_ready"], KC)

            chain = [0]

            def conf_conv(k, base, i, per):
                src = uh[:, bass.ds(k, 1), :]
                dst = acc[:, bass.ds(k, 1), :]
                for tap in range(CW):
                    w = pcol[:, bass.ds(k, 1), R_DW + tap:R_DW + tap + 1].rearrange("p a n -> p (a n)")
                    pairs = ((dst[:, :, 0:PT].rearrange("p a n -> p (a n)"),
                              src[:, :, tap:tap + PT].rearrange("p a n -> p (a n)")),
                             (dst[:, :, PT:T].rearrange("p a (n t) -> p (a n) t", n=NB),
                              src[:, :, CH + PT:UW].rearrange("p a (n t) -> p (a n) t", n=NB)[:, :, tap:tap + NS]))
                    for out, x in pairs:
                        if tap == 0:
                            bias = pcol[:, bass.ds(k, 1), R_BDW:R_BDW + 1].rearrange("p a n -> p (a n)")
                            last = v.tensor_scalar(out, x, w, bias, ALU.mult, ALU.add)
                        else:
                            last = stt(out, x, w, out, ALU.mult, ALU.add)
                    if tap < CW - 1:
                        last.then_inc(conf_chain, 1)
                        dve.wait_ge(conf_chain, i * per + (base + tap + 1))
                last.then_inc(s["conf_done"], 1)

            conf_chain = s["conv_chain"]
            with dve.Fori(0, 3) as it:
                for j in range(8):
                    k = it * 8 + j
                    dve.wait_ge(s["qkv_copied"], it * 8 + (j + 1))
                    v.tensor_copy(pre[:, j, SH + PT:QW].rearrange("p (n t) -> p n t", n=NB)[:, :, 0:SH],
                                  dh[:, bass.ds(k, 1), :].rearrange("p a (n t) -> p (a n) t", n=NB)
                                  ).then_inc(s["conv_chain"], 1)
                    dve.wait_ge(s["conv_chain"], it * (8 * SW + CH) + (j * SW + 1))
                    dst = qkv[:, bass.ds(k, 1), :]
                    for tap in range(SW):
                        w = pcol[:, j, bass.ds(it + (R_DN + 3 * tap), 1)]
                        pairs = ((dst[:, :, 0:PT].rearrange("p a n -> p (a n)"), pre[:, j, tap:tap + PT]),
                                 (dst[:, :, PT:T].rearrange("p a (n t) -> p (a n) t", n=NB),
                                  pre[:, j, SH + PT:QW].rearrange("p (n t) -> p n t", n=NB)[:, :, tap:tap + NS]))
                        for out, x in pairs:
                            if tap == 0:
                                last = v.tensor_scalar(out, x, w, None, ALU.mult)
                            else:
                                last = stt(out, x, w, out, ALU.mult, ALU.add)
                        if tap < SW - 1:
                            last.then_inc(s["conv_chain"], 1)
                            dve.wait_ge(s["conv_chain"], it * (8 * SW + CH) + (j * SW + tap + 2))
                    last.then_inc(s["conv_ready"], 1)
                conf_conv(it, 8 * SW, it, 8 * SW + CH)
            base = 3 * (8 * SW + CH)
            with dve.Fori(3, KC) as k:
                conf_conv(k, base - 3 * CH, k, CH)

            for g in range(8):
                dve.wait_ge(s["tail_t_done"], g + 1)
                if g < 2:
                    dst, src = uout[:, 512 * g:512 * (g + 1)], bank[4 + g][0:62, :]
                else:
                    dst, src = qout[:, 512 * (g - 2):512 * (g - 1)], bank[4 + g % 4][0:27, :]
                v.tensor_copy(dst, src).then_inc(s["tail_evac"], 1)

            dve.wait_ge(s["sum_done"], 1)
            then(v.tensor_scalar(mu, bank[4][:, 0:T], 1.0 / D, None, ALU.mult))
            v.tensor_tensor(acc[:, :, :], acc[:, :, :], mu.unsqueeze(1).to_broadcast((P, KC, T)), ALU.subtract
                            ).then_inc(s["centered"], 1)
            dve.wait_ge(s["rstd_c"], 1)
            v.tensor_tensor(acc[:, :, :], acc[:, :, :], rs[0].unsqueeze(1).to_broadcast((P, KC, T)), ALU.mult
                            ).then_inc(s["scaled"], 1)
            dve.wait_ge(s["win_bank_free"], 34)
            for m in range(KC):
                dve.wait_ge(s["conf_mm_done"], m + 1)
                stt(gate[:, m, :], bank[6 + m % 2][:, 0:T], pcol[:, m, R_BCO:R_BCO + 1], gate[:, m, :],
                    ALU.add, ALU.mult).then_inc(s["conf_mm_evac"], 1)
            for j in range(16):
                dve.wait_ge(s["l2_inv"], j + 1)
                v.tensor_tensor(qkv[:, j, :], qkv[:, j, :], rs[j % 2], ALU.mult).then_inc(s["l2_scaled"], 1)
            dve.wait_ge(s["l2_scaled"], 16)

            for c in range(3):
                R = ROWS[c]
                tt = tile_tokens(c)
                ng = (neg if c < 2 else neg2)[0:R, 0:R]
                kb, dt, eg, uu, qk, x, xt = (heads(w, R) for w in (u_kb, u_dt, u_eg, u_u, u_qk, u_x, u_xt))
                kqe = u_kqe[:, 0:2 * H * R].rearrange("p (h a n) -> p h a n", h=H, a=2)
                kd, vb, vn = (w.rearrange("p (h n) -> p h n", h=H) for w in (u_kd, u_vb, u_kb))

                def four(w, m, r):
                    return w[0:m, 0:4 * r].rearrange("p (h n) -> p h n", h=4)

                dve.wait_ge(s["small_mm"], c + 1)
                if c:
                    dve.wait_ge(s["tok_evac"], 4 * c)
                then(v.tensor_copy(gcs[0:R], bank[0][0:R, 0:16]))
                v.tensor_tensor(ekd[0:R], gcs[0:R, 8:16], gcs[0:R, 0:8], ALU.subtract).then_inc(s["ekd_arg"], 1)
                for g in range(2):
                    dve.wait_ge(s["eg_ready"], 2 * c + g + 1)
                    for h in range(4 * g, 4 * g + 4):
                        last = stt(dt[0:R, h, :], bank[1 + g][0:R, R * (h % 4):R * (h % 4 + 1)], gcs[0:R, h:h + 1], ng,
                                   ALU.subtract, ALU.add)
                last.then_inc(s["dt_arg"], 1)
                for g in range(2):
                    dve.wait_ge(s["brow_done"], 2 * c + 2)
                    v.tensor_tensor(kb[:, 4 * g:4 * g + 4, :], qkv[:, H + 4 * g:H + 4 * g + 4, tt],
                                    four(bank[3 + g], P, R), ALU.mult).then_inc(s["kb_ready"], 1)
                v.tensor_tensor(kqe[:, :, 0, :], qkv[:, H:2 * H, tt], eg, ALU.mult)
                v.tensor_tensor(kqe[:, :, 1, :], qkv[:, 0:H, tt], eg, ALU.mult)
                dve.wait_ge(s["dt_ready"], c + 1)
                for g in range(2):
                    dve.wait_ge(s["uq_done"], 4 * c + 2 * g + 1)
                    v.tensor_tensor(uu[0:R, 4 * g:4 * g + 4, :], four(bank[5 + g], R, R), dt[0:R, 4 * g:4 * g + 4, :],
                                    ALU.mult).then_inc(s["uq_evac"], 1)
                for g in range(2):
                    dve.wait_ge(s["uq_done"], 4 * c + 2 * g + 2)
                    v.tensor_tensor(qk[0:R, 4 * g:4 * g + 4, :], four(bank[7 - 7 * g], R, R), dt[0:R, 4 * g:4 * g + 4, :],
                                    ALU.mult).then_inc(s["uq_evac"], 1)
                dve.wait_ge(s["ekd_ready"], c + 1)
                for g in range(4):
                    dve.wait_ge(s["tok_done"], 4 * c + g + 1)
                    hs = slice(4 * (g % 2), 4 * (g % 2) + 4)
                    dst, w = (kd, ekd[0:R]) if g < 2 else (vb, beta[0:R, c, :])
                    v.tensor_tensor(dst[0:R, hs, :], four(bank[1 + g], R, P), w[:, hs].unsqueeze(2).to_broadcast((R, 4, P)),
                                    ALU.mult).then_inc(s["tok_evac"], 1)
                v.tensor_copy(x[0:R], ident[0:R, 0:R].unsqueeze(1).to_broadcast((R, H, R)))
                v.tensor_copy(xt[0:R], ident[0:R, 0:R].unsqueeze(1).to_broadcast((R, H, R))).then_inc(s["x_updated"], 1)
                dve.wait_ge(s["x_updated"], 15 * c + 1)
                for lev in levels(dve, c):
                    for g in range(2):
                        hs = slice(4 * g, 4 * g + 4)
                        dve.wait_ge(s["x_updated"], lev * 2 + (15 * c + g))
                        dve.wait_ge(s["vt_done"], lev * 2 + (14 * c + g + 1))
                        v.tensor_tensor(x[0:R, hs, :], x[0:R, hs, :], four(bank[2 + g], R, R), ALU.subtract)
                        v.tensor_tensor(xt[0:R, hs, :], xt[0:R, hs, :], four(bank[4 + g], R, R), ALU.subtract
                                        ).then_inc(s["x_updated"], 1)
                if c:
                    for g in range(2):
                        dve.wait_ge(s["kes_done"], 2 * (c - 1) + g + 1)
                        src = bank[6 + g] if c == 1 else bank[4 + g]
                        for h in range(4 * g, 4 * g + 4):
                            last = stt(vb[0:R, h, :], src[0:R, P * (h % 4):P * (h % 4 + 1)], nbeta[0:R, c, h:h + 1],
                                       vb[0:R, h, :], ALU.mult, ALU.add)
                        last.then_inc(s["r_ready"], 1)
                if c == 0:
                    for g in range(2):
                        dve.wait_ge(s["s_done"], g + 1)
                        v.tensor_copy(S[:, 4 * g:4 * g + 4, :], four(bank[4 + g], P, P)).then_inc(s["s_evac"], 1)
                    dve.wait_ge(s["s_evac"], 2)
                elif c == 1:
                    for g in range(2):
                        dve.wait_ge(s["s_done"], 2 + g + 1)
                        for h in range(4 * g, 4 * g + 4):
                            last = stt(S[:, h, :], S[:, h, :], eg[:, h, R - 1:R], bank[4 + g][:, P * (h % 4):P * (h % 4 + 1)],
                                       ALU.mult, ALU.add)
                        last.then_inc(s["s_evac"], 1)
                    dve.wait_ge(s["s_evac"], 4)
                else:
                    for g in range(2):
                        dve.wait_ge(s["o_done"], 4 + g + 1)
                        v.tensor_tensor(qkv[:, 4 * g:4 * g + 4, tt], kqs[:, 4 * g:4 * g + 4, 1, :], four(bank[2 + g], P, R),
                                        ALU.add).then_inc(s["o_evac"], 1)
                    for h in range(H):
                        dve.wait_ge(s["seg_done"], 2)
                        then(v.tensor_tensor(s0[:, h, :, :], s0[:, h, :, :],
                                             eg[:, h, TAIL + NS - 1:R:NS].unsqueeze(2).to_broadcast((P, NB, P)), ALU.mult))
                        dve.wait_ge(s["sn_done"], h + 1)
                        bs = (bank[4], bank[5], bank[6]) if h % 2 == 0 else (bank[7], bank[2], bank[3])
                        stt(S[:, h, :], S[:, h, :], eg[:, h, TAIL - 1:TAIL], bs[0][:, 0:P], ALU.mult, ALU.add)
                        v.tensor_tensor(s0[:, h, 0:3, :], s0[:, h, 0:3, :],
                                        bs[0][:, P:512].rearrange("p (n v) -> p n v", n=3), ALU.add)
                        v.tensor_tensor(s0[:, h, 3:7, :], s0[:, h, 3:7, :],
                                        bs[1][:, :].rearrange("p (n v) -> p n v", n=4), ALU.add)
                        v.tensor_tensor(s0[:, h, 7, :], s0[:, h, 7, :], bs[2][:, 0:P], ALU.add).then_inc(s["s_evac"], 1)
            dve.wait_ge(s["o_evac"], 6)
            for h in range(H):
                dve.wait_ge(s["on_inv"], h + 1)
                then(v.tensor_tensor(qkv[:, h, :], qkv[:, h, :], rs[h % 2], ALU.mult))
                stt(qkv[:, h, :], qkv[:, h, :], dnw, zs[:, h, :], ALU.mult, ALU.mult).then_inc(s["o_ready"], 1)
            for m in range(KC):
                dve.wait_ge(s["y_mm_done"], m + 1)
                then(v.tensor_tensor(gate[:, KC + m, :], bank[2 + m % 2][:, 0:T], gate[:, KC + m, :], ALU.mult))
                v.tensor_tensor(gate[:, m, :], gate[:, m, :], gate[:, KC + m, :], ALU.add).then_inc(s["y_mm_evac"], 1)
            for c in range(3):
                for f in range(2):
                    i = 2 * c + f
                    dve.wait_ge(s["o_mm_done"], i + 1)
                    w = xrow[0:ROWS[c], c, HALF * f:HALF * (f + 1)]
                    v.tensor_tensor(w, w, bank[(4, 5, 6, 7, 0, 1)[i]][0:ROWS[c], :], ALU.add).then_inc(s["h_ready"], 1)
            dve.wait_ge(s["norms_in"], 32)
            for c in range(3):
                dve.wait_ge(s["hrstd_ready"], c + 1)
                stt(xn2[0:ROWS[c], c, :], xrow[0:ROWS[c], c, :], rstd[0:ROWS[c], c:c + 1], nffn[0:ROWS[c], :],
                    ALU.mult, ALU.mult).then_inc(s["xn2_ready"], 1)
            for c in range(3):
                for g in range(2):
                    dve.wait_ge(s["xn2t_done"], 2 * c + g + 1)
                    v.tensor_copy(xn2T[:, 4 * g:4 * g + 4, tile_tokens(c)],
                                  bank[2 + g][:, 0:4 * ROWS[c]].rearrange("p (k n) -> p k n", k=4)
                                  ).then_inc(s["xn2t_evac"], 1)
            then(v.memset(halves, 0.0))
            v.memset(lg, 0.0)
            v.memset(rt[1], 0.0)
            then(v.memset(halves[0:1, 0:64], 1.0))
            then(v.tensor_scalar(halves[:, 64:128], halves[:, 0:64], -1.0, 1.0, ALU.mult, ALU.add))
            dve.wait_ge(s["lg_done"], 1)
            for c in range(3):
                R = ROWS[c]
                then(v.tensor_tensor(lg[0:R, c, :], bank[4][0:R, NE * c:NE * (c + 1)], brt[0:R], ALU.add))
                then(v.max(mx8[:, c, :], lg[:, c, :]))
                then(v.max_index(ix8[:, c, :], mx8[:, c, :], lg[:, c, :]))
            then(v.tensor_copy(ixf, ix8))
            v.tensor_tensor(gts, mx8[:, :, 0:TOPK], mx8[:, :, 0:1].to_broadcast((P, 3, TOPK)), ALU.subtract
                            ).then_inc(s["gsub_ready"], 1)
            for c in range(3):
                last = v.tensor_tensor(oh[:, c], iota_e.unsqueeze(1).to_broadcast((P, TOPK, NE)),
                                       ixf[:, c, 0:TOPK].unsqueeze(2).to_broadcast((P, TOPK, NE)), ALU.is_equal)
            then(last)
            then(v.tensor_tensor(rt[0], oh[:, :, 0, :], oh[:, :, 1, :], ALU.add))
            then(v.tensor_tensor(rt[0], rt[0], oh[:, :, 2, :], ALU.add))
            v.tensor_tensor(rt[0], rt[0], oh[:, :, 3, :], ALU.add).then_inc(s["mask_ready"], 1)
            dve.wait_ge(s["gexp_ready"], 1)
            then(v.tensor_reduce(gsum.unsqueeze(2), gts, AX.X, ALU.add))
            then(v.reciprocal(gsum, gsum))
            then(v.tensor_tensor(gts, gts, gsum.unsqueeze(2).to_broadcast((P, 3, TOPK)), ALU.mult))
            dve.wait_ge(s["pos_done"], 1)
            pos, pd, slot, t1, t2, dl, yl = rt[1], rt[2], rt[3], rt[4], rt[5], rt[6], rt[7]
            for c in range(3):
                last = v.tensor_copy(pos[0:ROWS[c], c, :], bank[5][0:ROWS[c], NE * c:NE * (c + 1)])
            then(v.tensor_copy(cnt, bank[5][:, 96:128]))
            v.tensor_scalar(pd, pos, float(SLOTS), None, ALU.is_ge)
            then(v.tensor_scalar(nbx, cnt, float(SLOTS), None, ALU.is_gt))
            for m in range(2, 5):
                stt(pd, pos, float(SLOTS * m), pd, ALU.is_ge, ALU.add)
                then(stt(nbx, cnt, float(SLOTS * m), nbx, ALU.is_gt, ALU.add))
            then(stt(slot, pd, -float(SLOTS), pos, ALU.mult, ALU.add))
            then(v.tensor_copy(cs[0], nbx))
            for i in range(5):
                w = 1 << i
                src, dst = cs[i % 2], cs[(i + 1) % 2]
                v.tensor_copy(dst[:, 0:w], src[:, 0:w])
                then(v.tensor_tensor(dst[:, w:NE], src[:, w:NE], src[:, 0:NE - w], ALU.add))
            incl = cs[1]
            then(v.tensor_tensor(xs, incl, nbx, ALU.subtract))
            then(stt(t1, pd, float(NE - 1), xs.unsqueeze(1).to_broadcast((P, 3, NE)), ALU.add, ALU.add))
            then(v.tensor_tensor(t2, iota_e.unsqueeze(1).to_broadcast((P, 3, NE)), t1, ALU.subtract))
            then(stt(t2, pd, 0.0, t2, ALU.is_equal, ALU.mult))
            then(v.tensor_tensor(t1, t1, t2, ALU.add))
            stt(dl, slot, float(NBLK), t1, ALU.mult, ALU.add)
            then(stt(yl, t1, float(SLOTS), slot, ALU.mult, ALU.add))
            for src, dst in ((dl, dli), (yl, yli)):
                then(v.tensor_tensor(ohm, oh, src.unsqueeze(2).to_broadcast((P, 3, TOPK, NE)), ALU.mult))
                then(v.tensor_reduce(self_.unsqueeze(3), ohm, AX.X, ALU.add))
                then(v.tensor_copy(dst, self_))
            v.tensor_copy(info[:, 0:1], incl[0:1, NE - 1:NE])
            shape = (1, XB, NE)
            then(v.tensor_scalar(xio, iota_e[0:1, 0:XB], 0.0, None, ALU.add))
            v.tensor_tensor(bx[0], xio.unsqueeze(2).to_broadcast(shape), xs[0:1].unsqueeze(1).to_broadcast(shape), ALU.is_ge)
            then(v.tensor_tensor(bx[1], xio.unsqueeze(2).to_broadcast(shape), incl[0:1].unsqueeze(1).to_broadcast(shape),
                                 ALU.is_ge))
            then(v.tensor_tensor(bx[0], bx[0], bx[1], ALU.subtract))
            then(v.tensor_tensor(bx[2], bx[0], iota_e[0:1].unsqueeze(1).to_broadcast(shape), ALU.mult))
            then(v.tensor_reduce(info[:, 1:1 + XB].unsqueeze(2), bx[2], AX.X, ALU.add))
            v.tensor_copy(info_i[0:1, :], info).then_inc(s["idx_ready"], 1)
            dve.wait_ge(s["tok_in"], 32)
            v.tensor_scalar(tokt, tokt, 2.0, half_col, ALU.mult, ALU.add).then_inc(s["tok_ready"], 1)

            moe_chain = s["expert_chain"]

            def expert(b):
                dve.wait_ge(s["up_used"], b * KC + KC)
                v.tensor_scalar(hg, bank[1][:], 7.0, None, ALU.min).then_inc(s["hg_ready"], 1)
                v.tensor_scalar(hl, bank[2][:], 7.0, -7.0, ALU.min, ALU.max).then_inc(moe_chain, 1)
                dve.wait_ge(moe_chain, b * 2 + 1)
                stt(hgl, hl, 1.0, hg, ALU.add, ALU.mult).then_inc(moe_chain, 1)
                dve.wait_ge(moe_chain, b * 2 + 2)
                dve.wait_ge(s["sg_ready"], b + 1)
                v.tensor_tensor(act_h, hgl, sg, ALU.mult).then_inc(s["act_ready"], 1)
                dve.wait_ge(s["down_used"], b * KC + KC)
                dve.wait_ge(s["y_stored"], b * 32)
                v.tensor_copy(ysb, bank[4][:]).then_inc(s["y_ready"], 1)

            with dve.Fori(0, NE) as b:
                expert(b)
            nx = dve.value_load(info_i[0:1, 0:1], min_val=0, max_val=XB)
            with dve.Fori(0, XB) as xx:
                with dve.If(xx < nx):
                    expert(xx + NE)
            for r in range(TOPK):
                dve.wait_ge(y_in[r], 48)
                for c in range(3):
                    R = ROWS[c]
                    last = stt(xrow[0:R, c, :], ygat[3 * r + c][0:R, :], gts[0:R, c, r:r + 1], xrow[0:R, c, :],
                               ALU.mult, ALU.add)
                    if r < TOPK - 1 and c == 2:
                        then(last)
                    if r == TOPK - 1:
                        last.then_inc(s["fsq_ready"], 1)
            dve.wait_ge(s["fsq_ready"], 3)
            for c in range(3):
                R = ROWS[c]
                dve.wait_ge(s["frstd_ready"], c + 1)
                stt(xn2[0:R, c, :], xrow[0:R, c, :], rstd[0:R, c:c + 1], nfin[0:R, :], ALU.mult, ALU.mult
                    ).then_inc(s["final_ready"], 1)


_INS = ['x_prompt', 'x_sample', 'state_conf_conv', 'state_dn_conv', 'state_dn_S', 'meta_tokens', 'norm_mix', 'w_in',
        'w_conf_dw', 'b_conf_dw', 'ln_conf_g', 'ln_conf_b', 'w_conf_out', 'b_conf_out', 'w_dn_conv', 'dn_a_log',
        'dn_dt_bias', 'dn_norm_w', 'w_dn_out', 'w_out', 'norm_ffn', 'w_router', 'b_router', 'w_up', 'b_up', 'w_down',
        'b_down', 'norm_final']
_OUTS = {'y_prompt': (1, 256, 1024), 'y_sample': (8, 4, 1024), 'cp': (1, 1, 30, 1024), 'dp': (1, 1, 3, 3072),
         'sp': (1, 1, 8, 128, 128), 'cs': (1, 8, 30, 1024), 'ds': (1, 8, 3, 3072), 'ss': (1, 8, 8, 128, 128)}


def kernel(**inputs):
    import numpy as _np
    import concourse.bacc as _bacc
    from concourse.bass_utils import run_bass_kernel_spmd as _run

    nc = _bacc.Bacc("TRN2", target_bir_lowering=False, num_devices=1)
    arrays, args = {}, {}
    for name in _INS:
        v = _np.ascontiguousarray(inputs[name])
        arrays[f"in_{name}"] = v
        args[name] = nc.dram_tensor(f"in_{name}", v.shape, mybir.dt.from_np(v.dtype), kind="ExternalInput").ap()
    for name, shape in _OUTS.items():
        args[name] = nc.dram_tensor(f"out_{name}", shape, F32, kind="ExternalOutput").ap()
    build(nc, args)
    r = _run(nc, [arrays], core_ids=[0])
    return tuple(r.results[0][f"out_{name}"] for name in _OUTS)
```

```python
import concourse.bass as bass
from concourse import mybir
from contextlib import ExitStack
import math

F32 = mybir.dt.float32
I32 = mybir.dt.int32
U32 = mybir.dt.uint32
ALU = mybir.AluOpType
ACT = mybir.ActivationFunctionType
AX = mybir.AxisListType

P = 128
D = 1024
KC = D // P
META = 16
SEQ = 256
NB, NS = 8, 4
PT = META + SEQ
T = PT + NB * NS
ROWS = [128, 128, T - 256]
TAIL = PT - 256
H = 8
CW = 31
CH = CW - 1
SW = 4
SH = SW - 1
UW = CH + PT + NB * (CH + NS)
QW = SH + PT + NB * (SH + NS)
NE = 32
TOPK = 4
SLOTS = 64
XB = 18
NBLK = NE + XB
HALF = 512
V_ROUND = 2
EPS = 1e-6
O_Z = 5120
O_A = 6144
O_GATE = 6160
BIG = 1e30
LEVELS = 7
LEVELS2 = 4

R_DW, R_NMIX, R_BDW, R_LNG, R_LNB, R_BCO, R_DN = 0, 31, 32, 33, 34, 35, 36
NROWS = R_DN + 3 * SW

WRING = 4
STEPS = 9 * WRING
A_UH = WRING * 2048
A_SQ = A_UH
A_XNT = A_UH + KC * UW
A_PRE = A_XNT + KC * T
A_XN = A_PRE + 8 * QW
A_PROW = A_XN + 3 * D
A_CH = A_PROW + D
A_QO = A_PRE + 16 * QW
A_S0 = 8192
A_PROJ = 16384
ARENA = 24576


def levels(eng, c):
    if c < 2:
        with eng.Fori(0, LEVELS) as lev:
            yield lev
    else:
        yield from range(LEVELS2)


def tile_tokens(c):
    return slice(128 * c, 128 * c + ROWS[c])


def build(nc, a):
    ctx = ExitStack()
    with ctx:
        def sb(name, shape, dt=F32):
            return ctx.enter_context(nc.sbuf_tensor(name, shape, dt))

        def sem(name):
            return ctx.enter_context(nc.semaphore(name))

        xn2_d = nc.dram_tensor("xn2_d", (T, D), F32, kind="Internal").ap()
        tok_d = nc.dram_tensor("tok_d", (SLOTS, NBLK), I32, kind="Internal").ap()
        y_d = nc.dram_tensor("y_d", (NBLK * SLOTS, D), F32, kind="Internal").ap()

        arena = sb("arena", [P, ARENA])
        xrow = sb("xrow", [P, 3, D])
        acc = sb("acc", [P, KC, T])
        qkv = sb("qkv", [P, 24, T])
        zs = sb("zs", [P, H, T])
        gate = sb("gate", [P, 2 * KC, T])
        pcol = sb("pcol", [P, KC, NROWS])
        ident = sb("ident", [P, P])
        ones = sb("ones", [P, P])
        causal = sb("causal", [P, P])
        causal2 = sb("causal2", [48, 48])
        same2 = sb("same2", [48, 48])
        neg = sb("neg", [P, P])
        neg2 = sb("neg2", [48, 48])
        segm = sb("segm", [48, 9])
        lmask = sb("lmask", [P, LEVELS, P])
        strict = sb("strict", [P, P])
        wab = sb("wab", [P, KC, 16])
        wr = sb("wr", [P, KC, NE])
        misc = sb("misc", [P, 720])
        temps = sb("temps", [P, 5 * 1024])

        off = [0]

        def small(n, dt=F32):
            v = misc[:, off[0]:off[0] + n]
            off[0] += n
            return v if dt == F32 else v.bitcast(dt)

        c_eps, c_one, c_epsq = small(1), small(1), small(1)
        half_col = small(1)
        dnw = small(1)
        ss = small(3)
        rstd = small(3)
        alog, dtb = small(8), small(8)
        abt = small(48).rearrange("p (c n) -> p c n", c=3)
        g_t = small(24).rearrange("p (c n) -> p c n", c=3)
        beta = small(24).rearrange("p (c n) -> p c n", c=3)
        nbeta = small(24).rearrange("p (c n) -> p c n", c=3)
        gw1 = small(24).rearrange("p (c n) -> p c n", c=3)
        gw2 = small(24).rearrange("p (c n) -> p c n", c=3)
        gcs = small(16)
        ekd = small(8)
        iota_e = small(32)
        tokid = small(3, I32)
        tokt = small(NBLK, I32)
        info_i = small(1 + XB, I32)
        idxcol = small(1, I32)
        brt = small(32)
        mx8 = small(24).rearrange("p (c n) -> p c n", c=3)
        ix8 = small(24, U32).rearrange("p (c n) -> p c n", c=3)
        gts = small(12).rearrange("p (c n) -> p c n", c=3)
        gsum = small(3)
        dli = small(12, I32).rearrange("p (c n) -> p c n", c=3)
        yli = small(12, I32).rearrange("p (c n) -> p c n", c=3)
        zero_i = small(NBLK, I32)
        wait_scratch = small(1)

        wring = arena[:, 0:WRING * 2048].rearrange("p (s k n) -> p s k n", s=WRING, k=KC)
        uh = arena[:, A_UH:A_XNT].rearrange("p (k n) -> p k n", k=KC)
        xnT = arena[:, A_XNT:A_PRE].rearrange("p (k n) -> p k n", k=KC)
        pre = arena[:, A_PRE:A_XN].rearrange("p (k n) -> p k n", k=8)
        xn = arena[:, A_XN:A_PROW].rearrange("p (c n) -> p c n", c=3)
        prow = arena[0:NROWS, A_PROW:A_CH]
        chrow = arena[0:120, A_CH:A_CH + 2 * D].rearrange("p (c n) -> p c n", c=2)
        dhrow = temps[0:24, 0:3072]
        dh = temps[:, 3072:3072 + 24 * 24].rearrange("p (k n) -> p k n", k=24)
        utail = temps[:, 3648:3648 + KC * 62].rearrange("p (k n) -> p k n", k=KC)
        qtail = temps[:, 4144:4144 + 24 * 27].rearrange("p (k n) -> p k n", k=24)
        uout = arena[0:62, A_SQ:A_SQ + 1024]
        qout = arena[0:27, A_QO:A_QO + 3072]

        def unit(n, w=1):
            if n < 5:
                return temps[:, n * 1024:(n + w) * 1024]
            return arena[:, (n - 5) * 1024:(n - 5 + w) * 1024]

        def heads(u, R):
            return u[:, 0:H * R].rearrange("p (h n) -> p h n", h=H)
        u_dt, u_eg, u_um, u_kb, u_s = (unit(n) for n in range(5))
        u_kqe, u_u, u_qk, u_vb, u_x, u_xt = unit(5, 2), unit(7), unit(8), unit(9), unit(10), unit(11)
        u_kd = acc[:, :, :].rearrange("p k n -> p (k n)")[:, 0:1024]
        S = u_s.rearrange("p (h n) -> p h n", h=H)
        s0 = arena[:, A_S0:A_S0 + 8192].rearrange("p (h n v) -> p h n v", h=H, n=NB)
        kqs = u_u[:, 0:768].rearrange("p (h a n) -> p h a n", h=H, a=2)
        vbd = qkv[:, 16:24, :].rearrange("p k n -> p (k n)")[0:48, 0:2304].rearrange("p (b s v) -> p b s v", b=2, s=9)
        proj = arena[:, A_PROJ:A_PROJ + 8192].rearrange("p (k n) -> p k n", k=KC)
        wout = arena[:, 0:8192].rearrange("p (k n) -> p k n", k=KC)
        sq = arena[:, A_SQ:A_SQ + KC * T].rearrange("p (k n) -> p k n", k=KC)
        mu = temps[:, 1024:1024 + T]
        rsc = temps[:, 1024 + T:1024 + 2 * T]
        sqh = [temps[:, T * i:T * (i + 1)] for i in range(3)]
        norms = [arena[:, o:o + KC * T].rearrange("p (k n) -> p k n", k=KC) for o in (A_UH, A_PRE + 8 * QW)]
        rs = [temps[:, 2048 + T * i:2048 + T * (i + 1)] for i in range(3)]

        nffn = acc[:, :, :].rearrange("p k n -> p (k n)")[:, 1024:2048]
        nfin = u_kd
        qflat = qkv[:, :, :].rearrange("p k n -> p (k n)")
        xn2 = gate[:, :, :].rearrange("p k n -> p (k n)")[:, 0:3072].rearrange("p (c n) -> p c n", c=3)
        xn2T = zs
        lg = temps[:, 0:96].rearrange("p (c n) -> p c n", c=3)
        oh = temps[:, 128:512].rearrange("p (c r n) -> p c r n", c=3, r=TOPK)
        ohm = temps[:, 512:896].rearrange("p (c r n) -> p c r n", c=3, r=TOPK)
        rt = [temps[:, 1024 + 96 * i:1120 + 96 * i].rearrange("p (c n) -> p c n", c=3) for i in range(9)]
        cnt, nbx, xs, ci = (temps[:, 2048 + 32 * i:2080 + 32 * i] for i in range(4))
        cs = [temps[:, 2304 + 32 * i:2336 + 32 * i] for i in range(2)]
        ixf = temps[:, 2400:2424].rearrange("p (c n) -> p c n", c=3)
        self_ = temps[:, 2432:2444].rearrange("p (c n) -> p c n", c=3)
        xio = temps[0:1, 2448:2448 + XB]
        info = temps[0:1, 2480:2480 + 1 + XB]
        bx = [temps[0:1, 2560 + 576 * i:3136 + 576 * i].rearrange("p (x e) -> p x e", x=XB) for i in range(3)]

        xg = qflat[:, 0:512]
        xgT = qflat[:, 512:1024].rearrange("p (c a n) -> p c a n", c=4, a=2)
        hg = qflat[:, 1024:1536]
        sg = qflat[:, 1536:2048]
        hl = qflat[:, 2048:2560]
        hgl = qflat[:, 2560:3072]
        act_h = qflat[:, 3072:3584]
        actT = qflat[:, 3584:4096].rearrange("p (c a n) -> p c a n", c=4, a=2)
        ysb = qflat[:, 4096:4608]
        brow = qflat[0:2, 4608:6144].rearrange("p (a n) -> p a n", a=3)
        halves = qflat[0:2, 6144:6272]
        wup = [arena[:, 2048 * ((k + 4) % KC):2048 * ((k + 4) % KC + 1)] for k in range(KC)]
        wdn = [arena[:, A_PROJ + 1024 * k:A_PROJ + 1024 * (k + 1)] for k in range(KC)]
        ygat = [arena[:, 1024 * i:1024 * (i + 1)] for i in range(12)]

        bank = [ctx.enter_context(nc.psum_tensor(f"bank{i}", [P, 512], F32)) for i in range(8)]

        names = """y_zero y_zeroed x_in par_in small_in hist_in chist_in const_ready pool_chain dve_chain act_chain ss_ready rstd_ready
            xn_ready job_done job_evac ab_done win_used win_bank_free u_ready conf_done qkv_copied conv_ready
            silu_done tail_t_done tail_evac tail_out sum_done sumsq_done centered squared scaled
            conf_act conf_mm_evac l2_sq l2_sum l2_root l2_scaled ab_ready beta_ready small_mm
            ekd_arg ekd_ready gl_ready bl_ready rows_done brow_done dt_arg dt_ready eg_ready kb_ready uq_done uq_evac
            tok_done tok_evac um_ready zt_done zt_copied vt_done x_updated kes_done r_ready vn_done vn_ready o_done
            o_evac s_done s_evac s0_in seg_done seg_copied vbd_ready sn_done s_out on_sq on_sum on_inv on_prod s_decayed router_in on_root ln_std o_ready
            projd_in y_mm_done y_mm_evac wout_in o_mm_done h_ready hrstd_ready xn2_ready xn2_stored xn2t_done
            xn2t_evac lg_done gsub_ready gexp_ready mask_ready pos_done idx_ready zero_in scattered tok_in tok_ready
            norms_in bias_in bias_used up_used down_used xg_in xgt_done xgt_ready hg_ready sg_ready act_ready
            actt_done actt_ready y_ready y_stored experts_done fsq_ready frstd_ready final_ready out_done
            sampleconf_out idx_copied conv_chain expert_chain""".split()
        s = {n: sem(n) for n in names}
        win_in = [sem(f"win_in{i}") for i in range(WRING)]
        up_in = [sem(f"up_in{i}") for i in range(KC)]
        down_in = [sem(f"down_in{i}") for i in range(KC)]
        y_in = [sem(f"y_in{i}") for i in range(TOPK)]

        block = ctx.enter_context(nc.Block())

        w_in_v = a["w_in"][0].rearrange("(k p) n -> p k n", p=P)
        w_up_v = a["w_up"][0].rearrange("e (k p) n -> p e k n", p=P)
        w_dn_v = a["w_down"][0].rearrange("e (k p) n -> p e k n", p=P)
        b_up_v = a["b_up"][0].rearrange("e (a f n) -> f e a n", a=2, f=2)
        b_dn_v = a["b_down"][0].rearrange("e (f n) -> f e n", f=2)

        def prompt_u(k):
            return uh[:, k, CH:CH + PT]

        def sample_u(k):
            return uh[:, k, CH + PT:UW].rearrange("p (n t) -> p n t", n=NB)

        def tok2(v):
            return v[:, PT:T].rearrange("p (n t) -> p n t", n=NB)

        @block.sync
        def _(sp):
            for dst, src in ((xrow[0:META, 0, :], a["meta_tokens"]),
                             (xrow[META:128, 0, :], a["x_prompt"][0, 0:112, :]),
                             (xrow[:, 1, :], a["x_prompt"][0, 112:240, :]),
                             (xrow[0:TAIL, 2, :], a["x_prompt"][0, 240:256, :]),
                             (xrow[TAIL:48, 2, :], a["x_sample"].rearrange("n t d -> (n t) d"))):
                sp.dma_start(dst, src).then_inc(s["x_in"], 16)
            for r, src in ((R_DW, a["w_conf_dw"][0]), (R_NMIX, a["norm_mix"]), (R_BDW, a["b_conf_dw"]),
                           (R_LNG, a["ln_conf_g"]), (R_LNB, a["ln_conf_b"]), (R_BCO, a["b_conf_out"]),
                           (R_DN, a["w_dn_conv"][0].rearrange("t (a n) -> (t a) n", a=3))):
                sp.dma_start(prow[r:r + src.shape[0], :], src).then_inc(s["par_in"], 16)

            def win_load(step, col_a, col_b):
                slot = step % WRING
                for j, col in enumerate((col_a, col_b)):
                    sp.dma_start(wring[:, slot, :, 128 * j:128 * (j + 1)],
                                 w_in_v[:, :, bass.ds(col, 128)]).then_inc(win_in[slot], 16)

            for t in range(2):
                sp.dma_start(chrow[:, t, :], a["state_conf_conv"][0, 4 * t:4 * t + 4].rearrange("n t d -> (n t) d")
                             ).then_inc(s["chist_in"], 16)
            sp.dma_start(dhrow, a["state_dn_conv"][0].rearrange("n t d -> (n t) d")).then_inc(s["hist_in"], 16)
            win_load(0, 0, D)
            sp.dma_start(wab[:, :, :], w_in_v[:, :, O_A:O_GATE]).then_inc(s["small_in"], 16)
            sp.dma_start(alog, a["dn_a_log"].to_broadcast((P, H))).then_inc(s["small_in"], 16)
            sp.dma_start(dtb, a["dn_dt_bias"].to_broadcast((P, H))).then_inc(s["small_in"], 16)
            for j in range(1, WRING):
                win_load(j, 128 * j, D + 128 * j)
            sp.dma_start(dnw, a["dn_norm_w"].rearrange("a n -> n a")).then_inc(s["router_in"], 16)
            sp.dma_start(wr[:, :, :], a["w_router"][0].rearrange("(k p) n -> p k n", p=P)).then_inc(s["router_in"], 16)
            sp.dma_start(brt, a["b_router"].to_broadcast((P, NE))).then_inc(s["router_in"], 16)
            for j in range(WRING):
                sp.wait_ge(s["win_used"], j + 1)
                win_load(j, 128 * (WRING + j), D + 128 * (WRING + j))

            def win_group(it, col0, weights=w_in_v):
                for j in range(WRING):
                    sp.wait_ge(s["win_used"], WRING * it + j - (WRING - 1))
                    for f in range(2):
                        sp.dma_start(wring[:, j, :, 128 * f:128 * (f + 1)],
                                     weights[:, :, bass.ds(col0 + (256 * j + 128 * f), 128)]).then_inc(win_in[j], 16)

            win_group(2, O_Z)
            with sp.Fori(3, 5) as it:
                win_group(it, it * 1024 + (O_GATE - 3 * 1024))
            with sp.Fori(5, 7) as it:
                win_group(it, it * 1024 + (2 * D - 5 * 1024))
            win_group(7, 0, a["w_conf_out"][0].rearrange("(k p) n -> p k n", p=P))
            win_group(8, 4 * D)
            sp.wait_ge(s["conv_ready"], 24)
            sp.wait_ge(s["tail_out"], 16 * (NB + 3))
            sp.wait_ge(s["win_used"], STEPS)
            for h in range(H):
                sp.dma_start(s0[:, h, :, :], a["state_dn_S"][0, :, h].rearrange("n k v -> k n v")
                             ).then_inc(s["s0_in"], 16)
            sp.dma_start(proj[:, :, :], a["w_dn_out"][0].rearrange("(k p) n -> p k n", p=P)).then_inc(s["projd_in"], 16)
            sp.dma_start(nffn, a["norm_ffn"].to_broadcast((P, D))).then_inc(s["norms_in"], 16)
            sp.wait_ge(s["o_done"], 6)
            sp.wait_ge(s["o_evac"], 6)
            sp.dma_start(wout[:, :, :], a["w_out"][0].rearrange("(k p) n -> p k n", p=P)).then_inc(s["wout_in"], 16)
            sp.wait_ge(s["sn_done"], H)
            sp.dma_start(nfin, a["norm_final"].rearrange("(a n) -> a n", a=1).to_broadcast((P, D))
                         ).then_inc(s["norms_in"], 16)

            def load_up(e, k):
                sp.dma_start(wup[k], w_up_v[:, e, k, :]).then_inc(up_in[k], 16)

            def load_down(e, k):
                sp.dma_start(wdn[k], w_dn_v[:, e, k, :]).then_inc(down_in[k], 16)

            def load_bias(e):
                sp.dma_start(brow[:, 0:2, :], b_up_v[:, e, :, :]).then_inc(s["bias_in"], 16)
                sp.dma_start(brow[:, 2, :], b_dn_v[:, e, :]).then_inc(s["bias_in"], 16)

            sp.wait_ge(s["y_mm_done"], KC)
            for k in range(KC):
                load_down(0, k)
            load_bias(0)
            sp.wait_ge(s["s_out"], 16 * (H + 1))
            for k in range(4):
                load_up(0, k)
            sp.wait_ge(s["o_mm_done"], 6)
            for k in range(4, KC):
                load_up(0, k)

            def load_block(b, e):
                for k in range(KC):
                    sp.wait_ge(s["up_used"], KC * b + k - (KC - 1))
                    load_up(e, k)
                sp.wait_ge(s["bias_used"], b)
                load_bias(e)
                for k in range(KC):
                    sp.wait_ge(s["down_used"], KC * b + k - (KC - 1))
                    load_down(e, k)

            with sp.Fori(1, NE) as b:
                load_block(b, b)
            sp.wait_ge(s["idx_ready"], 1)
            nx = sp.value_load(info_i[0:1, 0:1], min_val=0, max_val=XB)
            with sp.Fori(0, XB) as x:
                with sp.If(x < nx):
                    e = sp.value_load(info_i[0:1, bass.ds(x + 1, 1)], min_val=0, max_val=NE - 1)
                    load_block(x + NE, e)

            sp.wait_ge(s["final_ready"], 3)
            for dst, src in ((a["y_prompt"][0, 0:112, :], xn2[META:128, 0, :]),
                             (a["y_prompt"][0, 112:240, :], xn2[:, 1, :]),
                             (a["y_prompt"][0, 240:256, :], xn2[0:TAIL, 2, :]),
                             (a["y_sample"].rearrange("n t d -> (n t) d"), xn2[TAIL:48, 2, :])):
                sp.dma_start(dst, src).then_inc(s["out_done"], 16)
            sp.wait_ge(s["out_done"], 64)

        @block.gpsimd
        def _(pool):
            n = [0]

            def then(ins):
                n[0] += 1
                ins.then_inc(s["pool_chain"], 1)
                pool.wait_ge(s["pool_chain"], n[0])

            def keep(v, pattern, base, cm):
                then(nc.gpsimd.affine_select(out=v, in_=v, compare_op=ALU.is_ge, fill=0.0, base=base,
                                             pattern=pattern, channel_multiplier=cm))

            for v, c in ((ident, 0.0), (ones, 1.0), (causal, 1.0), (lmask, 0.0), (same2, 0.0)):
                nc.gpsimd.memset(v[:], c)
            for v, c in ((c_eps, EPS), (c_one, 1.0), (c_epsq, P * EPS), (zero_i, 0)):
                nc.gpsimd.memset(v, c)
            nc.gpsimd.iota(tokid, pattern=[[128, 3]], base=0, channel_multiplier=1)
            then(nc.gpsimd.iota(iota_e, pattern=[[1, NE]], base=0, channel_multiplier=0,
                                allow_small_or_imprecise_dtypes=True))
            nc.gpsimd.tensor_scalar(half_col, tokid[:, 0:1], 64.0, None, ALU.is_ge)
            then(nc.gpsimd.affine_select(out=ident[:], in_=ident[:], compare_op=ALU.not_equal, fill=1.0, base=0,
                                         pattern=[[-1, P]], channel_multiplier=1))
            keep(causal[:], [[1, P]], 0, -1)
            for lev in range(LEVELS):
                b = 1 << lev
                v = lmask[:, lev, :].rearrange("p (n a b) -> p n a b", a=2, b=b)[:, :, 1, :]
                then(nc.gpsimd.memset(v, 1.0))
                keep(v, [[-2 * b, P // (2 * b)], [0, b]], 0, 1)
                keep(v, [[2 * b, P // (2 * b)], [0, b]], b - 1, -1)
            nc.gpsimd.memset(same2[:, 0:TAIL], 1.0)
            then(nc.gpsimd.memset(same2[:, TAIL:48], 1.0))
            keep(same2[:, 0:TAIL], [[0, TAIL]], TAIL - 1, -1)
            v = same2[:, TAIL:48].rearrange("p (n t) -> p n t", n=NB)
            keep(v, [[-NS, NB], [0, NS]], -TAIL, 1)
            keep(v, [[NS, NB], [0, NS]], TAIL + NS - 1, -1)
            nc.gpsimd.tensor_copy(segm[:, 0:1], same2[:, 0:1])
            nc.gpsimd.tensor_copy(segm[:, 1:9], same2[:, TAIL:48:NS])
            nc.gpsimd.tensor_tensor(strict[:], causal[:], ident[:], ALU.subtract)
            then(nc.gpsimd.tensor_tensor(causal2[:], same2[:], causal[0:48, 0:48], ALU.mult))
            nc.gpsimd.tensor_scalar(neg[:], causal[:], -1.0, BIG, ALU.add, ALU.mult)
            nc.gpsimd.tensor_scalar(neg2[:], causal2[:], -1.0, BIG, ALU.add, ALU.mult).then_inc(s["const_ready"], 1)
            pool.dma_start(tok_d, zero_i[0:SLOTS, :]).then_inc(s["zero_in"], 16)
            nc.gpsimd.memset(zs[:, 0:4, :], 0.0).then_inc(s["y_zero"], 1)
            pool.wait_ge(s["y_zero"], 1)
            pool.wait_ge(s["win_used"], 2)
            pool.dma_start(y_d[NE * SLOTS:NBLK * SLOTS, :].rearrange("(p a) n -> p a n", p=P),
                           zs[:, 0:4, :].rearrange("p k n -> p (k n)")[:, 0:D].unsqueeze(1).to_broadcast((P, XB // 2, D))
                           ).then_inc(s["y_zeroed"], 16)
            pool.dma_start(a["cs"][0, :, 0:CH - NS, :], a["state_conf_conv"][0, :, NS:CH, :]
                           ).then_inc(s["sampleconf_out"], 16)
            pool.wait_ge(s["squared"], 1)
            for j in range(16):
                pool.wait_ge(s["silu_done"], j // 2 + 1)
                if j >= 3:
                    pool.wait_ge(s["l2_sum"], j - 2)
                nc.gpsimd.tensor_tensor(sqh[j % 3], qkv[:, j, :], qkv[:, j, :], ALU.mult).then_inc(s["l2_sq"], 1)
            pool.wait_ge(s["win_bank_free"], 2 + 12)
            pool.wait_ge(s["router_in"], 48)
            then(nc.gpsimd.tensor_scalar(dnw, dnw, math.sqrt(P), None, ALU.mult))
            then(nc.gpsimd.tensor_scalar(zs[:, :, :], zs[:, :, :], dnw, None, ALU.mult))
            pool.wait_ge(s["tail_evac"], 8)
            pool.dma_start(a["cp"][0, 0], uout[0:CH, :]).then_inc(s["tail_out"], 16)
            for b in range(NB):
                pool.dma_start(a["cs"][0, b, CH - NS:CH, :], uout[CH + NS * b:CH + NS * (b + 1), :]
                               ).then_inc(s["tail_out"], 16)
            pool.dma_start(a["dp"][0, 0], qout[0:SH, :]).then_inc(s["tail_out"], 16)
            pool.dma_start(a["ds"][0].rearrange("n t d -> (n t) d"), qout[SH:SH + NB * SH, :]
                           ).then_inc(s["tail_out"], 16)
            pool.wait_ge(s["tail_out"], 16 * (NB + 3))
            pool.wait_ge(s["sampleconf_out"], 16)

            def products():
                for h in range(H):
                    pool.wait_ge(s["on_sq"], h + 1)
                    nc.gpsimd.tensor_tensor(qkv[:, h, :], qkv[:, h, :], zs[:, h, :], ALU.mult).then_inc(s["on_prod"], 1)

            for c in range(3):
                R = ROWS[c]
                cm = (causal if c < 2 else causal2)[0:R, 0:R]
                um, kb, uu = heads(u_um, R), heads(u_kb, R), heads(u_u, R)
                if c == 0:
                    pool.wait_ge(s["beta_ready"], 1)
                    pool.wait_ge(s["l2_scaled"], 16)
                    pool.wait_ge(s["tail_t_done"], 8)
                if c:
                    pool.wait_ge(s["s_evac"], 2 * c)
                nc.gpsimd.tensor_tensor(um[0:R], g_t[0:R, c, :].unsqueeze(2).to_broadcast((R, H, R)),
                                        cm.unsqueeze(1).to_broadcast((R, H, R)), ALU.mult).then_inc(s["gl_ready"], 1)
                nc.gpsimd.tensor_tensor(kb[0:R], beta[0:R, c, :].unsqueeze(2).to_broadcast((R, H, R)),
                                        ident[0:R, 0:R].unsqueeze(1).to_broadcast((R, H, R)), ALU.mult
                                        ).then_inc(s["bl_ready"], 1)
                pool.wait_ge(s["uq_evac"], 4 * c + 2)
                for lev in levels(pool, c):
                    pool.wait_ge(s["zt_done"], lev * 2 + 14 * c)
                    nc.gpsimd.tensor_tensor(um[0:R], uu[0:R],
                                            lmask[0:R, bass.ds(lev, 1), 0:R].to_broadcast((R, H, R)), ALU.mult
                                            ).then_inc(s["um_ready"], 1)
                if c == 2:
                    for h in range(H):
                        if h == 2:
                            products()
                        pool.wait_ge(s["vn_ready"], 4 + h // 4 + 1)
                        if h >= 2:
                            pool.wait_ge(s["sn_done"], h - 1)
                        nc.gpsimd.tensor_tensor(vbd[:, h % 2, :, :],
                                                u_kb[0:48, :].rearrange("p (h n) -> p h n", h=H)[:, h, :].unsqueeze(1)
                                                .to_broadcast((48, 9, P)),
                                                segm[:].unsqueeze(2).to_broadcast((48, 9, P)), ALU.mult
                                                ).then_inc(s["vbd_ready"], 1)
                    for h in range(H):
                        pool.wait_ge(s["s_evac"], 4 + h + 1)
                        pool.dma_start(a["ss"][0, :, h].rearrange("n k v -> k n v"), s0[:, h, :, :]
                                       ).then_inc(s["s_out"], 16)
                    pool.dma_start(a["sp"][0, 0].rearrange("h k v -> k h v"), S).then_inc(s["s_out"], 16)
            pool.wait_ge(s["s_out"], 16 * (H + 1))

            pool.wait_ge(s["xn2_ready"], 3)
            for c in range(3):
                pool.dma_start(xn2_d[128 * c:128 * c + ROWS[c], :], xn2[0:ROWS[c], c, :]).then_inc(s["xn2_stored"], 16)
            pool.wait_ge(s["zero_in"], 16)
            pool.wait_ge(s["idx_ready"], 1)
            for c in range(3):
                for r in range(TOPK):
                    pool.indirect_dma_start(
                        out=tok_d.rearrange("a (b c) -> (a b) c", c=1),
                        out_offset=bass.IndirectOffsetOnAxis(ap=dli[0:ROWS[c], c, r:r + 1].bitcast(U32), axis=0),
                        in_=tokid[0:ROWS[c], c:c + 1], in_offset=None).then_inc(s["scattered"], 16)
            pool.wait_ge(s["scattered"], 16 * 3 * TOPK)
            for f in range(2):
                pool.dma_start(tokt[64 * f:64 * f + 64, :], tok_d).then_inc(s["tok_in"], 16)
            pool.wait_ge(s["tok_ready"], 1)
            pool.wait_ge(s["xn2_stored"], 48)
            xn2_halves = xn2_d.rearrange("t (f n) -> (t f) n", f=2)

            def gather(b):
                pool.wait_ge(s["xgt_done"], b)
                nc.gpsimd.tensor_copy(idxcol, tokt[:, bass.ds(b, 1)]).then_inc(s["idx_copied"], 1)
                pool.wait_ge(s["idx_copied"], b + 1)
                nc.gpsimd.tensor_tensor(wait_scratch, c_one, c_one, ALU.mult)
                pool.indirect_dma_start(out=xg, out_offset=None, in_=xn2_halves,
                                        in_offset=bass.IndirectOffsetOnAxis(ap=idxcol.bitcast(U32), axis=0)
                                        ).then_inc(s["xg_in"], 16)
                pool.wait_ge(s["xg_in"], b * 16 + 16)

            with pool.Fori(0, NE) as b:
                gather(b)
            nx = pool.value_load(info_i[0:1, 0:1], min_val=0, max_val=XB)
            with pool.Fori(0, XB) as x:
                with pool.If(x < nx):
                    gather(x + NE)
            pool.wait_ge(s["experts_done"], 1)
            for r in range(TOPK):
                for c in range(3):
                    pool.indirect_dma_start(out=ygat[3 * r + c][0:ROWS[c], :], out_offset=None, in_=y_d,
                                            in_offset=bass.IndirectOffsetOnAxis(
                                                ap=yli[0:ROWS[c], c, r:r + 1].bitcast(U32), axis=0)
                                            ).then_inc(y_in[r], 16)

        @block.tensor
        def _(pe):
            mm = nc.tensor.matmul
            pe.wait_ge(s["const_ready"], 1)
            job = [0]

            def job_bank():
                if job[0] >= 8:
                    pe.wait_ge(s["job_evac"], job[0] - 7)
                return bank[job[0] % 8]

            def transposes(parts):
                b = job_bank()
                for src, col in parts:
                    k, m = src.shape
                    last = nc.tensor.transpose(b[0:m, col:col + k], src, ident[0:k, 0:k])
                last.then_inc(s["job_done"], 1)
                job[0] += 1

            pe.wait_ge(s["par_in"], 112)
            transposes([(prow[:, P * k:P * (k + 1)], NROWS * k) for k in range(KC)])
            pe.wait_ge(s["xn_ready"], 3)
            for c in range(3):
                for g in range(2):
                    transposes([(xn[0:ROWS[c], c, P * k:P * (k + 1)], ROWS[c] * (k % 4)) for k in range(4 * g, 4 * g + 4)])
            pe.wait_ge(s["chist_in"], 32)
            for t in range(2):
                for g in range(2):
                    transposes([(chrow[:, t, P * k:P * (k + 1)], 120 * (k % 4)) for k in range(4 * g, 4 * g + 4)])
            pe.wait_ge(s["hist_in"], 16)
            for g in range(2):
                transposes([(dhrow[:, P * k:P * (k + 1)], 24 * (k % 12)) for k in range(12 * g, 12 * g + 12)])
            pe.wait_ge(s["job_evac"], 7)
            pe.wait_ge(s["small_in"], 48)
            b = job_bank()
            for c in range(3):
                for k in range(KC):
                    last = mm(b[0:ROWS[c], 16 * c:16 * c + 16], xnT[:, k, tile_tokens(c)], wab[:, k, :],
                              start=(k == 0), stop=(k == KC - 1))
            last.then_inc(s["ab_done"], 1)
            pe.wait_ge(s["job_evac"], 13)

            def win_step(it, j, rhs):
                pe.wait_ge(win_in[j], it * 32 + 32)
                for f in range(2):
                    for k in range(KC):
                        last = mm(bank[2 * (j % 2) + f][:, 0:T], wring[:, j, k, P * f:P * (f + 1)], rhs[:, k, :],
                                  start=(k == 0), stop=(k == KC - 1))
                last.then_inc(s["win_used"], 1)

            def win_round(it):
                for j in range(WRING):
                    pe.wait_ge(s["win_bank_free"], it * WRING + (j + 1))
                    win_step(it, j, xnT)

            def l2_sums(step):
                for n in range(4 * step, 4 * step + 4):
                    pe.wait_ge(s["l2_sq"], n + 1)
                    if n >= 4:
                        pe.wait_ge(s["l2_root"], n - 3)
                    mm(bank[4 + n % 4][:, 0:T], ones[:], sqh[n % 3], start=True, stop=True).then_inc(s["l2_sum"], 1)

            with pe.Fori(0, 4) as it:
                win_round(it)
            pe.wait_ge(s["conf_done"], KC)
            for k in range(KC):
                last = mm(bank[4][:, 0:T], ones[:], acc[:, k, :], start=(k == 0), stop=(k == KC - 1))
            last.then_inc(s["sum_done"], 1)
            win_round(4)
            pe.wait_ge(s["squared"], 1)
            for k in range(KC):
                last = mm(bank[5][:, 0:T], ones[:], sq[:, k, :], start=(k == 0), stop=(k == KC - 1))
            last.then_inc(s["sumsq_done"], 1)
            with pe.Fori(5, 7) as it:
                win_round(it)
            pe.wait_ge(s["conf_act"], KC)
            for j in range(WRING):
                if j < 2:
                    pe.wait_ge(s["win_bank_free"], 7 * WRING + (j + 1))
                else:
                    pe.wait_ge(s["conf_mm_evac"], 2 * j - 2)
                win_step(7, j, acc)
                l2_sums(j)
            for j in range(WRING):
                if j < 2:
                    pe.wait_ge(s["conf_mm_evac"], 2 * j + 6)
                else:
                    pe.wait_ge(s["win_bank_free"], 7 * WRING + (j + 1))
                win_step(8, j, xnT)
            pe.wait_ge(s["l2_root"], 16)
            pe.wait_ge(s["win_bank_free"], 34)
            for g in range(2):
                for k in range(4 * g, 4 * g + 4):
                    last = nc.tensor.transpose(bank[4 + g][0:62, P * (k % 4):P * (k % 4 + 1)], utail[:, k, :], ident[:])
                last.then_inc(s["tail_t_done"], 1)
            for g in range(6):
                if g >= 2:
                    pe.wait_ge(s["tail_evac"], g - 1)
                bk = bank[4 + (g + 2) % 4]
                for k in range(4 * g, 4 * g + 4):
                    last = nc.tensor.transpose(bk[0:27, P * (k % 4):P * (k % 4 + 1)], qtail[:, k, :], ident[:])
                last.then_inc(s["tail_t_done"], 1)
            pe.wait_ge(s["tail_evac"], 8)

            for c in range(3):
                R = ROWS[c]
                tt = tile_tokens(c)
                cm = (causal if c < 2 else causal2)[0:R, 0:R]
                sm = ones[0:R, 0:R] if c < 2 else same2[:, :]
                um, kb, dt, eg, uu, qk, x, xt = (heads(v, R) for v in
                                                 (u_um, u_kb, u_dt, u_eg, u_u, u_qk, u_x, u_xt))
                kqe = u_kqe[:, 0:2 * H * R].rearrange("p (h a n) -> p h a n", h=H, a=2)
                kd, vb, vn = (v.rearrange("p (h n) -> p h n", h=H) for v in (u_kd, u_vb, u_kb))
                zt = dt
                if c == 0:
                    pe.wait_ge(s["beta_ready"], 1)
                    pe.wait_ge(s["l2_scaled"], 16)
                    pe.wait_ge(s["silu_done"], 12)
                else:
                    pe.wait_ge(s["s_evac"], 2 * c)
                    pe.wait_ge(s["o_evac"], 2 * c)
                mm(bank[0][0:R, 0:8], cm, g_t[0:R, c, :], start=True, stop=True)
                mm(bank[0][0:R, 8:16], sm, g_t[0:R, c, :], start=True, stop=True).then_inc(s["small_mm"], 1)
                pe.wait_ge(s["gl_ready"], c + 1)
                for g in range(2):
                    mm(bank[1 + g][:, 0:4 * R], ones[0:R, :], um[0:R, 4 * g:4 * g + 4, :], start=True, stop=True
                       ).then_inc(s["rows_done"], 1)
                pe.wait_ge(s["bl_ready"], c + 1)
                for g in range(2):
                    mm(bank[3 + g][:, 0:4 * R], ones[0:R, :], kb[0:R, 4 * g:4 * g + 4, :], start=True, stop=True
                       ).then_inc(s["brow_done"], 1)
                for g in range(2):
                    pe.wait_ge(s["kb_ready"], 2 * c + 2)
                    for kind, (bk, rhs) in enumerate(((bank[5 + g], kb), (bank[7 - 7 * g], None))):
                        for h in range(4 * g, 4 * g + 4):
                            mv = kb[:, h, :] if kind == 0 else qkv[:, h, tt]
                            last = mm(bk[0:R, R * (h % 4):R * (h % 4 + 1)], qkv[:, H + h, tt], mv, start=True, stop=True)
                        last.then_inc(s["uq_done"], 1)
                for g in range(4):
                    if g == 0:
                        pe.wait_ge(s["dt_arg"], c + 1)
                    for h in range(4 * (g % 2), 4 * (g % 2) + 4):
                        last = nc.tensor.transpose(bank[1 + g][0:R, P * (h % 4):P * (h % 4 + 1)],
                                                   qkv[:, H + h if g < 2 else 2 * H + h, tt], ident[:])
                    last.then_inc(s["tok_done"], 1)
                pe.wait_ge(s["uq_evac"], 4 * c + 4)
                pe.wait_ge(s["tok_evac"], 4 * c + 4)
                pe.wait_ge(s["x_updated"], 15 * c + 1)
                for lev in levels(pe, c):
                    pe.wait_ge(s["um_ready"], lev + (7 * c + 1))
                    for g in range(2):
                        pe.wait_ge(s["x_updated"], lev * 2 + (15 * c + g))
                        for h in range(4 * g, 4 * g + 4):
                            last = mm(bank[g][0:R, R * (h % 4):R * (h % 4 + 1)], um[0:R, h, :], xt[0:R, h, :],
                                      start=True, stop=True)
                        last.then_inc(s["zt_done"], 1)
                    for g in range(2):
                        pe.wait_ge(s["zt_copied"], lev * 2 + (14 * c + g + 1))
                        for h in range(4 * g, 4 * g + 4):
                            mm(bank[2 + g][0:R, R * (h % 4):R * (h % 4 + 1)], zt[0:R, h, :], x[0:R, h, :],
                               start=True, stop=True)
                        for h in range(4 * g, 4 * g + 4):
                            last = mm(bank[4 + g][0:R, R * (h % 4):R * (h % 4 + 1)], x[0:R, h, :], zt[0:R, h, :],
                                      start=True, stop=True)
                        last.then_inc(s["vt_done"], 1)
                pe.wait_ge(s["x_updated"], 15 * c + 1 + 2 * (LEVELS if c < 2 else LEVELS2))
                if c == 1:
                    for g in range(2):
                        for h in range(4 * g, 4 * g + 4):
                            last = mm(bank[6 + g][0:R, P * (h % 4):P * (h % 4 + 1)], kqe[:, h, 0, :], S[:, h, :],
                                      start=True, stop=True)
                        last.then_inc(s["kes_done"], 1)
                if c == 2:
                    for g in range(2):
                        for h in range(4 * g, 4 * g + 4):
                            pe.wait_ge(s["s0_in"], 16 * H)
                            bv = bank[6 + g][:, 96 * (h % 4):96 * (h % 4 + 1)].rearrange("p (a n) -> p a n", a=2)
                            mm(bv[:, :, 0:TAIL], S[:, h, :], kqe[:, h, :, 0:TAIL], start=True, stop=True)
                            for b in range(NB):
                                w = slice(TAIL + NS * b, TAIL + NS * (b + 1))
                                last = mm(bv[:, :, w], s0[:, h, b, :], kqe[:, h, :, w], start=True, stop=True)
                        last.then_inc(s["seg_done"], 1)
                    for g in range(2):
                        pe.wait_ge(s["seg_copied"], g + 1)
                        for h in range(4 * g, 4 * g + 4):
                            last = nc.tensor.transpose(bank[4 + g][0:R, P * (h % 4):P * (h % 4 + 1)],
                                                       kqs[:, h, 0, :], ident[:])
                        last.then_inc(s["kes_done"], 1)
                for g in range(2):
                    if c:
                        pe.wait_ge(s["r_ready"], 2 * (c - 1) + g + 1)
                    for h in range(4 * g, 4 * g + 4):
                        last = mm(bank[g][0:R, P * (h % 4):P * (h % 4 + 1)], x[0:R, h, :], vb[0:R, h, :],
                                  start=True, stop=True)
                    last.then_inc(s["vn_done"], 1)
                for g in range(2):
                    pe.wait_ge(s["vn_ready"], 2 * c + g + 1)
                    for h in range(4 * g, 4 * g + 4):
                        o = bank[2 + g][:, R * (h % 4):R * (h % 4 + 1)]
                        if c == 1:
                            mm(o, S[:, h, :], kqe[:, h, 1, :], start=True, stop=False)
                        last = mm(o, vn[0:R, h, :], qk[0:R, h, :], start=(c != 1), stop=True)
                    last.then_inc(s["o_done"], 1)
                if c < 2:
                    for g in range(2):
                        for h in range(4 * g, 4 * g + 4):
                            last = mm(bank[4 + g][:, P * (h % 4):P * (h % 4 + 1)], kd[0:R, h, :], vn[0:R, h, :],
                                      start=True, stop=True)
                        last.then_inc(s["s_done"], 1)

            def new_state(h):
                pe.wait_ge(s["vbd_ready"], h + 1)
                if h == 0:
                    pe.wait_ge(s["r_ready"], 4)
                if h == 1:
                    pe.wait_ge(s["o_evac"], 6)
                if h >= 2:
                    pe.wait_ge(s["s_evac"], 4 + h - 1)
                bs = (bank[4], bank[5], bank[6]) if h % 2 == 0 else (bank[7], bank[2], bank[3])
                for q, (lo, hi) in enumerate(((0, 4), (4, 8), (8, 9))):
                    last = mm(bs[q][:, 0:P * (hi - lo)], kd[0:48, h, :], vbd[:, h % 2, lo:hi, :], start=True, stop=True)
                last.then_inc(s["sn_done"], 1)

            for h in range(H):
                pe.wait_ge(s["on_sq"], h + 1)
                if h >= 2:
                    pe.wait_ge(s["on_root"], h - 1)
                mm(bank[h % 2][:, 0:T], ones[:], sqh[h % 3], start=True, stop=True).then_inc(s["on_sum"], 1)
            pe.wait_ge(s["projd_in"], 16)
            pe.wait_ge(s["o_ready"], H)
            for m in range(KC):
                if m >= 2:
                    pe.wait_ge(s["y_mm_evac"], m - 1)
                for k in range(KC):
                    last = mm(bank[m % 2][:, 0:T], proj[:, k, P * m:P * (m + 1)], qkv[:, k, :],
                              start=(k == 0), stop=(k == KC - 1))
                last.then_inc(s["y_mm_done"], 1)
                new_state(m)
            pe.wait_ge(s["wout_in"], 16)
            pe.wait_ge(s["s_evac"], 4 + H)
            pe.wait_ge(s["y_mm_evac"], KC)
            for c in range(3):
                for f in range(2):
                    bk = bank[(4, 5, 6, 7, 0, 1)[2 * c + f]]
                    for k in range(KC):
                        last = mm(bk[0:ROWS[c], :], gate[:, k, tile_tokens(c)], wout[:, k, HALF * f:HALF * (f + 1)],
                                  start=(k == 0), stop=(k == KC - 1))
                    last.then_inc(s["o_mm_done"], 1)
            for c in range(3):
                pe.wait_ge(s["xn2_ready"], c + 1)
                for g in range(2):
                    n = 2 * c + g
                    if n >= 2:
                        pe.wait_ge(s["xn2t_evac"], n - 1)
                    for k in range(4 * g, 4 * g + 4):
                        last = nc.tensor.transpose(bank[2 + g][:, ROWS[c] * (k % 4):ROWS[c] * (k % 4 + 1)],
                                                   xn2[0:ROWS[c], c, P * k:P * (k + 1)], ident[0:ROWS[c], 0:ROWS[c]])
                    last.then_inc(s["xn2t_done"], 1)
            pe.wait_ge(s["xn2t_evac"], 6)
            pe.wait_ge(s["h_ready"], 6)
            for c in range(3):
                for k in range(KC):
                    last = mm(bank[4][0:ROWS[c], NE * c:NE * (c + 1)], xn2T[:, k, tile_tokens(c)], wr[:, k, :],
                              start=(k == 0), stop=(k == KC - 1))
            last.then_inc(s["lg_done"], 1)
            pe.wait_ge(s["mask_ready"], 1)
            mask = rt[0]
            for c in range(3):
                out = bank[5][0:ROWS[c], NE * c:NE * (c + 1)]
                for c2 in range(c):
                    mm(out, ones[:, 0:ROWS[c]], mask[:, c2, :], start=(c2 == 0), stop=False)
                mm(out, strict[0:ROWS[c], 0:ROWS[c]], mask[0:ROWS[c], c, :], start=(c == 0), stop=True)
            for c in range(3):
                last = mm(bank[5][:, 96:128], ones[0:ROWS[c], :], mask[0:ROWS[c], c, :], start=(c == 0), stop=(c == 2))
            last.then_inc(s["pos_done"], 1)

            def expert(b):
                pe.wait_ge(s["xg_in"], b * 16 + 16)
                for q in range(4):
                    last = nc.tensor.transpose(bank[0][:, P * q:P * (q + 1)], xg[:, P * q:P * (q + 1)], ident[:])
                last.then_inc(s["xgt_done"], 1)
                pe.wait_ge(s["bias_in"], b * 32 + 32)
                pe.wait_ge(s["act_ready"], b)
                for v in range(2):
                    mm(bank[1 + v][:], halves, brow[:, v, :], start=True, stop=False, skip_group_check=True)
                pe.wait_ge(s["xgt_ready"], b + 1)
                for k in range(KC):
                    pe.wait_ge(up_in[k], b * 16 + 16)
                    for v in range(2):
                        for f in range(2):
                            last = mm(bank[1 + v][64 * f:64 * f + 64, :], xgT[:, k % 4, k // 4, :],
                                      wup[k][:, D * v + HALF * f:D * v + HALF * (f + 1)],
                                      start=False, stop=(k == KC - 1), skip_group_check=True)
                    last.then_inc(s["up_used"], 1)
                pe.wait_ge(s["y_ready"], b)
                mm(bank[4][:], halves, brow[:, 2, :], start=True, stop=False, skip_group_check=True
                   ).then_inc(s["bias_used"], 1)
                pe.wait_ge(s["act_ready"], b + 1)
                for q in range(4):
                    last = nc.tensor.transpose(bank[3][:, P * q:P * (q + 1)], act_h[:, P * q:P * (q + 1)], ident[:])
                last.then_inc(s["actt_done"], 1)
                pe.wait_ge(s["actt_ready"], b + 1)
                for k in range(KC):
                    pe.wait_ge(down_in[k], b * 16 + 16)
                    for f in range(2):
                        last = mm(bank[4][64 * f:64 * f + 64, :], actT[:, k % 4, k // 4, :],
                                  wdn[k][:, HALF * f:HALF * (f + 1)],
                                  start=False, stop=(k == KC - 1), skip_group_check=True)
                    last.then_inc(s["down_used"], 1)

            pe.wait_ge(s["tok_ready"], 1)
            with pe.Fori(0, NE) as b:
                expert(b)
            nx = pe.value_load(info_i[0:1, 0:1], min_val=0, max_val=XB)
            with pe.Fori(0, XB) as x:
                with pe.If(x < nx):
                    expert(x + NE)

        @block.scalar
        def _(act):
            fn = nc.scalar.activation
            n = [0]

            def then(ins):
                n[0] += 1
                ins.then_inc(s["act_chain"], 1)
                act.wait_ge(s["act_chain"], n[0])

            act.wait_ge(s["const_ready"], 1)
            act.wait_ge(s["x_in"], 80)
            for c in range(3):
                last = fn(xn[0:ROWS[c], c, :], xrow[0:ROWS[c], c, :], ACT.Square, accum_out=ss[0:ROWS[c], c:c + 1])
            last.then_inc(s["ss_ready"], 1)
            act.wait_ge(s["ss_ready"], 1)
            for c in range(3):
                then(fn(rstd[0:ROWS[c], c:c + 1], ss[0:ROWS[c], c:c + 1], ACT.Ln, bias=c_eps[0:ROWS[c]], scale=1.0 / D))
            for c in range(3):
                last = fn(rstd[0:ROWS[c], c:c + 1], rstd[0:ROWS[c], c:c + 1], ACT.Exp, scale=-0.5)
                last.then_inc(s["rstd_ready"], 1)
            act.wait_ge(s["ab_ready"], 1)
            then(fn(gw2, gw1, ACT.Exp, scale=-1.0))
            then(fn(gw2, gw2, ACT.Ln, bias=c_one))
            then(fn(alog, alog, ACT.Exp))
            fn(beta, abt[:, :, 8:16], ACT.Sigmoid).then_inc(s["win_bank_free"], 1)
            fn(misc[:, off[0]:off[0] + 1], c_one, ACT.Copy).then_inc(s["win_bank_free"], 1)

            with act.Fori(0, 2) as it:
                for j in range(WRING):
                    act.wait_ge(s["win_used"], it * WRING + (j + 1))
                    bv, bg = bank[2 * (j % 2)], bank[2 * (j % 2) + 1]
                    k = it * WRING + j
                    fn(uh[:, bass.ds(k, 1), CH:CH + PT], bv[:, 0:PT].unsqueeze(1), ACT.Copy)
                    fn(uh[:, bass.ds(k, 1), CH + PT:UW].rearrange("p a (n t) -> p (a n) t", n=NB)[:, :, CH:CH + NS],
                       tok2(bv), ACT.Copy)
                    fn(acc[:, bass.ds(k, 1), :], bg[:, 0:T].unsqueeze(1), ACT.Sigmoid).then_inc(s["win_bank_free"], 1)

            def silu_step(v):
                act.wait_ge(s["conv_ready"], v * 2 + 2)
                fn(qkv[:, bass.ds(v * 2, 2), :], qkv[:, bass.ds(v * 2, 2), :], ACT.Silu).then_inc(s["silu_done"], 1)

            def qkv_round(it):
                for j in range(WRING):
                    act.wait_ge(s["win_used"], 8 * WRING + j + 1 if isinstance(it, int) else it * WRING + (5 * WRING + j + 1))
                    for f in range(2):
                        src = bank[2 * (j % 2) + f]
                        k = it * 8 + (2 * j + f)
                        fn(pre[:, 2 * j + f, SH:SH + PT], src[:, 0:PT], ACT.Copy)
                        fn(pre[:, 2 * j + f, SH + PT:QW].rearrange("p (n t) -> p n t", n=NB)[:, :, SH:SH + NS],
                           tok2(src), ACT.Copy).then_inc(s["qkv_copied"], 1)
                        fn(qtail[:, bass.ds(k, 1), 0:SH], src[:, PT - SH:PT].unsqueeze(1), ACT.Copy)
                        last = fn(qtail[:, bass.ds(k, 1), SH:27].rearrange("p a (n t) -> p (a n) t", n=NB),
                                  tok2(src)[:, :, NS - SH:NS], ACT.Copy)
                    last.then_inc(s["win_bank_free"], 1)
                for j in range(WRING):
                    silu_step(it * WRING + j)

            for k in range(KC):
                act.wait_ge(s["u_ready"], k + 1)
                fn(utail[:, k, 0:CH], uh[:, k, CH + PT - CH:CH + PT], ACT.Copy)
                fn(utail[:, k, CH:62].rearrange("p (n t) -> p n t", n=NB), sample_u(k)[:, :, CH:CH + NS], ACT.Copy)
            act.wait_ge(s["y_zeroed"], 16)
            for j in range(WRING):
                act.wait_ge(s["win_used"], 2 * WRING + j + 1)
                for f in range(2):
                    last = fn(zs[:, 2 * j + f, :], bank[2 * (j % 2) + f][:, 0:T], ACT.Silu)
                last.then_inc(s["win_bank_free"], 1)

            def gate_round(it):
                for j in range(WRING):
                    act.wait_ge(s["win_used"], (3 + it) * WRING + j + 1)
                    last = fn(gate[:, it * 8 + 2 * j, :], bank[2 * (j % 2)][:, 0:T], ACT.Sigmoid)
                    last = fn(gate[:, it * 8 + 2 * j + 1, :], bank[2 * (j % 2) + 1][:, 0:T], ACT.Sigmoid)
                    last.then_inc(s["win_bank_free"], 1)

            gate_round(0)
            act.wait_ge(s["centered"], 1)
            fn(sq[:, :, :], acc[:, :, :], ACT.Square).then_inc(s["squared"], 1)
            gate_round(1)
            act.wait_ge(s["sumsq_done"], 1)
            fn(rsc, bank[5][:, 0:T], ACT.Sqrt, bias=c_eps, scale=1.0 / D).then_inc(s["ln_std"], 1)
            act.wait_ge(s["scaled"], 1)
            for k in range(KC):
                fn(acc[:, k, :], acc[:, k, :], ACT.Silu, bias=pcol[:, k, R_LNB:R_LNB + 1],
                   scale=pcol[:, k, R_LNG:R_LNG + 1]).then_inc(s["conf_act"], 1)
            with act.Fori(0, 2) as it:
                qkv_round(it)
            for i in range(16):
                act.wait_ge(s["l2_sum"], i + 1)
                fn(norms[i // 8][:, i % 8, :], bank[4 + i % 4][:, 0:T], ACT.Sqrt, bias=c_epsq if i < H else c_eps,
                   scale=float(P) if i < H else 1.0).then_inc(s["l2_root"], 1)
            qkv_round(V_ROUND)
            for c in range(3):
                R = ROWS[c]
                dt, eg = heads(u_dt, R), heads(u_eg, R)
                vn = u_kb.rearrange("p (h n) -> p h n", h=H)
                act.wait_ge(s["ekd_arg"], c + 1)
                fn(ekd[0:R], ekd[0:R], ACT.Exp).then_inc(s["ekd_ready"], 1)
                act.wait_ge(s["rows_done"], 2 * c + 2)
                if c:
                    act.wait_ge(s["s_evac"], 2 * c)
                    act.wait_ge(s["o_evac"], 2 * c)
                for g in range(2):
                    fn(eg[:, 4 * g:4 * g + 4, :], bank[1 + g][:, 0:4 * R].rearrange("p (h n) -> p h n", h=4), ACT.Exp
                       ).then_inc(s["eg_ready"], 1)
                act.wait_ge(s["dt_arg"], c + 1)
                fn(dt[0:R], dt[0:R], ACT.Exp).then_inc(s["dt_ready"], 1)
                act.wait_ge(s["uq_evac"], 4 * c + 4)
                for lev in levels(act, c):
                    for g in range(2):
                        act.wait_ge(s["zt_done"], lev * 2 + (14 * c + g + 1))
                        fn(dt[0:R, 4 * g:4 * g + 4, :], bank[g][0:R, 0:4 * R].rearrange("p (h n) -> p h n", h=4), ACT.Copy
                           ).then_inc(s["zt_copied"], 1)
                if c == 2:
                    for g in range(2):
                        act.wait_ge(s["seg_done"], g + 1)
                        fn(kqs[:, 4 * g:4 * g + 4, :, :],
                           bank[6 + g][:, 0:384].rearrange("p (h a n) -> p h a n", h=4, a=2), ACT.Copy
                           ).then_inc(s["seg_copied"], 1)
                for g in range(2):
                    act.wait_ge(s["vn_done"], 2 * c + g + 1)
                    fn(vn[0:R, 4 * g:4 * g + 4, :], bank[g][0:R, :].rearrange("p (h n) -> p h n", h=4), ACT.Copy
                       ).then_inc(s["vn_ready"], 1)
                if c < 2:
                    for g in range(2):
                        act.wait_ge(s["o_done"], 2 * c + g + 1)
                        fn(qkv[:, 4 * g:4 * g + 4, tile_tokens(c)],
                           bank[2 + g][:, 0:4 * R].rearrange("p (h n) -> p h n", h=4), ACT.Copy).then_inc(s["o_evac"], 1)
            act.wait_ge(s["o_evac"], 6)

            def head_norm(h):
                act.wait_ge(s["on_sum"], h + 1)
                if h >= 3:
                    act.wait_ge(s["o_ready"], h - 2)
                fn(rs[h % 3], bank[h % 2][:, 0:T], ACT.Sqrt, bias=c_epsq).then_inc(s["on_root"], 1)

            for h in range(H):
                if h >= 3:
                    act.wait_ge(s["on_sum"], h - 2)
                fn(sqh[h % 3], qkv[:, h, :], ACT.Square).then_inc(s["on_sq"], 1)
                if h:
                    head_norm(h - 1)
            head_norm(H - 1)
            for c in range(3):
                act.wait_ge(s["h_ready"], 2 * c + 2)
                if c == 0:
                    act.wait_ge(s["o_mm_done"], 6)
                then(fn(xn2[0:ROWS[c], c, :], xrow[0:ROWS[c], c, :], ACT.Square, accum_out=ss[0:ROWS[c], c:c + 1]))
                then(fn(rstd[0:ROWS[c], c:c + 1], ss[0:ROWS[c], c:c + 1], ACT.Ln, bias=c_eps[0:ROWS[c]], scale=1.0 / D))
                fn(rstd[0:ROWS[c], c:c + 1], rstd[0:ROWS[c], c:c + 1], ACT.Exp, scale=-0.5).then_inc(s["hrstd_ready"], 1)
            act.wait_ge(s["gsub_ready"], 1)
            fn(gts, gts, ACT.Exp).then_inc(s["gexp_ready"], 1)

            def expert(b):
                act.wait_ge(s["xgt_done"], b + 1)
                fn(xgT, bank[0][:].rearrange("p (c a n) -> p c a n", c=4, a=2), ACT.Copy).then_inc(s["xgt_ready"], 1)
                act.wait_ge(s["hg_ready"], b + 1)
                fn(sg, hg, ACT.Sigmoid, scale=1.702).then_inc(s["sg_ready"], 1)
                act.wait_ge(s["actt_done"], b + 1)
                fn(actT, bank[3][:].rearrange("p (c a n) -> p c a n", c=4, a=2), ACT.Copy).then_inc(s["actt_ready"], 1)
                act.wait_ge(s["y_ready"], b + 1)
                for f in range(2):
                    act.dma_start(y_d[bass.ds(b * SLOTS, SLOTS), HALF * f:HALF * (f + 1)], ysb[64 * f:64 * f + 64, :]
                                  ).then_inc(s["y_stored"], 16)

            with act.Fori(0, NE) as b:
                expert(b)
            act.wait_ge(s["y_stored"], 32 * NE)
            nx = act.value_load(info_i[0:1, 0:1], min_val=0, max_val=XB)
            with act.Fori(0, XB) as x:
                with act.If(x < nx):
                    expert(x + NE)
            act.wait_ge(s["y_stored"], nx * 32 + 32 * NE)
            fn(misc[:, off[0]:off[0] + 1], c_one, ACT.Copy).then_inc(s["experts_done"], 1)
            for c in range(3):
                act.wait_ge(s["fsq_ready"], c + 1)
                then(fn(xn2[0:ROWS[c], c, :], xrow[0:ROWS[c], c, :], ACT.Square, accum_out=ss[0:ROWS[c], c:c + 1]))
                then(fn(rstd[0:ROWS[c], c:c + 1], ss[0:ROWS[c], c:c + 1], ACT.Ln, bias=c_eps[0:ROWS[c]], scale=1.0 / D))
                fn(rstd[0:ROWS[c], c:c + 1], rstd[0:ROWS[c], c:c + 1], ACT.Exp, scale=-0.5).then_inc(s["frstd_ready"], 1)

        @block.vector
        def _(dve):
            v = nc.vector
            n = [0]

            def then(ins):
                n[0] += 1
                ins.then_inc(s["dve_chain"], 1)
                dve.wait_ge(s["dve_chain"], n[0])

            stt = v.scalar_tensor_tensor
            for k in range(KC):
                v.memset(uh[:, k, 0:CH], 0.0)
            for k in range(8):
                v.memset(pre[:, k, 0:SH], 0.0)
            then(v.memset(abt, 0.0))
            for c in range(3):
                dve.wait_ge(s["rstd_ready"], c + 1)
                v.tensor_scalar(xn[0:ROWS[c], c, :], xrow[0:ROWS[c], c, :], rstd[0:ROWS[c], c:c + 1], None, ALU.mult
                                ).then_inc(s["xn_ready"], 1)
            dve.wait_ge(s["job_done"], 1)
            v.tensor_copy(pcol[:, :, :], bank[0][:, 0:KC * NROWS].rearrange("p (k n) -> p k n", k=KC)
                          ).then_inc(s["job_evac"], 1)
            dve.wait_ge(s["job_evac"], 1)
            for c in range(3):
                for g in range(2):
                    j = 1 + 2 * c + g
                    R = ROWS[c]
                    dve.wait_ge(s["job_done"], j + 1)
                    v.tensor_tensor(xnT[:, 4 * g:4 * g + 4, tile_tokens(c)],
                                    bank[j % 8][:, 0:4 * R].rearrange("p (k n) -> p k n", k=4),
                                    pcol[:, 4 * g:4 * g + 4, R_NMIX:R_NMIX + 1].to_broadcast((P, 4, R)), ALU.mult
                                    ).then_inc(s["job_evac"], 1)
            for t in range(2):
                for g in range(2):
                    j = 7 + 2 * t + g
                    dve.wait_ge(s["job_done"], j + 1)
                    for k in range(4 * g, 4 * g + 4):
                        last = v.tensor_copy(sample_u(k)[:, 4 * t:4 * t + 4, 0:CH],
                                             bank[j % 8][:, 120 * (k % 4):120 * (k % 4 + 1)]
                                             .rearrange("p (n t) -> p n t", n=4))
                    last.then_inc(s["job_evac"], 1)
            for g in range(2):
                j = 11 + g
                dve.wait_ge(s["job_done"], j + 1)
                v.tensor_copy(dh[:, 12 * g:12 * g + 12, :],
                              bank[j % 8][:, 0:288].rearrange("p (k n) -> p k n", k=12)).then_inc(s["job_evac"], 1)
            dve.wait_ge(s["ab_done"], 1)
            for c in range(3):
                last = v.tensor_copy(abt[0:ROWS[c], c, :], bank[13 % 8][0:ROWS[c], 16 * c:16 * c + 16])
            last.then_inc(s["job_evac"], 1)
            dve.wait_ge(s["job_evac"], 14)
            then(v.tensor_tensor(g_t, abt[:, :, 0:8], dtb.unsqueeze(1).to_broadcast((P, 3, H)), ALU.add))
            then(v.tensor_scalar(gw1, g_t, -1.0, None, ALU.mult))
            then(v.tensor_tensor(gw1, gw1, g_t, ALU.max))
            v.tensor_scalar(g_t, g_t, 0.0, None, ALU.max).then_inc(s["ab_ready"], 1)
            dve.wait_ge(s["win_bank_free"], 1)
            dve.wait_ge(s["ab_ready"], 1)
            then(v.tensor_tensor(g_t, g_t, gw2, ALU.add))
            then(stt(g_t, g_t, -1.0, alog.unsqueeze(1).to_broadcast((P, 3, H)), ALU.mult, ALU.mult))
            v.tensor_scalar(nbeta, beta, -1.0, None, ALU.mult).then_inc(s["beta_ready"], 1)

            def taps(n_taps, chunks, base, last_sem, bias=None):
                for tap in range(n_taps):
                    for part in range(2):
                        for i, (dst, src, weight) in enumerate(chunks):
                            out, x = ((dst[:, :, 0:PT].rearrange("p a n -> p (a n)"), src[0](tap)) if part == 0 else
                                      (dst[:, :, PT:T].rearrange("p a (n t) -> p (a n) t", n=NB), src[1](tap)))
                            if tap == 0:
                                last = v.tensor_scalar(out, x, weight(tap), bias[i] if bias else None, ALU.mult,
                                                       *([ALU.add] if bias else []))
                            else:
                                dve.wait_ge(s["conv_chain"], base + (4 * (tap - 1) + 2 * part + i + 1))
                                last = stt(out, x, weight(tap), out, ALU.mult, ALU.add)
                            if tap < n_taps - 1:
                                last.then_inc(s["conv_chain"], 1)
                            elif part == 1:
                                last.then_inc(last_sem, 1)

            CLINKS = 4 * (CW - 1)
            with dve.Fori(0, KC // 2) as it:
                pair = []
                for i in range(2):
                    k = it * 2 + i
                    dve.wait_ge(s["win_bank_free"], it * 2 + (i + 3))
                    up = uh[:, bass.ds(k, 1), CH:CH + PT]
                    v.tensor_tensor(up, up, acc[:, bass.ds(k, 1), 0:PT], ALU.mult)
                    us = uh[:, bass.ds(k, 1), CH + PT:UW].rearrange("p a (n t) -> p (a n) t", n=NB)[:, :, CH:CH + NS]
                    v.tensor_tensor(us, us, acc[:, bass.ds(k, 1), PT:T].rearrange("p a (n t) -> p (a n) t", n=NB), ALU.mult
                                    ).then_inc(s["u_ready"], 1)

                    def one(v4):
                        return v4.rearrange("p a n -> p (a n)")
                    src = uh[:, bass.ds(k, 1), :]
                    pair.append((acc[:, bass.ds(k, 1), :],
                                 (lambda tap, src=src: one(src[:, :, tap:tap + PT]),
                                  lambda tap, src=src: src[:, :, CH + PT:UW].rearrange("p a (n t) -> p (a n) t", n=NB)
                                  [:, :, tap:tap + NS]),
                                 lambda tap, k=k: one(pcol[:, bass.ds(k, 1), R_DW + tap:R_DW + tap + 1])))
                dve.wait_ge(s["u_ready"], it * 2 + 2)
                taps(CW, pair, it * CLINKS, s["conf_done"],
                     [one(pcol[:, bass.ds(it * 2 + i, 1), R_BDW:R_BDW + 1]) for i in range(2)])

            dve.wait_ge(s["sum_done"], 1)
            then(v.tensor_scalar(mu, bank[4][:, 0:T], 1.0 / D, None, ALU.mult))
            v.tensor_tensor(acc[:, :, :], acc[:, :, :], mu.unsqueeze(1).to_broadcast((P, KC, T)), ALU.subtract
                            ).then_inc(s["centered"], 1)
            dve.wait_ge(s["ln_std"], 1)
            then(v.reciprocal(rsc, rsc))
            v.tensor_tensor(acc[:, :, :], acc[:, :, :], rsc.unsqueeze(1).to_broadcast((P, KC, T)), ALU.mult
                            ).then_inc(s["scaled"], 1)

            QLINKS = 2 + 4 * (SW - 1)
            QBASE = KC // 2 * CLINKS

            def short_conv(it, j):
                pair = []
                base = it * (4 * QLINKS) + (QBASE + j // 2 * QLINKS)
                for i in (j, j + 1):
                    k = it * 8 + i
                    dve.wait_ge(s["qkv_copied"], it * 8 + (i + 1))
                    hist = pre[:, i, SH + PT:QW].rearrange("p (n t) -> p n t", n=NB)
                    v.tensor_copy(hist[:, :, 0:SH], dh[:, bass.ds(k, 1), :].rearrange("p a (n t) -> p (a n) t", n=NB)
                                  ).then_inc(s["conv_chain"], 1)
                    pair.append((qkv[:, bass.ds(k, 1), :],
                                 (lambda tap, i=i: pre[:, i, tap:tap + PT],
                                  lambda tap, hist=hist: hist[:, :, tap:tap + NS]),
                                 lambda tap, i=i: pcol[:, i, bass.ds(it + (R_DN + 3 * tap), 1)]))
                dve.wait_ge(s["conv_chain"], base + 2)
                taps(SW, pair, base + 2, s["conv_ready"])

            def l2_scale(i):
                dve.wait_ge(s["l2_root"], 8 * i + 8)
                then(v.reciprocal(norms[i], norms[i]))
                w = qkv[:, 8 * i:8 * i + 8, :]
                v.tensor_tensor(w, w, norms[i], ALU.mult).then_inc(s["l2_scaled"], 8)

            with dve.Fori(0, 2) as it:
                for j in range(0, 8, 2):
                    short_conv(it, j)
            dve.wait_ge(s["win_bank_free"], 2 + 20)
            for j in range(WRING):
                for m in (2 * j, 2 * j + 1):
                    dve.wait_ge(s["win_used"], 7 * WRING + j + 1)
                    stt(gate[:, m, :], bank[2 * (j % 2) + m % 2][:, 0:T], pcol[:, m, R_BCO:R_BCO + 1], gate[:, m, :],
                        ALU.add, ALU.mult).then_inc(s["conf_mm_evac"], 1)
            for j in range(WRING):
                short_conv(V_ROUND, 2 * j)
                if j < 2:
                    l2_scale(j)

            for g in range(8):
                dve.wait_ge(s["tail_t_done"], g + 1)
                if g < 2:
                    dst, src = uout[:, 512 * g:512 * (g + 1)], bank[4 + g][0:62, :]
                else:
                    dst, src = qout[:, 512 * (g - 2):512 * (g - 1)], bank[4 + g % 4][0:27, :]
                v.tensor_copy(dst, src).then_inc(s["tail_evac"], 1)

            dve.wait_ge(s["l2_scaled"], 16)

            for c in range(3):
                R = ROWS[c]
                tt = tile_tokens(c)
                ng = (neg if c < 2 else neg2)[0:R, 0:R]
                kb, dt, eg, uu, qk, x, xt = (heads(w, R) for w in (u_kb, u_dt, u_eg, u_u, u_qk, u_x, u_xt))
                kqe = u_kqe[:, 0:2 * H * R].rearrange("p (h a n) -> p h a n", h=H, a=2)
                kd, vb, vn = (w.rearrange("p (h n) -> p h n", h=H) for w in (u_kd, u_vb, u_kb))

                def four(w, m, r):
                    return w[0:m, 0:4 * r].rearrange("p (h n) -> p h n", h=4)

                dve.wait_ge(s["small_mm"], c + 1)
                if c:
                    dve.wait_ge(s["tok_evac"], 4 * c)
                then(v.tensor_copy(gcs[0:R], bank[0][0:R, 0:16]))
                v.tensor_tensor(ekd[0:R], gcs[0:R, 8:16], gcs[0:R, 0:8], ALU.subtract).then_inc(s["ekd_arg"], 1)
                for g in range(2):
                    dve.wait_ge(s["eg_ready"], 2 * c + g + 1)
                    for h in range(4 * g, 4 * g + 4):
                        last = stt(dt[0:R, h, :], bank[1 + g][0:R, R * (h % 4):R * (h % 4 + 1)], gcs[0:R, h:h + 1], ng,
                                   ALU.subtract, ALU.add)
                last.then_inc(s["dt_arg"], 1)
                for g in range(2):
                    dve.wait_ge(s["brow_done"], 2 * c + 2)
                    v.tensor_tensor(kb[:, 4 * g:4 * g + 4, :], qkv[:, H + 4 * g:H + 4 * g + 4, tt],
                                    four(bank[3 + g], P, R), ALU.mult).then_inc(s["kb_ready"], 1)
                v.tensor_tensor(kqe[:, :, 0, :], qkv[:, H:2 * H, tt], eg, ALU.mult)
                v.tensor_tensor(kqe[:, :, 1, :], qkv[:, 0:H, tt], eg, ALU.mult)
                dve.wait_ge(s["dt_ready"], c + 1)
                for g in range(2):
                    dve.wait_ge(s["uq_done"], 4 * c + 2 * g + 1)
                    v.tensor_tensor(uu[0:R, 4 * g:4 * g + 4, :], four(bank[5 + g], R, R), dt[0:R, 4 * g:4 * g + 4, :],
                                    ALU.mult).then_inc(s["uq_evac"], 1)
                for g in range(2):
                    dve.wait_ge(s["uq_done"], 4 * c + 2 * g + 2)
                    v.tensor_tensor(qk[0:R, 4 * g:4 * g + 4, :], four(bank[7 - 7 * g], R, R), dt[0:R, 4 * g:4 * g + 4, :],
                                    ALU.mult).then_inc(s["uq_evac"], 1)
                dve.wait_ge(s["ekd_ready"], c + 1)
                for g in range(4):
                    dve.wait_ge(s["tok_done"], 4 * c + g + 1)
                    hs = slice(4 * (g % 2), 4 * (g % 2) + 4)
                    dst, w = (kd, ekd[0:R]) if g < 2 else (vb, beta[0:R, c, :])
                    v.tensor_tensor(dst[0:R, hs, :], four(bank[1 + g], R, P), w[:, hs].unsqueeze(2).to_broadcast((R, 4, P)),
                                    ALU.mult).then_inc(s["tok_evac"], 1)
                v.tensor_copy(x[0:R], ident[0:R, 0:R].unsqueeze(1).to_broadcast((R, H, R)))
                v.tensor_copy(xt[0:R], ident[0:R, 0:R].unsqueeze(1).to_broadcast((R, H, R))).then_inc(s["x_updated"], 1)
                dve.wait_ge(s["x_updated"], 15 * c + 1)
                for lev in levels(dve, c):
                    for g in range(2):
                        hs = slice(4 * g, 4 * g + 4)
                        dve.wait_ge(s["x_updated"], lev * 2 + (15 * c + g))
                        dve.wait_ge(s["vt_done"], lev * 2 + (14 * c + g + 1))
                        v.tensor_tensor(x[0:R, hs, :], x[0:R, hs, :], four(bank[2 + g], R, R), ALU.subtract)
                        v.tensor_tensor(xt[0:R, hs, :], xt[0:R, hs, :], four(bank[4 + g], R, R), ALU.subtract
                                        ).then_inc(s["x_updated"], 1)
                if c:
                    for g in range(2):
                        dve.wait_ge(s["kes_done"], 2 * (c - 1) + g + 1)
                        src = bank[6 + g] if c == 1 else bank[4 + g]
                        for h in range(4 * g, 4 * g + 4):
                            last = stt(vb[0:R, h, :], src[0:R, P * (h % 4):P * (h % 4 + 1)], nbeta[0:R, c, h:h + 1],
                                       vb[0:R, h, :], ALU.mult, ALU.add)
                        last.then_inc(s["r_ready"], 1)
                if c == 0:
                    for g in range(2):
                        dve.wait_ge(s["s_done"], g + 1)
                        v.tensor_copy(S[:, 4 * g:4 * g + 4, :], four(bank[4 + g], P, P)).then_inc(s["s_evac"], 1)
                    dve.wait_ge(s["s_evac"], 2)
                elif c == 1:
                    for g in range(2):
                        dve.wait_ge(s["s_done"], 2 + g + 1)
                        for h in range(4 * g, 4 * g + 4):
                            last = stt(S[:, h, :], S[:, h, :], eg[:, h, R - 1:R], bank[4 + g][:, P * (h % 4):P * (h % 4 + 1)],
                                       ALU.mult, ALU.add)
                        last.then_inc(s["s_evac"], 1)
                    dve.wait_ge(s["s_evac"], 4)
                else:
                    for g in range(2):
                        dve.wait_ge(s["o_done"], 4 + g + 1)
                        v.tensor_tensor(qkv[:, 4 * g:4 * g + 4, tt], kqs[:, 4 * g:4 * g + 4, 1, :], four(bank[2 + g], P, R),
                                        ALU.add).then_inc(s["o_evac"], 1)

            dve.wait_ge(s["o_evac"], 6)
            for h in range(H):
                v.tensor_tensor(s0[:, h, :, :], s0[:, h, :, :],
                                eg[:, h, TAIL + NS - 1:48:NS]
                                .unsqueeze(2).to_broadcast((P, NB, P)), ALU.mult).then_inc(s["s_decayed"], 1)
                dve.wait_ge(s["on_root"], h + 1)
                v.reciprocal(rs[h % 3], rs[h % 3]).then_inc(s["on_inv"], 1)
                dve.wait_ge(s["on_inv"], h + 1)
                dve.wait_ge(s["on_prod"], h + 1)
                v.tensor_tensor(qkv[:, h, :], qkv[:, h, :], rs[h % 3], ALU.mult).then_inc(s["o_ready"], 1)
            dve.wait_ge(s["s_decayed"], H)
            for m in range(KC):
                dve.wait_ge(s["y_mm_done"], m + 1)
                then(v.tensor_tensor(gate[:, KC + m, :], bank[m % 2][:, 0:T], gate[:, KC + m, :], ALU.mult))
                v.tensor_tensor(gate[:, m, :], gate[:, m, :], gate[:, KC + m, :], ALU.add).then_inc(s["y_mm_evac"], 1)
                dve.wait_ge(s["sn_done"], m + 1)
                bs = (bank[4], bank[5], bank[6]) if m % 2 == 0 else (bank[7], bank[2], bank[3])
                stt(S[:, m, :], S[:, m, :], eg[:, m, TAIL - 1:TAIL], bs[0][:, 0:P], ALU.mult, ALU.add)
                v.tensor_tensor(s0[:, m, 0:3, :], s0[:, m, 0:3, :], bs[0][:, P:512].rearrange("p (n v) -> p n v", n=3),
                                ALU.add)
                v.tensor_tensor(s0[:, m, 3:7, :], s0[:, m, 3:7, :], bs[1][:, :].rearrange("p (n v) -> p n v", n=4),
                                ALU.add)
                v.tensor_tensor(s0[:, m, 7, :], s0[:, m, 7, :], bs[2][:, 0:P], ALU.add).then_inc(s["s_evac"], 1)
            for c in range(3):
                for f in range(2):
                    i = 2 * c + f
                    dve.wait_ge(s["o_mm_done"], i + 1)
                    w = xrow[0:ROWS[c], c, HALF * f:HALF * (f + 1)]
                    v.tensor_tensor(w, w, bank[(4, 5, 6, 7, 0, 1)[i]][0:ROWS[c], :], ALU.add).then_inc(s["h_ready"], 1)
            dve.wait_ge(s["norms_in"], 32)
            dve.wait_ge(s["router_in"], 48)
            for c in range(3):
                dve.wait_ge(s["hrstd_ready"], c + 1)
                stt(xn2[0:ROWS[c], c, :], xrow[0:ROWS[c], c, :], rstd[0:ROWS[c], c:c + 1], nffn[0:ROWS[c], :],
                    ALU.mult, ALU.mult).then_inc(s["xn2_ready"], 1)
            for c in range(3):
                for g in range(2):
                    dve.wait_ge(s["xn2t_done"], 2 * c + g + 1)
                    v.tensor_copy(xn2T[:, 4 * g:4 * g + 4, tile_tokens(c)],
                                  bank[2 + g][:, 0:4 * ROWS[c]].rearrange("p (k n) -> p k n", k=4)
                                  ).then_inc(s["xn2t_evac"], 1)
            then(v.memset(halves, 0.0))
            v.memset(lg, 0.0)
            v.memset(rt[1], 0.0)
            then(v.memset(halves[0:1, 0:64], 1.0))
            then(v.tensor_scalar(halves[:, 64:128], halves[:, 0:64], -1.0, 1.0, ALU.mult, ALU.add))
            dve.wait_ge(s["lg_done"], 1)
            for c in range(3):
                R = ROWS[c]
                then(v.tensor_tensor(lg[0:R, c, :], bank[4][0:R, NE * c:NE * (c + 1)], brt[0:R], ALU.add))
                then(v.max(mx8[:, c, :], lg[:, c, :]))
                then(v.max_index(ix8[:, c, :], mx8[:, c, :], lg[:, c, :]))
            then(v.tensor_copy(ixf, ix8))
            v.tensor_tensor(gts, mx8[:, :, 0:TOPK], mx8[:, :, 0:1].to_broadcast((P, 3, TOPK)), ALU.subtract
                            ).then_inc(s["gsub_ready"], 1)
            for c in range(3):
                last = v.tensor_tensor(oh[:, c], iota_e.unsqueeze(1).to_broadcast((P, TOPK, NE)),
                                       ixf[:, c, 0:TOPK].unsqueeze(2).to_broadcast((P, TOPK, NE)), ALU.is_equal)
            then(last)
            then(v.tensor_tensor(rt[0], oh[:, :, 0, :], oh[:, :, 1, :], ALU.add))
            then(v.tensor_tensor(rt[0], rt[0], oh[:, :, 2, :], ALU.add))
            v.tensor_tensor(rt[0], rt[0], oh[:, :, 3, :], ALU.add).then_inc(s["mask_ready"], 1)
            dve.wait_ge(s["gexp_ready"], 1)
            then(v.tensor_reduce(gsum.unsqueeze(2), gts, AX.X, ALU.add))
            then(v.reciprocal(gsum, gsum))
            then(v.tensor_tensor(gts, gts, gsum.unsqueeze(2).to_broadcast((P, 3, TOPK)), ALU.mult))
            dve.wait_ge(s["pos_done"], 1)
            pos, pd, slot, t1, t2, dl, yl = rt[1], rt[2], rt[3], rt[4], rt[5], rt[6], rt[7]
            for c in range(3):
                last = v.tensor_copy(pos[0:ROWS[c], c, :], bank[5][0:ROWS[c], NE * c:NE * (c + 1)])
            then(v.tensor_copy(cnt, bank[5][:, 96:128]))
            v.tensor_scalar(pd, pos, float(SLOTS), None, ALU.is_ge)
            then(v.tensor_scalar(nbx, cnt, float(SLOTS), None, ALU.is_gt))
            for m in range(2, 5):
                stt(pd, pos, float(SLOTS * m), pd, ALU.is_ge, ALU.add)
                then(stt(nbx, cnt, float(SLOTS * m), nbx, ALU.is_gt, ALU.add))
            then(stt(slot, pd, -float(SLOTS), pos, ALU.mult, ALU.add))
            then(v.tensor_copy(cs[0], nbx))
            for i in range(5):
                w = 1 << i
                src, dst = cs[i % 2], cs[(i + 1) % 2]
                v.tensor_copy(dst[:, 0:w], src[:, 0:w])
                then(v.tensor_tensor(dst[:, w:NE], src[:, w:NE], src[:, 0:NE - w], ALU.add))
            incl = cs[1]
            then(v.tensor_tensor(xs, incl, nbx, ALU.subtract))
            then(stt(t1, pd, float(NE - 1), xs.unsqueeze(1).to_broadcast((P, 3, NE)), ALU.add, ALU.add))
            then(v.tensor_tensor(t2, iota_e.unsqueeze(1).to_broadcast((P, 3, NE)), t1, ALU.subtract))
            then(stt(t2, pd, 0.0, t2, ALU.is_equal, ALU.mult))
            then(v.tensor_tensor(t1, t1, t2, ALU.add))
            stt(dl, slot, float(NBLK), t1, ALU.mult, ALU.add)
            then(stt(yl, t1, float(SLOTS), slot, ALU.mult, ALU.add))
            for src, dst in ((dl, dli), (yl, yli)):
                then(v.tensor_tensor(ohm, oh, src.unsqueeze(2).to_broadcast((P, 3, TOPK, NE)), ALU.mult))
                then(v.tensor_reduce(self_.unsqueeze(3), ohm, AX.X, ALU.add))
                then(v.tensor_copy(dst, self_))
            dve.wait_ge(s["s_out"], 16 * (H + 1))
            v.tensor_copy(info[:, 0:1], incl[0:1, NE - 1:NE])
            shape = (1, XB, NE)
            then(v.tensor_scalar(xio, iota_e[0:1, 0:XB], 0.0, None, ALU.add))
            v.tensor_tensor(bx[0], xio.unsqueeze(2).to_broadcast(shape), xs[0:1].unsqueeze(1).to_broadcast(shape), ALU.is_ge)
            then(v.tensor_tensor(bx[1], xio.unsqueeze(2).to_broadcast(shape), incl[0:1].unsqueeze(1).to_broadcast(shape),
                                 ALU.is_ge))
            then(v.tensor_tensor(bx[0], bx[0], bx[1], ALU.subtract))
            then(v.tensor_tensor(bx[2], bx[0], iota_e[0:1].unsqueeze(1).to_broadcast(shape), ALU.mult))
            then(v.tensor_reduce(info[:, 1:1 + XB].unsqueeze(2), bx[2], AX.X, ALU.add))
            v.tensor_copy(info_i[0:1, :], info).then_inc(s["idx_ready"], 1)
            dve.wait_ge(s["tok_in"], 32)
            v.tensor_scalar(tokt, tokt, 2.0, half_col, ALU.mult, ALU.add).then_inc(s["tok_ready"], 1)

            moe_chain = s["expert_chain"]

            def expert(b):
                dve.wait_ge(s["up_used"], b * KC + KC)
                v.tensor_scalar(hg, bank[1][:], 7.0, None, ALU.min).then_inc(s["hg_ready"], 1)
                v.tensor_scalar(hl, bank[2][:], 7.0, -7.0, ALU.min, ALU.max).then_inc(moe_chain, 1)
                dve.wait_ge(moe_chain, b * 2 + 1)
                stt(hgl, hl, 1.0, hg, ALU.add, ALU.mult).then_inc(moe_chain, 1)
                dve.wait_ge(moe_chain, b * 2 + 2)
                dve.wait_ge(s["sg_ready"], b + 1)
                v.tensor_tensor(act_h, hgl, sg, ALU.mult).then_inc(s["act_ready"], 1)
                dve.wait_ge(s["down_used"], b * KC + KC)
                dve.wait_ge(s["y_stored"], b * 32)
                v.tensor_copy(ysb, bank[4][:]).then_inc(s["y_ready"], 1)

            with dve.Fori(0, NE) as b:
                expert(b)
            nx = dve.value_load(info_i[0:1, 0:1], min_val=0, max_val=XB)
            with dve.Fori(0, XB) as xx:
                with dve.If(xx < nx):
                    expert(xx + NE)
            for r in range(TOPK):
                dve.wait_ge(y_in[r], 48)
                for c in range(3):
                    R = ROWS[c]
                    last = stt(xrow[0:R, c, :], ygat[3 * r + c][0:R, :], gts[0:R, c, r:r + 1], xrow[0:R, c, :],
                               ALU.mult, ALU.add)
                    if r < TOPK - 1 and c == 2:
                        then(last)
                    if r == TOPK - 1:
                        last.then_inc(s["fsq_ready"], 1)
            dve.wait_ge(s["fsq_ready"], 3)
            for c in range(3):
                R = ROWS[c]
                dve.wait_ge(s["frstd_ready"], c + 1)
                stt(xn2[0:R, c, :], xrow[0:R, c, :], rstd[0:R, c:c + 1], nfin[0:R, :], ALU.mult, ALU.mult
                    ).then_inc(s["final_ready"], 1)


_INS = ['x_prompt', 'x_sample', 'state_conf_conv', 'state_dn_conv', 'state_dn_S', 'meta_tokens', 'norm_mix', 'w_in',
        'w_conf_dw', 'b_conf_dw', 'ln_conf_g', 'ln_conf_b', 'w_conf_out', 'b_conf_out', 'w_dn_conv', 'dn_a_log',
        'dn_dt_bias', 'dn_norm_w', 'w_dn_out', 'w_out', 'norm_ffn', 'w_router', 'b_router', 'w_up', 'b_up', 'w_down',
        'b_down', 'norm_final']
_OUTS = {'y_prompt': (1, 256, 1024), 'y_sample': (8, 4, 1024), 'cp': (1, 1, 30, 1024), 'dp': (1, 1, 3, 3072),
         'sp': (1, 1, 8, 128, 128), 'cs': (1, 8, 30, 1024), 'ds': (1, 8, 3, 3072), 'ss': (1, 8, 8, 128, 128)}


def kernel(**inputs):
    import numpy as _np
    import concourse.bacc as _bacc
    from concourse.bass_utils import run_bass_kernel_spmd as _run

    nc = _bacc.Bacc("TRN2", target_bir_lowering=False, num_devices=1)
    arrays, args = {}, {}
    for name in _INS:
        v = _np.ascontiguousarray(inputs[name])
        arrays[f"in_{name}"] = v
        args[name] = nc.dram_tensor(f"in_{name}", v.shape, mybir.dt.from_np(v.dtype), kind="ExternalInput").ap()
    for name, shape in _OUTS.items():
        args[name] = nc.dram_tensor(f"out_{name}", shape, F32, kind="ExternalOutput").ap()
    build(nc, args)
    r = _run(nc, [arrays], core_ids=[0])
    return tuple(r.results[0][f"out_{name}"] for name in _OUTS)
```

```python
import concourse.bass as bass
from concourse import mybir
from contextlib import ExitStack
import math

F32 = mybir.dt.float32
I32 = mybir.dt.int32
U32 = mybir.dt.uint32
ALU = mybir.AluOpType
ACT = mybir.ActivationFunctionType
AX = mybir.AxisListType

P = 128
D = 1024
KC = D // P
META = 16
SEQ = 256
NB, NS = 8, 4
PT = META + SEQ
T = PT + NB * NS
ROWS = [128, 128, T - 256]
TAIL = PT - 256
H = 8
CW = 31
CH = CW - 1
SW = 4
SH = SW - 1
UW = CH + PT + NB * (CH + NS)
QW = SH + PT + NB * (SH + NS)
NE = 32
TOPK = 4
SLOTS = 64
XB = 18
NBLK = NE + XB
HALF = 512
V_ROUND = 2
EPS = 1e-6
O_Z = 5120
O_A = 6144
O_GATE = 6160
BIG = 1e30
LEVELS = 7
LEVELS2 = 4

R_DW, R_NMIX, R_BDW, R_LNG, R_LNB, R_BCO, R_DN = 0, 31, 32, 33, 34, 35, 36
NROWS = R_DN + 3 * SW

WRING = 4
STEPS = 9 * WRING
A_UH = WRING * 2048
A_SQ = A_UH
A_XNT = A_UH + KC * UW
A_PRE = A_XNT + KC * T
A_XN = A_PRE + 8 * QW
A_PROW = A_XN + 3 * D
A_CH = A_PROW + D
A_KN = A_PRE + 8 * QW
A_QO = A_KN + KC * T
A_DH = A_QO + 3072
A_S0 = 8192
A_PROJ = 16384
ARENA = 24576


def levels(eng, c):
    n = LEVELS if c < 2 else LEVELS2
    if c < 2:
        with eng.Fori(1, n - 1) as lev:
            yield lev, False
    else:
        for lev in range(1, n - 1):
            yield lev, False
    yield n - 1, True


def first(b):
    return isinstance(b, int) and b == 0


def tile_tokens(c):
    return slice(128 * c, 128 * c + ROWS[c])


def build(nc, a):
    ctx = ExitStack()
    with ctx:
        def sb(name, shape, dt=F32):
            return ctx.enter_context(nc.sbuf_tensor(name, shape, dt))

        def sem(name):
            return ctx.enter_context(nc.semaphore(name))

        xn2_d = nc.dram_tensor("xn2_d", (T, D), F32, kind="Internal").ap()
        tok_d = nc.dram_tensor("tok_d", (SLOTS, NBLK), I32, kind="Internal").ap()
        y_d = nc.dram_tensor("y_d", (NBLK * SLOTS, D), F32, kind="Internal").ap()

        arena = sb("arena", [P, ARENA])
        xrow = sb("xrow", [P, 3, D])
        acc = sb("acc", [P, KC, T])
        qkv = sb("qkv", [P, 24, T])
        zs = sb("zs", [P, H, T])
        gate = sb("gate", [P, 2 * KC, T])
        pcol = sb("pcol", [P, KC, NROWS])
        ident = sb("ident", [P, P])
        ones = sb("ones", [P, P])
        causal = sb("causal", [P, P])
        causal2 = sb("causal2", [48, 48])
        same2 = sb("same2", [48, 48])
        neg = sb("neg", [P, P])
        neg2 = sb("neg2", [48, 48])
        segm = sb("segm", [48, 9])
        lmask = sb("lmask", [P, LEVELS, P])
        strict = sb("strict", [P, P])
        wab = sb("wab", [P, KC, 16])
        wr = sb("wr", [P, KC, NE])
        misc = sb("misc", [P, 720])
        temps = sb("temps", [P, 5 * 1024])

        off = [0]

        def small(n, dt=F32):
            v = misc[:, off[0]:off[0] + n]
            off[0] += n
            return v if dt == F32 else v.bitcast(dt)

        c_eps, c_one, c_epsq = small(1), small(1), small(1)
        half_col = small(1)
        dnw = small(1)
        ss = small(3)
        rstd = small(3)
        alog, dtb = small(8), small(8)
        abt = small(48).rearrange("p (c n) -> p c n", c=3)
        g_t = small(24).rearrange("p (c n) -> p c n", c=3)
        beta = small(24).rearrange("p (c n) -> p c n", c=3)
        nbeta = small(24).rearrange("p (c n) -> p c n", c=3)
        gw1 = small(24).rearrange("p (c n) -> p c n", c=3)
        gw2 = small(24).rearrange("p (c n) -> p c n", c=3)
        gcs = small(16)
        ekd = small(8)
        iota_e = small(32)
        tokid = small(3, I32)
        tokt = small(NBLK, I32)
        info_i = small(1 + XB, I32)
        idxcol = small(1, I32)
        brt = small(32)
        mx8 = small(24).rearrange("p (c n) -> p c n", c=3)
        ix8 = small(24, U32).rearrange("p (c n) -> p c n", c=3)
        gts = small(12).rearrange("p (c n) -> p c n", c=3)
        gsum = small(3)
        dli = small(12, I32).rearrange("p (c n) -> p c n", c=3)
        yli = small(12, I32).rearrange("p (c n) -> p c n", c=3)
        zero_i = small(NBLK, I32)
        wait_scratch, final_scratch = small(1), small(1)
        credit = small(2)

        wring = arena[:, 0:WRING * 2048].rearrange("p (s k n) -> p s k n", s=WRING, k=KC)
        uh = arena[:, A_UH:A_XNT].rearrange("p (k n) -> p k n", k=KC)
        xnT = arena[:, A_XNT:A_PRE].rearrange("p (k n) -> p k n", k=KC)
        pre = arena[:, A_PRE:A_XN].rearrange("p (k n) -> p k n", k=8)
        xn = arena[:, A_XN:A_PROW].rearrange("p (c n) -> p c n", c=3)
        prow = arena[0:NROWS, A_PROW:A_CH]
        chrow = arena[0:120, A_CH:A_CH + 2 * D].rearrange("p (c n) -> p c n", c=2)
        dhrow = temps[0:24, 0:3072]
        dh = arena[:, A_DH:A_DH + 24 * 24].rearrange("p (k n) -> p k n", k=24)
        utail = arena[:, A_DH + 576:A_DH + 576 + KC * 62].rearrange("p (k n) -> p k n", k=KC)
        samp = temps[:, 3072:3072 + KC * NB * NS].rearrange("p (k n t) -> p k n t", k=KC, n=NB)
        qtail = temps[:, 4144:4144 + 24 * 27].rearrange("p (k n) -> p k n", k=24)
        uout = arena[0:62, A_SQ:A_SQ + 1024]
        qout = arena[0:27, A_QO:A_QO + 3072]

        def unit(n, w=1):
            if n < 5:
                return temps[:, n * 1024:(n + w) * 1024]
            return arena[:, (n - 5) * 1024:(n - 5 + w) * 1024]

        def heads(u, R):
            return u[:, 0:H * R].rearrange("p (h n) -> p h n", h=H)
        u_dt, u_eg, u_um, u_kb, u_s = (unit(n) for n in range(5))
        u_kqe, u_u, u_qk, u_vb, u_x, u_xt = unit(5, 2), unit(7), unit(8), unit(9), unit(10), unit(11)
        u_kd = acc[:, :, :].rearrange("p k n -> p (k n)")[:, 0:1024]
        S = u_s.rearrange("p (h n) -> p h n", h=H)
        s0 = arena[:, A_S0:A_S0 + 8192].rearrange("p (h n v) -> p h n v", h=H, n=NB)
        kqs = u_u[:, 0:768].rearrange("p (h a n) -> p h a n", h=H, a=2)
        vbd = qkv[:, 16:24, :].rearrange("p k n -> p (k n)")[0:48, 0:2304].rearrange("p (b s v) -> p b s v", b=2, s=9)
        proj = arena[:, A_PROJ:A_PROJ + 8192].rearrange("p (k n) -> p k n", k=KC)
        wout = arena[:, 0:8192].rearrange("p (k n) -> p k n", k=KC)
        sq = arena[:, A_SQ:A_SQ + KC * T].rearrange("p (k n) -> p k n", k=KC)
        mu = temps[:, 1024:1024 + T]
        rsc = temps[:, 1024 + T:1024 + 2 * T]
        sqh = [temps[:, T * i:T * (i + 1)] for i in range(3)]
        norms = [arena[:, o:o + KC * T].rearrange("p (k n) -> p k n", k=KC) for o in (A_UH, A_KN)]
        hnorm = qkv[:, 8:16, :]

        nffn = acc[:, :, :].rearrange("p k n -> p (k n)")[:, 1024:2048]
        nfin = u_kd
        qflat = qkv[:, :, :].rearrange("p k n -> p (k n)")
        xn2 = qflat[:, 0:3072].rearrange("p (c n) -> p c n", c=3)
        xn2T = zs
        lg = temps[:, 0:96].rearrange("p (c n) -> p c n", c=3)
        oh = temps[:, 128:512].rearrange("p (c r n) -> p c r n", c=3, r=TOPK)
        ohm = temps[:, 512:896].rearrange("p (c r n) -> p c r n", c=3, r=TOPK)
        rt = [temps[:, 1024 + 96 * i:1120 + 96 * i].rearrange("p (c n) -> p c n", c=3) for i in range(9)]
        cnt, nbx, xs, ci = (temps[:, 2048 + 32 * i:2080 + 32 * i] for i in range(4))
        cs = [temps[:, 2304 + 32 * i:2336 + 32 * i] for i in range(2)]
        ixf = temps[:, 2400:2424].rearrange("p (c n) -> p c n", c=3)
        self_ = temps[:, 2432:2444].rearrange("p (c n) -> p c n", c=3)
        xio = temps[0:1, 2448:2448 + XB]
        info = temps[0:1, 2480:2480 + 1 + XB]
        bx = [temps[0:1, 2560 + 576 * i:3136 + 576 * i].rearrange("p (x e) -> p x e", x=XB) for i in range(3)]

        xg = qflat[:, 0:512]
        xgT = qflat[:, 512:1024].rearrange("p (c a n) -> p c a n", c=4, a=2)
        hg = qflat[:, 1024:1536]
        sg = qflat[:, 1536:2048]
        hl = qflat[:, 2048:2560]
        hgl = qflat[:, 2560:3072]
        act_h = qflat[:, 3072:3584]
        actT = qflat[:, 3584:4096].rearrange("p (c a n) -> p c a n", c=4, a=2)
        ysb = qflat[:, 4096:4608]
        brow = qflat[0:2, 4608:6144].rearrange("p (a n) -> p a n", a=3)
        halves = qflat[0:2, 6144:6272]
        wup = [arena[:, 2048 * ((k + 4) % KC):2048 * ((k + 4) % KC + 1)] for k in range(KC)]
        wdn = [arena[:, A_PROJ + 1024 * k:A_PROJ + 1024 * (k + 1)] for k in range(KC)]
        ygat = [arena[:, 1024 * i:1024 * (i + 1)] for i in range(12)]

        bank = [ctx.enter_context(nc.psum_tensor(f"bank{i}", [P, 512], F32)) for i in range(8)]

        names = """y_zero y_zeroed x_in par_in small_in hist_in chist_in const_ready pool_chain dve_chain act_chain
            ss_ready rstd_ready xn_ready job_done job_evac ab_done win_used win_bank_free u_ready
            conf_done qkv_copied conv_ready silu_done tail_t_done tail_evac tail_out sum_done
            sumsq_done centered squared scaled conf_act conf_mm_evac l2_sq l2_sum l2_root l2_scaled
            ab_ready beta_ready small_mm ekd_arg ekd_ready gl_ready bl_ready rows_done brow_done
            dt_arg dt_ready eg_ready kb_ready uq_done uq_evac tok_done tok_evac um_ready zt_done
            zt_copied vt_done x_updated kes_done r_ready vn_done vn_ready o_done o_evac s_done
            s_evac s0_in seg_done seg_copied vbd_ready sn_done s_out on_sq on_sum on_inv on_prod
            s_decayed router_in on_ln ln_std samp_chain zs_ready beta_act l2_inv o_ready projd_in
            y_mm_done y_mm_evac wout_in o_mm_done h_ready hrstd_ready xn2_ready xn2_stored xn2t_done
            xn2t_evac lg_done gsub_ready gexp_ready mask_ready pos_done idx_ready dl_ready yl_ready
            zero_in scattered tok_in tok_ready norms_in bias_in bias_used up_used down_used xg_in
            xgt_done xgt_ready hg_ready sg_ready act_ready actt_done actt_ready y_ready y_stored
            fsq_ready frstd_ready final_ready out_done sampleconf_out idx_copied conv_chain
            expert_chain""".split()
        s = {n: sem(n) for n in names}
        win_in = [sem(f"win_in{i}") for i in range(WRING)]
        up_in = [sem(f"up_in{i}") for i in range(KC)]
        down_in = [sem(f"down_in{i}") for i in range(KC)]
        y_in = [sem(f"y_in{i}") for i in range(3)]

        block = ctx.enter_context(nc.Block())

        w_in_v = a["w_in"][0].rearrange("(k p) n -> p k n", p=P)
        w_up_v = a["w_up"][0].rearrange("e (k p) n -> p e k n", p=P)
        w_dn_v = a["w_down"][0].rearrange("e (k p) n -> p e k n", p=P)
        b_up_v = a["b_up"][0].rearrange("e (a f n) -> f e a n", a=2, f=2)
        b_dn_v = a["b_down"][0].rearrange("e (f n) -> f e n", f=2)

        def prompt_u(k):
            return uh[:, k, CH:CH + PT]

        def sample_u(k):
            return uh[:, k, CH + PT:UW].rearrange("p (n t) -> p n t", n=NB)

        def tok2(v):
            return v[:, PT:T].rearrange("p (n t) -> p n t", n=NB)

        @block.sync
        def _(sp):
            for dst, src in ((xrow[0:META, 0, :], a["meta_tokens"]),
                             (xrow[META:128, 0, :], a["x_prompt"][0, 0:112, :]),
                             (xrow[:, 1, :], a["x_prompt"][0, 112:240, :]),
                             (xrow[0:TAIL, 2, :], a["x_prompt"][0, 240:256, :]),
                             (xrow[TAIL:48, 2, :], a["x_sample"].rearrange("n t d -> (n t) d"))):
                sp.dma_start(dst, src).then_inc(s["x_in"], 16)
            for r, src in ((R_DW, a["w_conf_dw"][0]), (R_NMIX, a["norm_mix"]), (R_BDW, a["b_conf_dw"]),
                           (R_LNG, a["ln_conf_g"]), (R_LNB, a["ln_conf_b"]), (R_BCO, a["b_conf_out"]),
                           (R_DN, a["w_dn_conv"][0].rearrange("t (a n) -> (t a) n", a=3))):
                sp.dma_start(prow[r:r + src.shape[0], :], src).then_inc(s["par_in"], 16)

            def win_load(step, col_a, col_b):
                slot = step % WRING
                for j, col in enumerate((col_a, col_b)):
                    sp.dma_start(wring[:, slot, :, 128 * j:128 * (j + 1)],
                                 w_in_v[:, :, bass.ds(col, 128)]).then_inc(win_in[slot], 16)

            for t in range(2):
                sp.dma_start(chrow[:, t, :], a["state_conf_conv"][0, 4 * t:4 * t + 4].rearrange("n t d -> (n t) d")
                             ).then_inc(s["chist_in"], 16)
            sp.dma_start(dhrow, a["state_dn_conv"][0].rearrange("n t d -> (n t) d")).then_inc(s["hist_in"], 16)
            win_load(0, 0, D)
            sp.dma_start(wab[:, :, :], w_in_v[:, :, O_A:O_GATE]).then_inc(s["small_in"], 16)
            sp.dma_start(alog, a["dn_a_log"].to_broadcast((P, H))).then_inc(s["small_in"], 16)
            sp.dma_start(dtb, a["dn_dt_bias"].to_broadcast((P, H))).then_inc(s["small_in"], 16)
            for j in range(1, WRING):
                win_load(j, 128 * j, D + 128 * j)
            sp.dma_start(dnw, a["dn_norm_w"].rearrange("a n -> n a")).then_inc(s["router_in"], 16)
            sp.dma_start(wr[:, :, :], a["w_router"][0].rearrange("(k p) n -> p k n", p=P)).then_inc(s["router_in"], 16)
            sp.dma_start(brt, a["b_router"].to_broadcast((P, NE))).then_inc(s["router_in"], 16)
            for j in range(WRING):
                sp.wait_ge(s["win_used"], j + 1)
                win_load(j, 128 * (WRING + j), D + 128 * (WRING + j))

            def win_group(it, col0, weights=w_in_v):
                for j in range(WRING):
                    sp.wait_ge(s["win_used"], WRING * it + j - (WRING - 1))
                    for f in range(2):
                        sp.dma_start(wring[:, j, :, 128 * f:128 * (f + 1)],
                                     weights[:, :, bass.ds(col0 + (256 * j + 128 * f), 128)]).then_inc(win_in[j], 16)

            win_group(2, O_Z)
            with sp.Fori(3, 5) as it:
                win_group(it, it * 1024 + (O_GATE - 3 * 1024))
            with sp.Fori(5, 7) as it:
                win_group(it, it * 1024 + (2 * D - 5 * 1024))
            win_group(7, 0, a["w_conf_out"][0].rearrange("(k p) n -> p k n", p=P))
            win_group(8, 4 * D)
            sp.wait_ge(s["tail_evac"], 8)
            sp.dma_start(a["cp"][0, 0], uout[0:CH, :]).then_inc(s["tail_out"], 16)
            for b in range(NB):
                sp.dma_start(a["cs"][0, b, CH - NS:CH, :], uout[CH + NS * b:CH + NS * (b + 1), :]
                             ).then_inc(s["tail_out"], 16)
            sp.dma_start(a["dp"][0, 0], qout[0:SH, :]).then_inc(s["tail_out"], 16)
            sp.dma_start(a["ds"][0].rearrange("n t d -> (n t) d"), qout[SH:SH + NB * SH, :]
                         ).then_inc(s["tail_out"], 16)
            sp.wait_ge(s["conv_ready"], 24)
            sp.wait_ge(s["tail_out"], 16 * (NB + 3))
            sp.wait_ge(s["win_used"], STEPS)
            for h in range(H):
                sp.dma_start(s0[:, h, :, :], a["state_dn_S"][0, :, h].rearrange("n k v -> k n v")
                             ).then_inc(s["s0_in"], 16)
            sp.dma_start(proj[:, :, :], a["w_dn_out"][0].rearrange("(k p) n -> p k n", p=P)).then_inc(s["projd_in"], 16)
            sp.dma_start(nffn, a["norm_ffn"].to_broadcast((P, D))).then_inc(s["norms_in"], 16)
            sp.wait_ge(s["o_done"], 6)
            sp.wait_ge(s["o_evac"], 6)
            sp.dma_start(wout[:, :, :], a["w_out"][0].rearrange("(k p) n -> p k n", p=P)).then_inc(s["wout_in"], 16)
            sp.wait_ge(s["sn_done"], H)
            sp.dma_start(nfin, a["norm_final"].rearrange("(a n) -> a n", a=1).to_broadcast((P, D))
                         ).then_inc(s["norms_in"], 16)

            def load_up(e, k):
                sp.dma_start(wup[k], w_up_v[:, e, k, :]).then_inc(up_in[k], 16)

            def load_down(e, k):
                sp.dma_start(wdn[k], w_dn_v[:, e, k, :]).then_inc(down_in[k], 16)

            def load_bias(e):
                sp.dma_start(brow[:, 0:2, :], b_up_v[:, e, :, :]).then_inc(s["bias_in"], 16)
                sp.dma_start(brow[:, 2, :], b_dn_v[:, e, :]).then_inc(s["bias_in"], 16)

            sp.wait_ge(s["y_mm_done"], KC)
            for k in range(KC):
                load_down(0, k)
            load_bias(0)
            sp.wait_ge(s["s_out"], 16 * (H + 1))
            for k in range(4):
                load_up(0, k)
            sp.wait_ge(s["o_mm_done"], 6)
            for k in range(4, KC):
                load_up(0, k)

            def load_block(b, e):
                for k in range(KC):
                    sp.wait_ge(s["up_used"], KC * b + k - (KC - 1))
                    load_up(e, k)
                sp.wait_ge(s["bias_used"], b)
                load_bias(e)
                for k in range(KC):
                    sp.wait_ge(s["down_used"], KC * b + k - (KC - 1))
                    load_down(e, k)

            with sp.Fori(1, NE) as b:
                load_block(b, b)
            sp.wait_ge(s["idx_ready"], 1)
            nx = sp.value_load(info_i[0:1, 0:1], min_val=0, max_val=XB)
            with sp.Fori(0, XB) as x:
                with sp.If(x < nx):
                    e = sp.value_load(info_i[0:1, bass.ds(x + 1, 1)], min_val=0, max_val=NE - 1)
                    load_block(x + NE, e)

            sp.wait_ge(s["final_ready"], 3)
            for dst, src in ((a["y_prompt"][0, 0:112, :], xn2[META:128, 0, :]),
                             (a["y_prompt"][0, 112:240, :], xn2[:, 1, :]),
                             (a["y_prompt"][0, 240:256, :], xn2[0:TAIL, 2, :]),
                             (a["y_sample"].rearrange("n t d -> (n t) d"), xn2[TAIL:48, 2, :])):
                sp.dma_start(dst, src).then_inc(s["out_done"], 16)
            sp.wait_ge(s["out_done"], 64)

        @block.gpsimd
        def _(pool):
            n = [0]

            def then(ins):
                n[0] += 1
                ins.then_inc(s["pool_chain"], 1)
                pool.wait_ge(s["pool_chain"], n[0])

            def keep(v, pattern, base, cm):
                then(nc.gpsimd.affine_select(out=v, in_=v, compare_op=ALU.is_ge, fill=0.0, base=base,
                                             pattern=pattern, channel_multiplier=cm))

            for v, c in ((ident, 0.0), (ones, 1.0), (causal, 1.0), (lmask, 0.0), (same2, 0.0)):
                nc.gpsimd.memset(v[:], c)
            for v, c in ((c_eps, EPS), (c_one, 1.0), (c_epsq, P * EPS), (zero_i, 0)):
                nc.gpsimd.memset(v, c)
            nc.gpsimd.iota(tokid, pattern=[[128, 3]], base=0, channel_multiplier=1)
            then(nc.gpsimd.iota(iota_e, pattern=[[1, NE]], base=0, channel_multiplier=0,
                                allow_small_or_imprecise_dtypes=True))
            nc.gpsimd.tensor_scalar(half_col, tokid[:, 0:1], 64.0, None, ALU.is_ge)
            then(nc.gpsimd.affine_select(out=ident[:], in_=ident[:], compare_op=ALU.not_equal, fill=1.0, base=0,
                                         pattern=[[-1, P]], channel_multiplier=1))
            nc.gpsimd.memset(wait_scratch, 0.0).then_inc(s["const_ready"], 1)
            keep(causal[:], [[1, P]], 0, -1)
            for lev in range(LEVELS):
                b = 1 << lev
                v = lmask[:, lev, :].rearrange("p (n a b) -> p n a b", a=2, b=b)[:, :, 1, :]
                then(nc.gpsimd.memset(v, 1.0))
                keep(v, [[-2 * b, P // (2 * b)], [0, b]], 0, 1)
                keep(v, [[2 * b, P // (2 * b)], [0, b]], b - 1, -1)
            nc.gpsimd.memset(same2[:, 0:TAIL], 1.0)
            then(nc.gpsimd.memset(same2[:, TAIL:48], 1.0))
            keep(same2[:, 0:TAIL], [[0, TAIL]], TAIL - 1, -1)
            v = same2[:, TAIL:48].rearrange("p (n t) -> p n t", n=NB)
            keep(v, [[-NS, NB], [0, NS]], -TAIL, 1)
            keep(v, [[NS, NB], [0, NS]], TAIL + NS - 1, -1)
            nc.gpsimd.tensor_copy(segm[:, 0:1], same2[:, 0:1])
            nc.gpsimd.tensor_copy(segm[:, 1:9], same2[:, TAIL:48:NS])
            nc.gpsimd.tensor_tensor(strict[:], causal[:], ident[:], ALU.subtract)
            then(nc.gpsimd.tensor_tensor(causal2[:], same2[:], causal[0:48, 0:48], ALU.mult))
            nc.gpsimd.tensor_scalar(neg[:], causal[:], -1.0, BIG, ALU.add, ALU.mult)
            nc.gpsimd.tensor_scalar(neg2[:], causal2[:], -1.0, BIG, ALU.add, ALU.mult).then_inc(s["const_ready"], 1)
            pool.dma_start(tok_d, zero_i[0:SLOTS, :]).then_inc(s["zero_in"], 16)
            nc.gpsimd.memset(zs[:, 0:4, :], 0.0).then_inc(s["y_zero"], 1)
            pool.wait_ge(s["y_zero"], 1)
            pool.wait_ge(s["win_used"], 2)
            pool.dma_start(y_d[NE * SLOTS:NBLK * SLOTS, :].rearrange("(p a) n -> p a n", p=P),
                           zs[:, 0:4, :].rearrange("p k n -> p (k n)")[:, 0:D].unsqueeze(1).to_broadcast((P, XB // 2, D))
                           ).then_inc(s["y_zeroed"], 16)
            pool.dma_start(a["cs"][0, :, 0:CH - NS, :], a["state_conf_conv"][0, :, NS:CH, :]
                           ).then_inc(s["sampleconf_out"], 16)
            u_samples = uh[:, :, CH + PT:UW].rearrange("p k (n t) -> p k n t", n=NB)
            conf_samples = acc[:, :, PT:T].rearrange("p k (n t) -> p k n t", n=NB)

            def per_channel(row):
                return pcol[:, :, bass.ds(row, 1)].unsqueeze(3).to_broadcast((P, KC, NB, NS))

            pool.wait_ge(s["u_ready"], KC)
            nc.gpsimd.tensor_tensor(conf_samples, u_samples[:, :, :, 0:NS], per_channel(R_DW), ALU.mult
                                    ).then_inc(s["samp_chain"], 1)
            pool.wait_ge(s["samp_chain"], 1)
            nc.gpsimd.tensor_tensor(conf_samples, conf_samples, per_channel(R_BDW), ALU.add).then_inc(s["samp_chain"], 1)
            with pool.Fori(1, CW) as tap:
                pool.wait_ge(s["samp_chain"], tap * 2)
                nc.gpsimd.tensor_tensor(samp, u_samples[:, :, :, bass.ds(tap, NS)], per_channel(tap + R_DW), ALU.mult
                                        ).then_inc(s["samp_chain"], 1)
                pool.wait_ge(s["samp_chain"], tap * 2 + 1)
                nc.gpsimd.tensor_tensor(conf_samples, conf_samples, samp, ALU.add).then_inc(s["samp_chain"], 1)
            pool.wait_ge(s["win_bank_free"], 2 + 12)
            pool.wait_ge(s["router_in"], 48)
            nc.gpsimd.tensor_scalar(zs[:, :, :], zs[:, :, :], dnw, None, ALU.mult).then_inc(s["zs_ready"], 1)
            for j in range(16):
                pool.wait_ge(s["silu_done"], j // 2 + 1)
                if j >= 3:
                    pool.wait_ge(s["l2_sum"], j - 2)
                nc.gpsimd.tensor_tensor(sqh[j % 3], qkv[:, j, :], qkv[:, j, :], ALU.mult).then_inc(s["l2_sq"], 1)
            pool.wait_ge(s["sampleconf_out"], 16)

            def products():
                pool.wait_ge(s["zs_ready"], 1)
                for h in range(H):
                    pool.wait_ge(s["on_sq"], h + 1)
                    nc.gpsimd.tensor_tensor(qkv[:, h, :], qkv[:, h, :], zs[:, h, :], ALU.mult).then_inc(s["on_prod"], 1)

            for c in range(3):
                R = ROWS[c]
                cm = (causal if c < 2 else causal2)[0:R, 0:R]
                um, kb, uu = heads(u_um, R), heads(u_kb, R), heads(u_u, R)
                if c == 0:
                    pool.wait_ge(s["beta_ready"], 1)
                if c:
                    pool.wait_ge(s["s_evac"], 2 * c)
                nc.gpsimd.tensor_tensor(um[0:R], g_t[0:R, c, :].unsqueeze(2).to_broadcast((R, H, R)),
                                        cm.unsqueeze(1).to_broadcast((R, H, R)), ALU.mult).then_inc(s["gl_ready"], 1)
                nc.gpsimd.tensor_tensor(kb[0:R], beta[0:R, c, :].unsqueeze(2).to_broadcast((R, H, R)),
                                        ident[0:R, 0:R].unsqueeze(1).to_broadcast((R, H, R)), ALU.mult
                                        ).then_inc(s["bl_ready"], 1)
                pool.wait_ge(s["uq_evac"], 4 * c + 2)
                nc.gpsimd.tensor_tensor(um[0:R], uu[0:R], lmask[0:R, 0:1, 0:R].to_broadcast((R, H, R)), ALU.mult
                                        ).then_inc(s["um_ready"], 1)
                for lev, _ in levels(pool, c):
                    pool.wait_ge(s["zt_done"], lev * 2 + 14 * c)
                    pool.wait_ge(s["x_updated"], 14 * c + 1)
                    nc.gpsimd.tensor_tensor(um[0:R], uu[0:R],
                                            lmask[0:R, bass.ds(lev, 1), 0:R].to_broadcast((R, H, R)), ALU.mult
                                            ).then_inc(s["um_ready"], 1)
                if c == 2:
                    products()
                    for h in range(H):
                        pool.wait_ge(s["vn_ready"], 4 + h // 4 + 1)
                        if h >= 2:
                            pool.wait_ge(s["sn_done"], h - 1)
                        nc.gpsimd.tensor_tensor(vbd[:, h % 2, :, :],
                                                u_kb[0:48, :].rearrange("p (h n) -> p h n", h=H)[:, h, :].unsqueeze(1)
                                                .to_broadcast((48, 9, P)),
                                                segm[:].unsqueeze(2).to_broadcast((48, 9, P)), ALU.mult
                                                ).then_inc(s["vbd_ready"], 1)
                    for h in range(H):
                        pool.wait_ge(s["s_evac"], 4 + h + 1)
                        pool.dma_start(a["ss"][0, :, h].rearrange("n k v -> k n v"), s0[:, h, :, :]
                                       ).then_inc(s["s_out"], 16)
                    pool.dma_start(a["sp"][0, 0].rearrange("h k v -> k h v"), S).then_inc(s["s_out"], 16)
            pool.wait_ge(s["s_out"], 16 * (H + 1))

            pool.wait_ge(s["xn2_ready"], 3)
            for c in range(3):
                pool.dma_start(xn2_d[128 * c:128 * c + ROWS[c], :], xn2[0:ROWS[c], c, :]).then_inc(s["xn2_stored"], 16)
            pool.wait_ge(s["zero_in"], 16)
            pool.wait_ge(s["dl_ready"], 1)
            for c in range(3):
                for r in range(TOPK):
                    pool.indirect_dma_start(
                        out=tok_d.rearrange("a (b c) -> (a b) c", c=1),
                        out_offset=bass.IndirectOffsetOnAxis(ap=dli[0:ROWS[c], c, r:r + 1].bitcast(U32), axis=0),
                        in_=tokid[0:ROWS[c], c:c + 1], in_offset=None).then_inc(s["scattered"], 16)
            pool.wait_ge(s["scattered"], 16 * 3 * TOPK)
            for f in range(2):
                pool.dma_start(tokt[64 * f:64 * f + 64, :], tok_d).then_inc(s["tok_in"], 16)
            pool.wait_ge(s["tok_ready"], 1)
            pool.wait_ge(s["xn2_stored"], 48)
            xn2_halves = xn2_d.rearrange("t (f n) -> (t f) n", f=2)

            def gather(b):
                if not first(b):
                    pool.wait_ge(s["xgt_done"], b)
                nc.gpsimd.tensor_copy(idxcol, tokt[:, bass.ds(b, 1)]).then_inc(s["idx_copied"], 1)
                pool.wait_ge(s["idx_copied"], b + 1)
                nc.gpsimd.tensor_tensor(wait_scratch, c_one, c_one, ALU.mult)
                pool.indirect_dma_start(out=xg, out_offset=None, in_=xn2_halves,
                                        in_offset=bass.IndirectOffsetOnAxis(ap=idxcol.bitcast(U32), axis=0)
                                        ).then_inc(s["xg_in"], 16)
                pool.wait_ge(s["xg_in"], b * 16 + 16)

            gather(0)
            with pool.Fori(1, NE) as b:
                gather(b)
            pool.wait_ge(s["idx_ready"], 1)
            nx = pool.value_load(info_i[0:1, 0:1], min_val=0, max_val=XB)
            with pool.Fori(0, XB) as x:
                with pool.If(x < nx):
                    gather(x + NE)
            pool.wait_ge(s["y_stored"], nx * 32 + 32 * NE)
            nc.gpsimd.tensor_tensor(final_scratch, c_one, c_one, ALU.mult)
            pool.wait_ge(s["y_zeroed"], 16)
            pool.wait_ge(s["yl_ready"], 1)
            pool.wait_ge(s["down_used"], NE * KC)
            for c in range(3):
                for r in range(TOPK):
                    pool.indirect_dma_start(out=ygat[TOPK * c + r][0:ROWS[c], :], out_offset=None, in_=y_d,
                                            in_offset=bass.IndirectOffsetOnAxis(
                                                ap=yli[0:ROWS[c], c, r:r + 1].bitcast(U32), axis=0)
                                            ).then_inc(y_in[c], 16)

        @block.tensor
        def _(pe):
            mm = nc.tensor.matmul
            pe.wait_ge(s["const_ready"], 1)
            job = [0]

            def job_bank():
                if job[0] >= 8:
                    pe.wait_ge(s["job_evac"], job[0] - 7)
                return bank[job[0] % 8]

            def transposes(parts):
                b = job_bank()
                for src, col in parts:
                    k, m = src.shape
                    last = nc.tensor.transpose(b[0:m, col:col + k], src, ident[0:k, 0:k])
                last.then_inc(s["job_done"], 1)
                job[0] += 1

            pe.wait_ge(s["par_in"], 112)
            transposes([(prow[:, P * k:P * (k + 1)], NROWS * k) for k in range(KC)])
            pe.wait_ge(s["chist_in"], 32)
            for t in range(2):
                for g in range(2):
                    transposes([(chrow[:, t, P * k:P * (k + 1)], 120 * (k % 4)) for k in range(4 * g, 4 * g + 4)])
            pe.wait_ge(s["hist_in"], 16)
            for g in range(2):
                transposes([(dhrow[:, P * k:P * (k + 1)], 24 * (k % 12)) for k in range(12 * g, 12 * g + 12)])
            for c in range(3):
                pe.wait_ge(s["xn_ready"], c + 1)
                for g in range(2):
                    transposes([(xn[0:ROWS[c], c, P * k:P * (k + 1)], ROWS[c] * (k % 4)) for k in range(4 * g, 4 * g + 4)])
            pe.wait_ge(s["job_evac"], 13)

            def win_step(it, j, rhs):
                pe.wait_ge(win_in[j], it * 32 + 32)
                for f in range(2):
                    for k in range(KC):
                        last = mm(bank[2 * (j % 2) + f][:, 0:T], wring[:, j, k, P * f:P * (f + 1)], rhs[:, k, :],
                                  start=(k == 0), stop=(k == KC - 1))
                last.then_inc(s["win_used"], 1)

            def win_round(it, steps=range(WRING)):
                for j in steps:
                    pe.wait_ge(s["win_bank_free"], it * WRING + (j + 1))
                    win_step(it, j, xnT)

            def l2_sums(step):
                for n in range(4 * step, 4 * step + 4):
                    pe.wait_ge(s["l2_sq"], n + 1)
                    if n >= 4:
                        pe.wait_ge(s["l2_root"], n - 3)
                    mm(bank[4 + n % 4][:, 0:T], ones[:], sqh[n % 3], start=True, stop=True).then_inc(s["l2_sum"], 1)

            with pe.Fori(0, 4) as it:
                win_round(it)
            pe.wait_ge(s["small_in"], 48)
            for c in range(3):
                for k in range(KC):
                    last = mm(bank[6][0:ROWS[c], 16 * c:16 * c + 16], xnT[:, k, tile_tokens(c)], wab[:, k, :],
                              start=(k == 0), stop=(k == KC - 1))
            last.then_inc(s["ab_done"], 1)
            win_round(4, range(0, 2))
            pe.wait_ge(s["conf_done"], KC)
            pe.wait_ge(s["samp_chain"], 2 * CW)
            for k in range(KC):
                last = mm(bank[4][:, 0:T], ones[:], acc[:, k, :], start=(k == 0), stop=(k == KC - 1))
            last.then_inc(s["sum_done"], 1)
            win_round(4, range(2, WRING))
            pe.wait_ge(s["squared"], 1)
            for k in range(KC):
                last = mm(bank[5][:, 0:T], ones[:], sq[:, k, :], start=(k == 0), stop=(k == KC - 1))
            last.then_inc(s["sumsq_done"], 1)
            with pe.Fori(5, 7) as it:
                win_round(it)
            pe.wait_ge(s["conf_act"], KC)
            for j in range(WRING):
                if j < 2:
                    pe.wait_ge(s["win_bank_free"], 7 * WRING + (j + 1))
                else:
                    pe.wait_ge(s["conf_mm_evac"], 2 * j - 2)
                win_step(7, j, acc)
                l2_sums(j)
            for j in range(WRING):
                if j < 2:
                    pe.wait_ge(s["conf_mm_evac"], 2 * j + 6)
                else:
                    pe.wait_ge(s["win_bank_free"], 7 * WRING + (j + 1))
                win_step(8, j, xnT)
            pe.wait_ge(s["l2_root"], 16)
            pe.wait_ge(s["win_bank_free"], 34)
            for g in range(2):
                for k in range(4 * g, 4 * g + 4):
                    last = nc.tensor.transpose(bank[4 + g][0:62, P * (k % 4):P * (k % 4 + 1)], utail[:, k, :], ident[:])
                last.then_inc(s["tail_t_done"], 1)
            for g in range(6):
                if g >= 2:
                    pe.wait_ge(s["tail_evac"], g - 1)
                bk = bank[4 + (g + 2) % 4]
                for k in range(4 * g, 4 * g + 4):
                    last = nc.tensor.transpose(bk[0:27, P * (k % 4):P * (k % 4 + 1)], qtail[:, k, :], ident[:])
                last.then_inc(s["tail_t_done"], 1)
            pe.wait_ge(s["tail_evac"], 8)

            for c in range(3):
                R = ROWS[c]
                tt = tile_tokens(c)
                cm = (causal if c < 2 else causal2)[0:R, 0:R]
                sm = ones[0:R, 0:R] if c < 2 else same2[:, :]
                um, kb, dt, eg, uu, qk, x, xt = (heads(v, R) for v in
                                                 (u_um, u_kb, u_dt, u_eg, u_u, u_qk, u_x, u_xt))
                kqe = u_kqe[:, 0:2 * H * R].rearrange("p (h a n) -> p h a n", h=H, a=2)
                kd, vb, vn = (v.rearrange("p (h n) -> p h n", h=H) for v in (u_kd, u_vb, u_kb))
                zt = dt
                if c == 0:
                    pe.wait_ge(s["beta_ready"], 1)
                    pe.wait_ge(s["l2_scaled"], 16)
                    pe.wait_ge(s["silu_done"], 12)
                    pe.wait_ge(s["const_ready"], 2)
                else:
                    pe.wait_ge(s["s_evac"], 2 * c)
                    pe.wait_ge(s["o_evac"], 2 * c)
                mm(bank[0][0:R, 0:8], cm, g_t[0:R, c, :], start=True, stop=True)
                mm(bank[0][0:R, 8:16], sm, g_t[0:R, c, :], start=True, stop=True).then_inc(s["small_mm"], 1)
                pe.wait_ge(s["gl_ready"], c + 1)
                for g in range(2):
                    mm(bank[1 + g][:, 0:4 * R], ones[0:R, :], um[0:R, 4 * g:4 * g + 4, :], start=True, stop=True
                       ).then_inc(s["rows_done"], 1)
                pe.wait_ge(s["bl_ready"], c + 1)
                for g in range(2):
                    mm(bank[3 + g][:, 0:4 * R], ones[0:R, :], kb[0:R, 4 * g:4 * g + 4, :], start=True, stop=True
                       ).then_inc(s["brow_done"], 1)
                for g in range(2):
                    pe.wait_ge(s["kb_ready"], 2 * c + 2)
                    for kind, (bk, rhs) in enumerate(((bank[5 + g], kb), (bank[7 - 7 * g], None))):
                        for h in range(4 * g, 4 * g + 4):
                            mv = kb[:, h, :] if kind == 0 else qkv[:, h, tt]
                            last = mm(bk[0:R, R * (h % 4):R * (h % 4 + 1)], qkv[:, H + h, tt], mv, start=True, stop=True)
                        last.then_inc(s["uq_done"], 1)
                for g in range(4):
                    if g == 0:
                        pe.wait_ge(s["dt_arg"], c + 1)
                    for h in range(4 * (g % 2), 4 * (g % 2) + 4):
                        last = nc.tensor.transpose(bank[1 + g][0:R, P * (h % 4):P * (h % 4 + 1)],
                                                   qkv[:, H + h if g < 2 else 2 * H + h, tt], ident[:])
                    last.then_inc(s["tok_done"], 1)
                pe.wait_ge(s["uq_evac"], 4 * c + 4)
                pe.wait_ge(s["tok_evac"], 4 * c + 4)
                pe.wait_ge(s["um_ready"], 7 * c + 1)
                for g in range(2):
                    for h in range(4 * g, 4 * g + 4):
                        last = nc.tensor.transpose(bank[g][0:R, R * (h % 4):R * (h % 4 + 1)], um[0:R, h, :], ident[0:R, 0:R])
                    last.then_inc(s["zt_done"], 1)
                for lev, final in levels(pe, c):
                    pe.wait_ge(s["um_ready"], lev + (7 * c + 1))
                    for g in range(2):
                        pe.wait_ge(s["x_updated"], lev * 2 + (14 * c + g - 1))
                        for h in range(4 * g, 4 * g + 4):
                            last = mm(bank[g][0:R, R * (h % 4):R * (h % 4 + 1)], um[0:R, h, :], xt[0:R, h, :],
                                      start=True, stop=True)
                        last.then_inc(s["zt_done"], 1)
                    for g in range(2):
                        pe.wait_ge(s["zt_copied"], lev * 2 + (12 * c + g - 1))
                        for h in range(4 * g, 4 * g + 4):
                            last = mm(bank[2 + g][0:R, R * (h % 4):R * (h % 4 + 1)], zt[0:R, h, :], x[0:R, h, :],
                                      start=True, stop=True)
                        if not final:
                            for h in range(4 * g, 4 * g + 4):
                                last = mm(bank[4 + g][0:R, R * (h % 4):R * (h % 4 + 1)], x[0:R, h, :], zt[0:R, h, :],
                                          start=True, stop=True)
                        last.then_inc(s["vt_done"], 1)
                pe.wait_ge(s["x_updated"], 14 * c + 2 * (LEVELS if c < 2 else LEVELS2))
                if c == 1:
                    for g in range(2):
                        for h in range(4 * g, 4 * g + 4):
                            last = mm(bank[6 + g][0:R, P * (h % 4):P * (h % 4 + 1)], kqe[:, h, 0, :], S[:, h, :],
                                      start=True, stop=True)
                        last.then_inc(s["kes_done"], 1)
                if c == 2:
                    for g in range(2):
                        for h in range(4 * g, 4 * g + 4):
                            pe.wait_ge(s["s0_in"], 16 * H)
                            bv = bank[6 + g][:, 96 * (h % 4):96 * (h % 4 + 1)].rearrange("p (a n) -> p a n", a=2)
                            mm(bv[:, :, 0:TAIL], S[:, h, :], kqe[:, h, :, 0:TAIL], start=True, stop=True)
                            for b in range(NB):
                                w = slice(TAIL + NS * b, TAIL + NS * (b + 1))
                                last = mm(bv[:, :, w], s0[:, h, b, :], kqe[:, h, :, w], start=True, stop=True)
                        last.then_inc(s["seg_done"], 1)
                    for g in range(2):
                        pe.wait_ge(s["seg_copied"], g + 1)
                        for h in range(4 * g, 4 * g + 4):
                            last = nc.tensor.transpose(bank[4 + g][0:R, P * (h % 4):P * (h % 4 + 1)],
                                                       kqs[:, h, 0, :], ident[:])
                        last.then_inc(s["kes_done"], 1)
                for g in range(2):
                    if c:
                        pe.wait_ge(s["r_ready"], 2 * (c - 1) + g + 1)
                    for h in range(4 * g, 4 * g + 4):
                        last = mm(bank[g][0:R, P * (h % 4):P * (h % 4 + 1)], x[0:R, h, :], vb[0:R, h, :],
                                  start=True, stop=True)
                    last.then_inc(s["vn_done"], 1)
                for g in range(2):
                    pe.wait_ge(s["vn_ready"], 2 * c + g + 1)
                    for h in range(4 * g, 4 * g + 4):
                        o = bank[2 + g][:, R * (h % 4):R * (h % 4 + 1)]
                        if c == 1:
                            mm(o, S[:, h, :], kqe[:, h, 1, :], start=True, stop=False)
                        last = mm(o, vn[0:R, h, :], qk[0:R, h, :], start=(c != 1), stop=True)
                    last.then_inc(s["o_done"], 1)
                if c < 2:
                    for g in range(2):
                        for h in range(4 * g, 4 * g + 4):
                            last = mm(bank[4 + g][:, P * (h % 4):P * (h % 4 + 1)], kd[0:R, h, :], vn[0:R, h, :],
                                      start=True, stop=True)
                        last.then_inc(s["s_done"], 1)

            def new_state(h):
                pe.wait_ge(s["vbd_ready"], h + 1)
                if h == 0:
                    pe.wait_ge(s["r_ready"], 4)
                if h == 1:
                    pe.wait_ge(s["o_evac"], 6)
                if h >= 2:
                    pe.wait_ge(s["s_evac"], 4 + h - 1)
                bs = (bank[4], bank[5], bank[6]) if h % 2 == 0 else (bank[7], bank[2], bank[3])
                for q, (lo, hi) in enumerate(((0, 4), (4, 8), (8, 9))):
                    last = mm(bs[q][:, 0:P * (hi - lo)], kd[0:48, h, :], vbd[:, h % 2, lo:hi, :], start=True, stop=True)
                last.then_inc(s["sn_done"], 1)

            for h in range(H):
                pe.wait_ge(s["on_sq"], h + 1)
                if h >= 2:
                    pe.wait_ge(s["on_ln"], h - 1)
                mm(bank[h % 2][:, 0:T], ones[:], sqh[h % 3], start=True, stop=True).then_inc(s["on_sum"], 1)
            pe.wait_ge(s["projd_in"], 16)
            pe.wait_ge(s["o_ready"], H)
            for m in range(KC):
                if m >= 2:
                    pe.wait_ge(s["y_mm_evac"], m - 1)
                for k in range(KC):
                    last = mm(bank[m % 2][:, 0:T], proj[:, k, P * m:P * (m + 1)], qkv[:, k, :],
                              start=(k == 0), stop=(k == KC - 1))
                last.then_inc(s["y_mm_done"], 1)
                new_state(m)
            pe.wait_ge(s["wout_in"], 16)
            pe.wait_ge(s["s_evac"], 4 + H)
            pe.wait_ge(s["y_mm_evac"], KC)
            for c in range(3):
                for f in range(2):
                    bk = bank[(4, 5, 6, 7, 0, 1)[2 * c + f]]
                    for k in range(KC):
                        last = mm(bk[0:ROWS[c], :], gate[:, k, tile_tokens(c)], wout[:, k, HALF * f:HALF * (f + 1)],
                                  start=(k == 0), stop=(k == KC - 1))
                    last.then_inc(s["o_mm_done"], 1)
            for c in range(3):
                pe.wait_ge(s["xn2_ready"], c + 1)
                for g in range(2):
                    n = 2 * c + g
                    if n >= 2:
                        pe.wait_ge(s["xn2t_evac"], n - 1)
                    for k in range(4 * g, 4 * g + 4):
                        last = nc.tensor.transpose(bank[2 + g][:, ROWS[c] * (k % 4):ROWS[c] * (k % 4 + 1)],
                                                   xn2[0:ROWS[c], c, P * k:P * (k + 1)], ident[0:ROWS[c], 0:ROWS[c]])
                    last.then_inc(s["xn2t_done"], 1)
            pe.wait_ge(s["xn2t_evac"], 6)
            pe.wait_ge(s["h_ready"], 6)
            for c in range(3):
                for k in range(KC):
                    last = mm(bank[4][0:ROWS[c], NE * c:NE * (c + 1)], xn2T[:, k, tile_tokens(c)], wr[:, k, :],
                              start=(k == 0), stop=(k == KC - 1))
            last.then_inc(s["lg_done"], 1)
            pe.wait_ge(s["mask_ready"], 1)
            mask = rt[0]
            for c in range(3):
                out = bank[5][0:ROWS[c], NE * c:NE * (c + 1)]
                for c2 in range(c):
                    mm(out, ones[:, 0:ROWS[c]], mask[:, c2, :], start=(c2 == 0), stop=False)
                mm(out, strict[0:ROWS[c], 0:ROWS[c]], mask[0:ROWS[c], c, :], start=(c == 0), stop=True)
            for c in range(3):
                last = mm(bank[5][:, 96:128], ones[0:ROWS[c], :], mask[0:ROWS[c], c, :], start=(c == 0), stop=(c == 2))
            last.then_inc(s["pos_done"], 1)

            def expert(b):
                pe.wait_ge(s["xg_in"], b * 16 + 16)
                for q in range(4):
                    last = nc.tensor.transpose(bank[0][:, P * q:P * (q + 1)], xg[:, P * q:P * (q + 1)], ident[:])
                last.then_inc(s["xgt_done"], 1)
                pe.wait_ge(s["bias_in"], b * 32 + 32)
                if not first(b):
                    pe.wait_ge(s["act_ready"], b)
                for v in range(2):
                    mm(bank[1 + v][:], halves, brow[:, v, :], start=True, stop=False, skip_group_check=True)
                pe.wait_ge(s["xgt_ready"], b + 1)
                for k in range(KC):
                    pe.wait_ge(up_in[k], b * 16 + 16)
                    for v in range(2):
                        for f in range(2):
                            last = mm(bank[1 + v][64 * f:64 * f + 64, :], xgT[:, k % 4, k // 4, :],
                                      wup[k][:, D * v + HALF * f:D * v + HALF * (f + 1)],
                                      start=False, stop=(k == KC - 1), skip_group_check=True)
                    last.then_inc(s["up_used"], 1)
                if not first(b):
                    pe.wait_ge(s["y_ready"], b)
                mm(bank[4][:], halves, brow[:, 2, :], start=True, stop=False, skip_group_check=True
                   ).then_inc(s["bias_used"], 1)
                pe.wait_ge(s["act_ready"], b + 1)
                for q in range(4):
                    last = nc.tensor.transpose(bank[3][:, P * q:P * (q + 1)], act_h[:, P * q:P * (q + 1)], ident[:])
                last.then_inc(s["actt_done"], 1)
                pe.wait_ge(s["actt_ready"], b + 1)
                for k in range(KC):
                    pe.wait_ge(down_in[k], b * 16 + 16)
                    for f in range(2):
                        last = mm(bank[4][64 * f:64 * f + 64, :], actT[:, k % 4, k // 4, :],
                                  wdn[k][:, HALF * f:HALF * (f + 1)],
                                  start=False, stop=(k == KC - 1), skip_group_check=True)
                    last.then_inc(s["down_used"], 1)

            pe.wait_ge(s["tok_ready"], 1)
            expert(0)
            with pe.Fori(1, NE) as b:
                expert(b)
            nx = pe.value_load(info_i[0:1, 0:1], min_val=0, max_val=XB)
            with pe.Fori(0, XB) as x:
                with pe.If(x < nx):
                    expert(x + NE)

        @block.scalar
        def _(act):
            fn = nc.scalar.activation
            n = [0]

            def then(ins):
                n[0] += 1
                ins.then_inc(s["act_chain"], 1)
                act.wait_ge(s["act_chain"], n[0])

            act.wait_ge(s["const_ready"], 1)
            act.wait_ge(s["x_in"], 80)
            for c in range(3):
                last = fn(xn[0:ROWS[c], c, :], xrow[0:ROWS[c], c, :], ACT.Square, accum_out=ss[0:ROWS[c], c:c + 1])
            last.then_inc(s["ss_ready"], 1)
            act.wait_ge(s["ss_ready"], 1)
            for c in range(3):
                then(fn(rstd[0:ROWS[c], c:c + 1], ss[0:ROWS[c], c:c + 1], ACT.Ln, bias=c_eps[0:ROWS[c]], scale=1.0 / D))
            for c in range(3):
                last = fn(rstd[0:ROWS[c], c:c + 1], rstd[0:ROWS[c], c:c + 1], ACT.Exp, scale=-0.5)
                last.then_inc(s["rstd_ready"], 1)
            fn(credit[:, 0:1], c_one, ACT.Copy).then_inc(s["win_bank_free"], 1)
            fn(credit[:, 1:2], c_one, ACT.Copy).then_inc(s["win_bank_free"], 1)

            with act.Fori(0, 2) as it:
                for j in range(WRING):
                    act.wait_ge(s["win_used"], it * WRING + (j + 1))
                    bv, bg = bank[2 * (j % 2)], bank[2 * (j % 2) + 1]
                    k = it * WRING + j
                    fn(uh[:, bass.ds(k, 1), CH:CH + PT], bv[:, 0:PT].unsqueeze(1), ACT.Copy)
                    fn(uh[:, bass.ds(k, 1), CH + PT:UW].rearrange("p a (n t) -> p (a n) t", n=NB)[:, :, CH:CH + NS],
                       tok2(bv), ACT.Copy)
                    fn(acc[:, bass.ds(k, 1), :], bg[:, 0:T].unsqueeze(1), ACT.Sigmoid).then_inc(s["win_bank_free"], 1)

            def silu_step(v):
                act.wait_ge(s["conv_ready"], v * 2 + 2)
                fn(qkv[:, bass.ds(v * 2, 2), :], qkv[:, bass.ds(v * 2, 2), :], ACT.Silu).then_inc(s["silu_done"], 1)

            def qkv_round(it):
                for j in range(WRING):
                    act.wait_ge(s["win_used"], 8 * WRING + j + 1 if isinstance(it, int) else it * WRING + (5 * WRING + j + 1))
                    for f in range(2):
                        src = bank[2 * (j % 2) + f]
                        k = it * 8 + (2 * j + f)
                        fn(pre[:, 2 * j + f, SH:SH + PT], src[:, 0:PT], ACT.Copy)
                        fn(pre[:, 2 * j + f, SH + PT:QW].rearrange("p (n t) -> p n t", n=NB)[:, :, SH:SH + NS],
                           tok2(src), ACT.Copy).then_inc(s["qkv_copied"], 1)
                        fn(qtail[:, bass.ds(k, 1), 0:SH], src[:, PT - SH:PT].unsqueeze(1), ACT.Copy)
                        last = fn(qtail[:, bass.ds(k, 1), SH:27].rearrange("p a (n t) -> p (a n) t", n=NB),
                                  tok2(src)[:, :, NS - SH:NS], ACT.Copy)
                    last.then_inc(s["win_bank_free"], 1)
                for j in range(WRING):
                    silu_step(it * WRING + j)

            act.wait_ge(s["y_zeroed"], 16)
            for j in range(WRING):
                act.wait_ge(s["win_used"], 2 * WRING + j + 1)
                for f in range(2):
                    last = fn(zs[:, 2 * j + f, :], bank[2 * (j % 2) + f][:, 0:T], ACT.Silu)
                last.then_inc(s["win_bank_free"], 1)

            def gate_round(it, steps=range(WRING)):
                for j in steps:
                    act.wait_ge(s["win_used"], (3 + it) * WRING + j + 1)
                    last = fn(gate[:, it * 8 + 2 * j, :], bank[2 * (j % 2)][:, 0:T], ACT.Sigmoid)
                    last = fn(gate[:, it * 8 + 2 * j + 1, :], bank[2 * (j % 2) + 1][:, 0:T], ACT.Sigmoid)
                    last.then_inc(s["win_bank_free"], 1)

            gate_round(0)
            for k in range(KC):
                act.wait_ge(s["u_ready"], k + 1)
                fn(utail[:, k, 0:CH], uh[:, k, CH + PT - CH:CH + PT], ACT.Copy)
                fn(utail[:, k, CH:62].rearrange("p (n t) -> p n t", n=NB), sample_u(k)[:, :, CH:CH + NS], ACT.Copy)
            gate_round(1, range(0, 2))
            act.wait_ge(s["ab_ready"], 1)
            then(fn(gw2, gw1, ACT.Exp, scale=-1.0))
            fn(alog, alog, ACT.Exp)
            fn(gw2, gw2, ACT.Ln, bias=c_one)
            fn(beta, abt[:, :, 8:16], ACT.Sigmoid).then_inc(s["beta_act"], 1)
            act.wait_ge(s["centered"], 1)
            fn(sq[:, :, :], acc[:, :, :], ACT.Square).then_inc(s["squared"], 1)
            gate_round(1, range(2, WRING))
            act.wait_ge(s["sumsq_done"], 1)
            then(fn(rsc, bank[5][:, 0:T], ACT.Ln, bias=c_eps, scale=1.0 / D))
            fn(rsc, rsc, ACT.Exp, scale=-0.5).then_inc(s["ln_std"], 1)
            act.wait_ge(s["scaled"], 1)
            for k in range(KC):
                fn(acc[:, k, :], acc[:, k, :], ACT.Silu, bias=pcol[:, k, R_LNB:R_LNB + 1],
                   scale=pcol[:, k, R_LNG:R_LNG + 1]).then_inc(s["conf_act"], 1)
            with act.Fori(0, 2) as it:
                qkv_round(it)
            for i in range(16):
                act.wait_ge(s["l2_sum"], i + 1)
                fn(norms[i // 8][:, i % 8, :], bank[4 + i % 4][:, 0:T], ACT.Ln, bias=c_epsq if i < H else c_eps,
                   scale=float(P) if i < H else 1.0).then_inc(s["l2_root"], 1)
            act.wait_ge(s["l2_root"], 16)
            for i in range(2):
                fn(norms[i], norms[i], ACT.Exp, scale=-0.5).then_inc(s["l2_inv"], 1)
            qkv_round(V_ROUND)
            for c in range(3):
                R = ROWS[c]
                dt, eg = heads(u_dt, R), heads(u_eg, R)
                vn = u_kb.rearrange("p (h n) -> p h n", h=H)
                act.wait_ge(s["ekd_arg"], c + 1)
                fn(ekd[0:R], ekd[0:R], ACT.Exp).then_inc(s["ekd_ready"], 1)
                act.wait_ge(s["rows_done"], 2 * c + 2)
                if c:
                    act.wait_ge(s["s_evac"], 2 * c)
                    act.wait_ge(s["o_evac"], 2 * c)
                for g in range(2):
                    fn(eg[:, 4 * g:4 * g + 4, :], bank[1 + g][:, 0:4 * R].rearrange("p (h n) -> p h n", h=4), ACT.Exp
                       ).then_inc(s["eg_ready"], 1)
                act.wait_ge(s["dt_arg"], c + 1)
                fn(dt[0:R], dt[0:R], ACT.Exp).then_inc(s["dt_ready"], 1)
                act.wait_ge(s["uq_evac"], 4 * c + 4)
                for lev, _ in levels(act, c):
                    for g in range(2):
                        act.wait_ge(s["zt_done"], lev * 2 + (14 * c + g + 1))
                        fn(dt[0:R, 4 * g:4 * g + 4, :], bank[g][0:R, 0:4 * R].rearrange("p (h n) -> p h n", h=4), ACT.Copy
                           ).then_inc(s["zt_copied"], 1)
                if c == 2:
                    for g in range(2):
                        act.wait_ge(s["seg_done"], g + 1)
                        fn(kqs[:, 4 * g:4 * g + 4, :, :],
                           bank[6 + g][:, 0:384].rearrange("p (h a n) -> p h a n", h=4, a=2), ACT.Copy
                           ).then_inc(s["seg_copied"], 1)
                for g in range(2):
                    act.wait_ge(s["vn_done"], 2 * c + g + 1)
                    fn(vn[0:R, 4 * g:4 * g + 4, :], bank[g][0:R, :].rearrange("p (h n) -> p h n", h=4), ACT.Copy
                       ).then_inc(s["vn_ready"], 1)
                if c < 2:
                    for g in range(2):
                        act.wait_ge(s["o_done"], 2 * c + g + 1)
                        fn(qkv[:, 4 * g:4 * g + 4, tile_tokens(c)],
                           bank[2 + g][:, 0:4 * R].rearrange("p (h n) -> p h n", h=4), ACT.Copy).then_inc(s["o_evac"], 1)
            act.wait_ge(s["o_evac"], 6)

            def head_norm(h):
                act.wait_ge(s["on_sum"], h + 1)
                fn(hnorm[:, h, :], bank[h % 2][:, 0:T], ACT.Ln, bias=c_eps, scale=1.0 / P).then_inc(s["on_ln"], 1)

            for h in range(H):
                if h >= 3:
                    act.wait_ge(s["on_sum"], h - 2)
                fn(sqh[h % 3], qkv[:, h, :], ACT.Square).then_inc(s["on_sq"], 1)
                if h:
                    head_norm(h - 1)
            head_norm(H - 1)
            act.wait_ge(s["on_ln"], H)
            for g in range(2):
                fn(hnorm[:, 4 * g:4 * g + 4, :], hnorm[:, 4 * g:4 * g + 4, :], ACT.Exp, scale=-0.5
                   ).then_inc(s["on_inv"], 1)
            for c in range(3):
                act.wait_ge(s["h_ready"], 2 * c + 2)
                then(fn(xn2[0:ROWS[c], c, :], xrow[0:ROWS[c], c, :], ACT.Square, accum_out=ss[0:ROWS[c], c:c + 1]))
                then(fn(rstd[0:ROWS[c], c:c + 1], ss[0:ROWS[c], c:c + 1], ACT.Ln, bias=c_eps[0:ROWS[c]], scale=1.0 / D))
                fn(rstd[0:ROWS[c], c:c + 1], rstd[0:ROWS[c], c:c + 1], ACT.Exp, scale=-0.5).then_inc(s["hrstd_ready"], 1)
            act.wait_ge(s["gsub_ready"], 1)
            fn(gts, gts, ACT.Exp).then_inc(s["gexp_ready"], 1)

            def expert(b):
                act.wait_ge(s["xgt_done"], b + 1)
                fn(xgT, bank[0][:].rearrange("p (c a n) -> p c a n", c=4, a=2), ACT.Copy).then_inc(s["xgt_ready"], 1)
                act.wait_ge(s["hg_ready"], b + 1)
                fn(sg, hg, ACT.Sigmoid, scale=1.702).then_inc(s["sg_ready"], 1)
                act.wait_ge(s["actt_done"], b + 1)
                fn(actT, bank[3][:].rearrange("p (c a n) -> p c a n", c=4, a=2), ACT.Copy).then_inc(s["actt_ready"], 1)
                act.wait_ge(s["y_ready"], b + 1)
                for f in range(2):
                    act.dma_start(y_d[bass.ds(b * SLOTS, SLOTS), HALF * f:HALF * (f + 1)], ysb[64 * f:64 * f + 64, :]
                                  ).then_inc(s["y_stored"], 16)

            expert(0)
            with act.Fori(1, NE) as b:
                expert(b)
            act.wait_ge(s["y_stored"], 32 * NE)
            nx = act.value_load(info_i[0:1, 0:1], min_val=0, max_val=XB)
            with act.Fori(0, XB) as x:
                with act.If(x < nx):
                    expert(x + NE)
            for c in range(3):
                act.wait_ge(s["fsq_ready"], c + 1)
                then(fn(xn2[0:ROWS[c], c, :], xrow[0:ROWS[c], c, :], ACT.Square, accum_out=ss[0:ROWS[c], c:c + 1]))
                then(fn(rstd[0:ROWS[c], c:c + 1], ss[0:ROWS[c], c:c + 1], ACT.Ln, bias=c_eps[0:ROWS[c]], scale=1.0 / D))
                fn(rstd[0:ROWS[c], c:c + 1], rstd[0:ROWS[c], c:c + 1], ACT.Exp, scale=-0.5).then_inc(s["frstd_ready"], 1)

        @block.vector
        def _(dve):
            v = nc.vector
            n = [0]

            def then(ins):
                n[0] += 1
                ins.then_inc(s["dve_chain"], 1)
                dve.wait_ge(s["dve_chain"], n[0])

            stt = v.scalar_tensor_tensor
            for k in range(KC):
                v.memset(uh[:, k, 0:CH], 0.0)
            for k in range(8):
                v.memset(pre[:, k, 0:SH], 0.0)
            then(v.memset(abt, 0.0))
            dve.wait_ge(s["job_done"], 1)
            v.tensor_copy(pcol[:, :, :], bank[0][:, 0:KC * NROWS].rearrange("p (k n) -> p k n", k=KC)
                          ).then_inc(s["job_evac"], 1)
            dve.wait_ge(s["job_evac"], 1)
            for t in range(2):
                for g in range(2):
                    j = 1 + 2 * t + g
                    dve.wait_ge(s["job_done"], j + 1)
                    for k in range(4 * g, 4 * g + 4):
                        last = v.tensor_copy(sample_u(k)[:, 4 * t:4 * t + 4, 0:CH],
                                             bank[j % 8][:, 120 * (k % 4):120 * (k % 4 + 1)]
                                             .rearrange("p (n t) -> p n t", n=4))
                    last.then_inc(s["job_evac"], 1)
            for g in range(2):
                j = 5 + g
                dve.wait_ge(s["job_done"], j + 1)
                v.tensor_copy(dh[:, 12 * g:12 * g + 12, :],
                              bank[j % 8][:, 0:288].rearrange("p (k n) -> p k n", k=12)).then_inc(s["job_evac"], 1)
            for c in range(3):
                dve.wait_ge(s["rstd_ready"], c + 1)
                v.tensor_scalar(xn[0:ROWS[c], c, :], xrow[0:ROWS[c], c, :], rstd[0:ROWS[c], c:c + 1], None, ALU.mult
                                ).then_inc(s["xn_ready"], 1)
            for c in range(3):
                for g in range(2):
                    j = 7 + 2 * c + g
                    R = ROWS[c]
                    dve.wait_ge(s["job_done"], j + 1)
                    v.tensor_tensor(xnT[:, 4 * g:4 * g + 4, tile_tokens(c)],
                                    bank[j % 8][:, 0:4 * R].rearrange("p (k n) -> p k n", k=4),
                                    pcol[:, 4 * g:4 * g + 4, R_NMIX:R_NMIX + 1].to_broadcast((P, 4, R)), ALU.mult
                                    ).then_inc(s["job_evac"], 1)

            def one(v4):
                return v4.rearrange("p a n -> p (a n)")

            def taps(n_taps, chunks, base, last_sem, bias=None):
                n_parts = len(chunks[0]) - 1
                for tap in range(n_taps):
                    for part in range(n_parts):
                        for i, chunk in enumerate(chunks):
                            weight, (out, src) = chunk[0], chunk[1 + part]
                            if tap == 0:
                                last = v.tensor_scalar(out, src(tap), weight(tap), bias[i] if bias else None, ALU.mult,
                                                       *([ALU.add] if bias else []))
                            else:
                                dve.wait_ge(s["conv_chain"], base + (2 * n_parts * (tap - 1) + 2 * part + i + 1))
                                last = stt(out, src(tap), weight(tap), out, ALU.mult, ALU.add)
                            if tap < n_taps - 1:
                                last.then_inc(s["conv_chain"], 1)
                            elif part == n_parts - 1:
                                last.then_inc(last_sem, 1)

            CLINKS = 2 * (CW - 1)
            with dve.Fori(0, KC // 2) as it:
                pair = []
                for i in range(2):
                    k = it * 2 + i
                    dve.wait_ge(s["win_bank_free"], it * 2 + (i + 3))
                    up = uh[:, bass.ds(k, 1), CH:CH + PT]
                    v.tensor_tensor(up, up, acc[:, bass.ds(k, 1), 0:PT], ALU.mult)
                    us = uh[:, bass.ds(k, 1), CH + PT:UW].rearrange("p a (n t) -> p (a n) t", n=NB)[:, :, CH:CH + NS]
                    v.tensor_tensor(us, us, acc[:, bass.ds(k, 1), PT:T].rearrange("p a (n t) -> p (a n) t", n=NB), ALU.mult
                                    ).then_inc(s["u_ready"], 1)
                    src = uh[:, bass.ds(k, 1), :]
                    pair.append((lambda tap, k=k: one(pcol[:, bass.ds(k, 1), R_DW + tap:R_DW + tap + 1]),
                                 (one(acc[:, bass.ds(k, 1), 0:PT]), lambda tap, src=src: one(src[:, :, tap:tap + PT]))))
                dve.wait_ge(s["u_ready"], it * 2 + 2)
                taps(CW, pair, it * CLINKS, s["conf_done"],
                     [one(pcol[:, bass.ds(it * 2 + i, 1), R_BDW:R_BDW + 1]) for i in range(2)])

            dve.wait_ge(s["ab_done"], 1)
            for c in range(3):
                last = v.tensor_copy(abt[0:ROWS[c], c, :], bank[6][0:ROWS[c], 16 * c:16 * c + 16])
            then(last)
            then(v.tensor_tensor(g_t, abt[:, :, 0:8], dtb.unsqueeze(1).to_broadcast((P, 3, H)), ALU.add))
            then(v.tensor_scalar(gw1, g_t, -1.0, None, ALU.mult))
            then(v.tensor_tensor(gw1, gw1, g_t, ALU.max))
            v.tensor_scalar(g_t, g_t, 0.0, None, ALU.max).then_inc(s["ab_ready"], 1)
            dve.wait_ge(s["sum_done"], 1)
            then(v.tensor_scalar(mu, bank[4][:, 0:T], 1.0 / D, None, ALU.mult))
            v.tensor_tensor(acc[:, :, :], acc[:, :, :], mu.unsqueeze(1).to_broadcast((P, KC, T)), ALU.subtract
                            ).then_inc(s["centered"], 1)
            dve.wait_ge(s["ln_std"], 1)
            v.tensor_tensor(acc[:, :, :], acc[:, :, :], rsc.unsqueeze(1).to_broadcast((P, KC, T)), ALU.mult
                            ).then_inc(s["scaled"], 1)

            dve.wait_ge(s["beta_act"], 1)
            dve.wait_ge(s["ab_ready"], 1)
            then(v.tensor_tensor(g_t, g_t, gw2, ALU.add))
            then(stt(g_t, g_t, -1.0, alog.unsqueeze(1).to_broadcast((P, 3, H)), ALU.mult, ALU.mult))
            v.tensor_scalar(nbeta, beta, -1.0, None, ALU.mult).then_inc(s["beta_ready"], 1)

            QLINKS = 2 + 4 * (SW - 1)
            QBASE = KC // 2 * CLINKS

            def short_conv(it, j):
                pair = []
                base = it * (4 * QLINKS) + (QBASE + j // 2 * QLINKS)
                for i in (j, j + 1):
                    k = it * 8 + i
                    dve.wait_ge(s["qkv_copied"], it * 8 + (i + 1))
                    hist = pre[:, i, SH + PT:QW].rearrange("p (n t) -> p n t", n=NB)
                    v.tensor_copy(hist[:, :, 0:SH], dh[:, bass.ds(k, 1), :].rearrange("p a (n t) -> p (a n) t", n=NB)
                                  ).then_inc(s["conv_chain"], 1)
                    dst = qkv[:, bass.ds(k, 1), :]
                    pair.append((lambda tap, i=i: pcol[:, i, bass.ds(it + (R_DN + 3 * tap), 1)],
                                 (one(dst[:, :, 0:PT]), lambda tap, i=i: pre[:, i, tap:tap + PT]),
                                 (dst[:, :, PT:T].rearrange("p a (n t) -> p (a n) t", n=NB),
                                  lambda tap, hist=hist: hist[:, :, tap:tap + NS])))
                dve.wait_ge(s["conv_chain"], base + 2)
                taps(SW, pair, base + 2, s["conv_ready"])

            def l2_scale(i):
                dve.wait_ge(s["l2_inv"], i + 1)
                w = qkv[:, 8 * i:8 * i + 8, :]
                v.tensor_tensor(w, w, norms[i], ALU.mult).then_inc(s["l2_scaled"], 8)

            with dve.Fori(0, 2) as it:
                for j in range(0, 8, 2):
                    short_conv(it, j)
            dve.wait_ge(s["win_bank_free"], 2 + 20)
            for j in range(WRING):
                for m in (2 * j, 2 * j + 1):
                    dve.wait_ge(s["win_used"], 7 * WRING + j + 1)
                    stt(gate[:, m, :], bank[2 * (j % 2) + m % 2][:, 0:T], pcol[:, m, R_BCO:R_BCO + 1], gate[:, m, :],
                        ALU.add, ALU.mult).then_inc(s["conf_mm_evac"], 1)
            for j in range(WRING):
                short_conv(V_ROUND, 2 * j)
                if j < 2:
                    l2_scale(j)

            for g in range(8):
                dve.wait_ge(s["tail_t_done"], g + 1)
                if g < 2:
                    dst, src = uout[:, 512 * g:512 * (g + 1)], bank[4 + g][0:62, :]
                else:
                    dst, src = qout[:, 512 * (g - 2):512 * (g - 1)], bank[4 + g % 4][0:27, :]
                v.tensor_copy(dst, src).then_inc(s["tail_evac"], 1)

            dve.wait_ge(s["l2_scaled"], 16)
            dve.wait_ge(s["const_ready"], 2)

            for c in range(3):
                R = ROWS[c]
                tt = tile_tokens(c)
                ng = (neg if c < 2 else neg2)[0:R, 0:R]
                kb, dt, eg, uu, qk, x, xt = (heads(w, R) for w in (u_kb, u_dt, u_eg, u_u, u_qk, u_x, u_xt))
                kqe = u_kqe[:, 0:2 * H * R].rearrange("p (h a n) -> p h a n", h=H, a=2)
                kd, vb, vn = (w.rearrange("p (h n) -> p h n", h=H) for w in (u_kd, u_vb, u_kb))

                def four(w, m, r):
                    return w[0:m, 0:4 * r].rearrange("p (h n) -> p h n", h=4)

                dve.wait_ge(s["small_mm"], c + 1)
                if c:
                    dve.wait_ge(s["tok_evac"], 4 * c)
                then(v.tensor_copy(gcs[0:R], bank[0][0:R, 0:16]))
                v.tensor_tensor(ekd[0:R], gcs[0:R, 8:16], gcs[0:R, 0:8], ALU.subtract).then_inc(s["ekd_arg"], 1)
                for g in range(2):
                    dve.wait_ge(s["eg_ready"], 2 * c + g + 1)
                    for h in range(4 * g, 4 * g + 4):
                        last = stt(dt[0:R, h, :], bank[1 + g][0:R, R * (h % 4):R * (h % 4 + 1)], gcs[0:R, h:h + 1], ng,
                                   ALU.subtract, ALU.add)
                last.then_inc(s["dt_arg"], 1)
                for g in range(2):
                    dve.wait_ge(s["brow_done"], 2 * c + 2)
                    v.tensor_tensor(kb[:, 4 * g:4 * g + 4, :], qkv[:, H + 4 * g:H + 4 * g + 4, tt],
                                    four(bank[3 + g], P, R), ALU.mult).then_inc(s["kb_ready"], 1)
                v.tensor_tensor(kqe[:, :, 0, :], qkv[:, H:2 * H, tt], eg, ALU.mult)
                v.tensor_tensor(kqe[:, :, 1, :], qkv[:, 0:H, tt], eg, ALU.mult)
                dve.wait_ge(s["dt_ready"], c + 1)
                for g in range(2):
                    dve.wait_ge(s["uq_done"], 4 * c + 2 * g + 1)
                    v.tensor_tensor(uu[0:R, 4 * g:4 * g + 4, :], four(bank[5 + g], R, R), dt[0:R, 4 * g:4 * g + 4, :],
                                    ALU.mult).then_inc(s["uq_evac"], 1)
                for g in range(2):
                    dve.wait_ge(s["uq_done"], 4 * c + 2 * g + 2)
                    v.tensor_tensor(qk[0:R, 4 * g:4 * g + 4, :], four(bank[7 - 7 * g], R, R), dt[0:R, 4 * g:4 * g + 4, :],
                                    ALU.mult).then_inc(s["uq_evac"], 1)
                dve.wait_ge(s["ekd_ready"], c + 1)
                for g in range(4):
                    dve.wait_ge(s["tok_done"], 4 * c + g + 1)
                    hs = slice(4 * (g % 2), 4 * (g % 2) + 4)
                    dst, w = (kd, ekd[0:R]) if g < 2 else (vb, beta[0:R, c, :])
                    v.tensor_tensor(dst[0:R, hs, :], four(bank[1 + g], R, P), w[:, hs].unsqueeze(2).to_broadcast((R, 4, P)),
                                    ALU.mult).then_inc(s["tok_evac"], 1)
                dve.wait_ge(s["um_ready"], 7 * c + 1)
                um = heads(u_um, R)
                v.tensor_tensor(x[0:R], ident[0:R, 0:R].unsqueeze(1).to_broadcast((R, H, R)), um[0:R], ALU.subtract)
                for g in range(2):
                    dve.wait_ge(s["zt_done"], 14 * c + g + 1)
                    v.tensor_tensor(xt[0:R, 4 * g:4 * g + 4, :], ident[0:R, 0:R].unsqueeze(1).to_broadcast((R, 4, R)),
                                    four(bank[g], R, R), ALU.subtract).then_inc(s["x_updated"], 1)
                for lev, final in levels(dve, c):
                    for g in range(2):
                        hs = slice(4 * g, 4 * g + 4)
                        dve.wait_ge(s["x_updated"], lev * 2 + (14 * c + g - 1))
                        dve.wait_ge(s["vt_done"], lev * 2 + (12 * c + g - 1))
                        last = v.tensor_tensor(x[0:R, hs, :], x[0:R, hs, :], four(bank[2 + g], R, R), ALU.subtract)
                        if not final:
                            last = v.tensor_tensor(xt[0:R, hs, :], xt[0:R, hs, :], four(bank[4 + g], R, R), ALU.subtract)
                        last.then_inc(s["x_updated"], 1)
                if c:
                    for g in range(2):
                        dve.wait_ge(s["kes_done"], 2 * (c - 1) + g + 1)
                        src = bank[6 + g] if c == 1 else bank[4 + g]
                        for h in range(4 * g, 4 * g + 4):
                            last = stt(vb[0:R, h, :], src[0:R, P * (h % 4):P * (h % 4 + 1)], nbeta[0:R, c, h:h + 1],
                                       vb[0:R, h, :], ALU.mult, ALU.add)
                        last.then_inc(s["r_ready"], 1)
                if c == 0:
                    for g in range(2):
                        dve.wait_ge(s["s_done"], g + 1)
                        v.tensor_copy(S[:, 4 * g:4 * g + 4, :], four(bank[4 + g], P, P)).then_inc(s["s_evac"], 1)
                    dve.wait_ge(s["s_evac"], 2)
                elif c == 1:
                    for g in range(2):
                        dve.wait_ge(s["s_done"], 2 + g + 1)
                        for h in range(4 * g, 4 * g + 4):
                            last = stt(S[:, h, :], S[:, h, :], eg[:, h, R - 1:R], bank[4 + g][:, P * (h % 4):P * (h % 4 + 1)],
                                       ALU.mult, ALU.add)
                        last.then_inc(s["s_evac"], 1)
                    dve.wait_ge(s["s_evac"], 4)
                else:
                    for g in range(2):
                        dve.wait_ge(s["o_done"], 4 + g + 1)
                        v.tensor_tensor(qkv[:, 4 * g:4 * g + 4, tt], kqs[:, 4 * g:4 * g + 4, 1, :], four(bank[2 + g], P, R),
                                        ALU.add).then_inc(s["o_evac"], 1)

            dve.wait_ge(s["o_evac"], 6)
            for h in range(H):
                v.tensor_tensor(s0[:, h, :, :], s0[:, h, :, :],
                                eg[:, h, TAIL + NS - 1:48:NS]
                                .unsqueeze(2).to_broadcast((P, NB, P)), ALU.mult).then_inc(s["s_decayed"], 1)
            for g in range(2):
                dve.wait_ge(s["on_inv"], g + 1)
                dve.wait_ge(s["on_prod"], 4 * g + 4)
                v.tensor_tensor(qkv[:, 4 * g:4 * g + 4, :], qkv[:, 4 * g:4 * g + 4, :], hnorm[:, 4 * g:4 * g + 4, :], ALU.mult
                                ).then_inc(s["o_ready"], 4)
            dve.wait_ge(s["s_decayed"], H)
            for m in range(KC):
                dve.wait_ge(s["y_mm_done"], m + 1)
                then(v.tensor_tensor(gate[:, KC + m, :], bank[m % 2][:, 0:T], gate[:, KC + m, :], ALU.mult))
                v.tensor_tensor(gate[:, m, :], gate[:, m, :], gate[:, KC + m, :], ALU.add).then_inc(s["y_mm_evac"], 1)
                dve.wait_ge(s["sn_done"], m + 1)
                bs = (bank[4], bank[5], bank[6]) if m % 2 == 0 else (bank[7], bank[2], bank[3])
                stt(S[:, m, :], S[:, m, :], eg[:, m, TAIL - 1:TAIL], bs[0][:, 0:P], ALU.mult, ALU.add)
                v.tensor_tensor(s0[:, m, 0:3, :], s0[:, m, 0:3, :], bs[0][:, P:512].rearrange("p (n v) -> p n v", n=3),
                                ALU.add)
                v.tensor_tensor(s0[:, m, 3:7, :], s0[:, m, 3:7, :], bs[1][:, :].rearrange("p (n v) -> p n v", n=4),
                                ALU.add)
                v.tensor_tensor(s0[:, m, 7, :], s0[:, m, 7, :], bs[2][:, 0:P], ALU.add).then_inc(s["s_evac"], 1)
            dve.wait_ge(s["norms_in"], 32)
            dve.wait_ge(s["router_in"], 48)

            def normalised(c):
                dve.wait_ge(s["hrstd_ready"], c + 1)
                stt(xn2[0:ROWS[c], c, :], xrow[0:ROWS[c], c, :], rstd[0:ROWS[c], c:c + 1], nffn[0:ROWS[c], :],
                    ALU.mult, ALU.mult).then_inc(s["xn2_ready"], 1)

            for c in range(3):
                for f in range(2):
                    i = 2 * c + f
                    dve.wait_ge(s["o_mm_done"], i + 1)
                    w = xrow[0:ROWS[c], c, HALF * f:HALF * (f + 1)]
                    v.tensor_tensor(w, w, bank[(4, 5, 6, 7, 0, 1)[i]][0:ROWS[c], :], ALU.add).then_inc(s["h_ready"], 1)
                if c:
                    normalised(c - 1)
            normalised(2)
            for c in range(3):
                for g in range(2):
                    dve.wait_ge(s["xn2t_done"], 2 * c + g + 1)
                    v.tensor_copy(xn2T[:, 4 * g:4 * g + 4, tile_tokens(c)],
                                  bank[2 + g][:, 0:4 * ROWS[c]].rearrange("p (k n) -> p k n", k=4)
                                  ).then_inc(s["xn2t_evac"], 1)
            then(v.memset(halves, 0.0))
            v.memset(lg, 0.0)
            v.memset(rt[1], 0.0)
            then(v.memset(halves[0:1, 0:64], 1.0))
            then(v.tensor_scalar(halves[:, 64:128], halves[:, 0:64], -1.0, 1.0, ALU.mult, ALU.add))
            dve.wait_ge(s["lg_done"], 1)
            for c in range(3):
                R = ROWS[c]
                then(v.tensor_tensor(lg[0:R, c, :], bank[4][0:R, NE * c:NE * (c + 1)], brt[0:R], ALU.add))
                then(v.max(mx8[:, c, :], lg[:, c, :]))
                then(v.max_index(ix8[:, c, :], mx8[:, c, :], lg[:, c, :]))
            then(v.tensor_copy(ixf, ix8))
            v.tensor_tensor(gts, mx8[:, :, 0:TOPK], mx8[:, :, 0:1].to_broadcast((P, 3, TOPK)), ALU.subtract
                            ).then_inc(s["gsub_ready"], 1)
            for c in range(3):
                last = v.tensor_tensor(oh[:, c], iota_e.unsqueeze(1).to_broadcast((P, TOPK, NE)),
                                       ixf[:, c, 0:TOPK].unsqueeze(2).to_broadcast((P, TOPK, NE)), ALU.is_equal)
            then(last)
            then(v.tensor_tensor(rt[0], oh[:, :, 0, :], oh[:, :, 1, :], ALU.add))
            then(v.tensor_tensor(rt[0], rt[0], oh[:, :, 2, :], ALU.add))
            v.tensor_tensor(rt[0], rt[0], oh[:, :, 3, :], ALU.add).then_inc(s["mask_ready"], 1)
            dve.wait_ge(s["gexp_ready"], 1)
            then(v.tensor_reduce(gsum.unsqueeze(2), gts, AX.X, ALU.add))
            then(v.reciprocal(gsum, gsum))
            then(v.tensor_tensor(gts, gts, gsum.unsqueeze(2).to_broadcast((P, 3, TOPK)), ALU.mult))
            dve.wait_ge(s["pos_done"], 1)
            pos, pd, slot, t1, t2, dl, yl = rt[1], rt[2], rt[3], rt[4], rt[5], rt[6], rt[7]
            for c in range(3):
                last = v.tensor_copy(pos[0:ROWS[c], c, :], bank[5][0:ROWS[c], NE * c:NE * (c + 1)])
            then(v.tensor_copy(cnt, bank[5][:, 96:128]))
            v.tensor_scalar(pd, pos, float(SLOTS), None, ALU.is_ge)
            then(v.tensor_scalar(nbx, cnt, float(SLOTS), None, ALU.is_gt))
            for m in range(2, 5):
                stt(pd, pos, float(SLOTS * m), pd, ALU.is_ge, ALU.add)
                then(stt(nbx, cnt, float(SLOTS * m), nbx, ALU.is_gt, ALU.add))
            then(stt(slot, pd, -float(SLOTS), pos, ALU.mult, ALU.add))
            then(v.tensor_copy(cs[0], nbx))
            for i in range(5):
                w = 1 << i
                src, dst = cs[i % 2], cs[(i + 1) % 2]
                v.tensor_copy(dst[:, 0:w], src[:, 0:w])
                then(v.tensor_tensor(dst[:, w:NE], src[:, w:NE], src[:, 0:NE - w], ALU.add))
            incl = cs[1]
            then(v.tensor_tensor(xs, incl, nbx, ALU.subtract))
            then(stt(t1, pd, float(NE - 1), xs.unsqueeze(1).to_broadcast((P, 3, NE)), ALU.add, ALU.add))
            then(v.tensor_tensor(t2, iota_e.unsqueeze(1).to_broadcast((P, 3, NE)), t1, ALU.subtract))
            then(stt(t2, pd, 0.0, t2, ALU.is_equal, ALU.mult))
            then(v.tensor_tensor(t1, t1, t2, ALU.add))
            stt(dl, slot, float(NBLK), t1, ALU.mult, ALU.add)
            then(stt(yl, t1, float(SLOTS), slot, ALU.mult, ALU.add))
            for src, dst, ready in ((dl, dli, s["dl_ready"]), (yl, yli, s["yl_ready"])):
                then(v.tensor_tensor(ohm, oh, src.unsqueeze(2).to_broadcast((P, 3, TOPK, NE)), ALU.mult))
                then(v.tensor_reduce(self_.unsqueeze(3), ohm, AX.X, ALU.add))
                v.tensor_copy(dst, self_).then_inc(ready, 1)
                dve.wait_ge(ready, 1)
            dve.wait_ge(s["s_out"], 16 * (H + 1))
            v.tensor_copy(info[:, 0:1], incl[0:1, NE - 1:NE])
            shape = (1, XB, NE)
            then(v.tensor_scalar(xio, iota_e[0:1, 0:XB], 0.0, None, ALU.add))
            v.tensor_tensor(bx[0], xio.unsqueeze(2).to_broadcast(shape), xs[0:1].unsqueeze(1).to_broadcast(shape), ALU.is_ge)
            then(v.tensor_tensor(bx[1], xio.unsqueeze(2).to_broadcast(shape), incl[0:1].unsqueeze(1).to_broadcast(shape),
                                 ALU.is_ge))
            then(v.tensor_tensor(bx[0], bx[0], bx[1], ALU.subtract))
            then(v.tensor_tensor(bx[2], bx[0], iota_e[0:1].unsqueeze(1).to_broadcast(shape), ALU.mult))
            then(v.tensor_reduce(info[:, 1:1 + XB].unsqueeze(2), bx[2], AX.X, ALU.add))
            v.tensor_copy(info_i[0:1, :], info).then_inc(s["idx_ready"], 1)
            dve.wait_ge(s["tok_in"], 32)
            v.tensor_scalar(tokt, tokt, 2.0, half_col, ALU.mult, ALU.add).then_inc(s["tok_ready"], 1)

            moe_chain = s["expert_chain"]

            def expert(b):
                dve.wait_ge(s["up_used"], b * KC + KC)
                v.tensor_scalar(hg, bank[1][:], 7.0, None, ALU.min).then_inc(s["hg_ready"], 1)
                v.tensor_scalar(hl, bank[2][:], 7.0, -7.0, ALU.min, ALU.max).then_inc(moe_chain, 1)
                dve.wait_ge(moe_chain, b * 2 + 1)
                stt(hgl, hl, 1.0, hg, ALU.add, ALU.mult).then_inc(moe_chain, 1)
                dve.wait_ge(moe_chain, b * 2 + 2)
                dve.wait_ge(s["sg_ready"], b + 1)
                v.tensor_tensor(act_h, hgl, sg, ALU.mult).then_inc(s["act_ready"], 1)
                dve.wait_ge(s["down_used"], b * KC + KC)
                if not first(b):
                    dve.wait_ge(s["y_stored"], b * 32)
                v.tensor_copy(ysb, bank[4][:]).then_inc(s["y_ready"], 1)

            expert(0)
            with dve.Fori(1, NE) as b:
                expert(b)
            nx = dve.value_load(info_i[0:1, 0:1], min_val=0, max_val=XB)
            with dve.Fori(0, XB) as xx:
                with dve.If(xx < nx):
                    expert(xx + NE)
            for c in range(3):
                R = ROWS[c]
                dve.wait_ge(y_in[c], 16 * TOPK)
                for r in range(TOPK):
                    ins = stt(xrow[0:R, c, :], ygat[TOPK * c + r][0:R, :], gts[0:R, c, r:r + 1], xrow[0:R, c, :],
                              ALU.mult, ALU.add)
                    if r < TOPK - 1:
                        then(ins)
                    else:
                        ins.then_inc(s["fsq_ready"], 1)
            dve.wait_ge(s["fsq_ready"], 3)
            for c in range(3):
                R = ROWS[c]
                dve.wait_ge(s["frstd_ready"], c + 1)
                stt(xn2[0:R, c, :], xrow[0:R, c, :], rstd[0:R, c:c + 1], nfin[0:R, :], ALU.mult, ALU.mult
                    ).then_inc(s["final_ready"], 1)


_INS = ['x_prompt', 'x_sample', 'state_conf_conv', 'state_dn_conv', 'state_dn_S', 'meta_tokens', 'norm_mix', 'w_in',
        'w_conf_dw', 'b_conf_dw', 'ln_conf_g', 'ln_conf_b', 'w_conf_out', 'b_conf_out', 'w_dn_conv', 'dn_a_log',
        'dn_dt_bias', 'dn_norm_w', 'w_dn_out', 'w_out', 'norm_ffn', 'w_router', 'b_router', 'w_up', 'b_up', 'w_down',
        'b_down', 'norm_final']
_OUTS = {'y_prompt': (1, 256, 1024), 'y_sample': (8, 4, 1024), 'cp': (1, 1, 30, 1024), 'dp': (1, 1, 3, 3072),
         'sp': (1, 1, 8, 128, 128), 'cs': (1, 8, 30, 1024), 'ds': (1, 8, 3, 3072), 'ss': (1, 8, 8, 128, 128)}


def kernel(**inputs):
    import numpy as _np
    import concourse.bacc as _bacc
    from concourse.bass_utils import run_bass_kernel_spmd as _run

    nc = _bacc.Bacc("TRN2", target_bir_lowering=False, num_devices=1)
    arrays, args = {}, {}
    for name in _INS:
        v = _np.ascontiguousarray(inputs[name])
        arrays[f"in_{name}"] = v
        args[name] = nc.dram_tensor(f"in_{name}", v.shape, mybir.dt.from_np(v.dtype), kind="ExternalInput").ap()
    for name, shape in _OUTS.items():
        args[name] = nc.dram_tensor(f"out_{name}", shape, F32, kind="ExternalOutput").ap()
    build(nc, args)
    r = _run(nc, [arrays], core_ids=[0])
    return tuple(r.results[0][f"out_{name}"] for name in _OUTS)
```
